# Optimizing a Trainium2 kernel written in Bass

```python
import jax, jax.numpy as jnp
from jax import lax
import numpy as np
import math

D_MODEL = 1024
BATCH = 1
SEQ = 256
DEPTH = 2

N_MIXERS = 2
N_LRU_LAYERS = (DEPTH + 1) // 2
N_POOL_LAYERS = DEPTH // 2
D_FF = 11 * D_MODEL // 4
D_RNN = 5 * D_MODEL // 4
LRU_HEADS = 16
LRU_HEAD_DIM = D_RNN // LRU_HEADS
CONV_WIDTH = 4
LRU_C = 8.0
POOL_WINDOWS = (2, 4, 8, 16)
POOL_GROUPS = len(POOL_WINDOWS)
POOL_GROUP_DIM = D_MODEL // POOL_GROUPS
PLE_DIM = 256
RMS_EPS = 1e-6


def rms_norm(x, g):
    xf = x.astype(jnp.float32)
    y = xf * lax.rsqrt(jnp.mean(xf * xf, axis=-1, keepdims=True) + RMS_EPS)
    return (y * g.astype(jnp.float32)).astype(x.dtype)

def swiglu(x, w_gate, w_up, w_down):
    return (jax.nn.silu(x @ w_gate) * (x @ w_up)) @ w_down

def _lin_combine(c1, c2):
    a1, b1 = c1
    a2, b2 = c2
    return a1 * a2, a2 * b1 + b2

def rglru_mixer(x, w_in, conv_w, conv_b, w_a, b_a, w_x, b_x, a_param, w_out):
    B, S, _ = x.shape
    z = x @ w_in
    gate_branch, xb = z[..., :D_RNN], z[..., D_RNN:]
    xp = jnp.pad(xb, ((0, 0), (CONV_WIDTH - 1, 0), (0, 0)))
    xc = conv_b + conv_w[0] * xp[:, 0:S]
    for k in range(1, CONV_WIDTH):
        xc = xc + conv_w[k] * xp[:, k:k + S]
    xh = xc.reshape(B, S, LRU_HEADS, LRU_HEAD_DIM)
    r = jax.nn.sigmoid(jnp.einsum('bshi,hij->bshj', xh, w_a).reshape(B, S, D_RNN) + b_a)
    ig = jax.nn.sigmoid(jnp.einsum('bshi,hij->bshj', xh, w_x).reshape(B, S, D_RNN) + b_x)
    log_a = -LRU_C * r.astype(jnp.float32) * jax.nn.softplus(-a_param.astype(jnp.float32))
    a = jnp.exp(log_a)
    mult = jnp.sqrt(-jnp.expm1(2.0 * log_a))
    bterm = mult * (ig * xc).astype(jnp.float32)
    _, h = lax.associative_scan(_lin_combine, (a, bterm), axis=1)
    y = h.astype(x.dtype) * jax.nn.gelu(gate_branch)
    return y @ w_out

def pool_mixer(x, w, b, scale):
    B, S, _ = x.shape
    xf = x.astype(jnp.float32)
    cs = jnp.cumsum(xf, axis=1)
    t = jnp.arange(S)
    outs = []
    for g, win in enumerate(POOL_WINDOWS):
        lo, hi = g * POOL_GROUP_DIM, (g + 1) * POOL_GROUP_DIM
        c = cs[..., lo:hi]
        prev = jnp.pad(c[:, :S - win], ((0, 0), (win, 0), (0, 0)))
        count = jnp.minimum(t + 1, win).astype(jnp.float32)[None, :, None]
        outs.append((c - prev) / count - xf[..., lo:hi])
    u = jnp.stack(outs, axis=2).astype(x.dtype)
    y = jnp.einsum('bsgc,gcd->bsgd', u, w).reshape(B, S, D_MODEL)
    return (y + b) * scale

def first_inputs(seed: int = 0) -> dict:
    key = jax.random.key(seed)
    ks = iter(jax.random.split(key, 40))

    def nrm(shape, scale):
        return scale * jax.random.normal(next(ks), shape, jnp.float32)

    D, F, L = D_MODEL, D_FF, DEPTH
    NL, NP = N_LRU_LAYERS, N_POOL_LAYERS
    x = nrm((BATCH, SEQ, D), 1.0)
    p = nrm((DEPTH, BATCH, SEQ, PLE_DIM), 1.0)
    ffn1_norm = 1.0 + nrm((L, D), 0.1)
    ffn1_w_gate = nrm((L, D, F), D ** -0.5)
    ffn1_w_up = nrm((L, D, F), D ** -0.5)
    ffn1_w_down = nrm((L, F, D), F ** -0.5)
    mix_norm = 1.0 + nrm((L, D), 0.1)
    lru_w_in = nrm((NL, D, 2 * D_RNN), D ** -0.5)
    lru_conv_w = nrm((NL, CONV_WIDTH, D_RNN), CONV_WIDTH ** -0.5)
    lru_conv_b = nrm((NL, D_RNN), 0.01)
    lru_w_a = nrm((NL, LRU_HEADS, LRU_HEAD_DIM, LRU_HEAD_DIM), LRU_HEAD_DIM ** -0.5)
    lru_b_a = nrm((NL, D_RNN), 0.01)
    lru_w_x = nrm((NL, LRU_HEADS, LRU_HEAD_DIM, LRU_HEAD_DIM), LRU_HEAD_DIM ** -0.5)
    lru_b_x = nrm((NL, D_RNN), 0.01)
    u = jax.random.uniform(next(ks), (NL, D_RNN), jnp.float32, minval=0.9, maxval=0.999)
    a0 = u ** (1.0 / LRU_C)
    lru_a_param = jnp.log(a0) - jnp.log1p(-a0)
    lru_w_out = nrm((NL, D_RNN, D), D_RNN ** -0.5)
    pool_w = nrm((NP, POOL_GROUPS, POOL_GROUP_DIM, POOL_GROUP_DIM), POOL_GROUP_DIM ** -0.5)
    pool_b = nrm((NP, D), 0.01)
    pool_scale = 1.0 + nrm((NP, D), 0.1)
    ffn2_norm = 1.0 + nrm((L, D), 0.1)
    ffn2_w_gate = nrm((L, D, F), D ** -0.5)
    ffn2_w_up = nrm((L, D, F), D ** -0.5)
    ffn2_w_down = nrm((L, F, D), F ** -0.5)
    ple_norm = 1.0 + nrm((L, D), 0.1)
    ple_w_gate = nrm((L, D, D), D ** -0.5)
    ple_w_proj = nrm((L, PLE_DIM, D), PLE_DIM ** -0.5)
    final_norm = 1.0 + nrm((D,), 0.1)
    return {"x": x, "p": p,
            "ffn1_norm": ffn1_norm, "ffn1_w_gate": ffn1_w_gate, "ffn1_w_up": ffn1_w_up, "ffn1_w_down": ffn1_w_down,
            "mix_norm": mix_norm,
            "lru_w_in": lru_w_in, "lru_conv_w": lru_conv_w, "lru_conv_b": lru_conv_b,
            "lru_w_a": lru_w_a, "lru_b_a": lru_b_a, "lru_w_x": lru_w_x, "lru_b_x": lru_b_x,
            "lru_a_param": lru_a_param, "lru_w_out": lru_w_out,
            "pool_w": pool_w, "pool_b": pool_b, "pool_scale": pool_scale,
            "ffn2_norm": ffn2_norm, "ffn2_w_gate": ffn2_w_gate, "ffn2_w_up": ffn2_w_up, "ffn2_w_down": ffn2_w_down,
            "ple_norm": ple_norm, "ple_w_gate": ple_w_gate, "ple_w_proj": ple_w_proj,
            "final_norm": final_norm}

def first_block(x, p, ffn1_norm, ffn1_w_gate, ffn1_w_up, ffn1_w_down, mix_norm,
              lru_w_in, lru_conv_w, lru_conv_b, lru_w_a, lru_b_a, lru_w_x, lru_b_x, lru_a_param, lru_w_out,
              pool_w, pool_b, pool_scale,
              ffn2_norm, ffn2_w_gate, ffn2_w_up, ffn2_w_down,
              ple_norm, ple_w_gate, ple_w_proj, final_norm):
    h = x
    for i in range(DEPTH):
        h = h + 0.5 * swiglu(rms_norm(h, ffn1_norm[i]), ffn1_w_gate[i], ffn1_w_up[i], ffn1_w_down[i])
        hn = rms_norm(h, mix_norm[i])
        j = i // N_MIXERS
        if i % N_MIXERS == 0:
            m = rglru_mixer(hn, lru_w_in[j], lru_conv_w[j], lru_conv_b[j], lru_w_a[j], lru_b_a[j],
                            lru_w_x[j], lru_b_x[j], lru_a_param[j], lru_w_out[j])
        else:
            m = pool_mixer(hn, pool_w[j], pool_b[j], pool_scale[j])
        h = h + m
        h = h + 0.5 * swiglu(rms_norm(h, ffn2_norm[i]), ffn2_w_gate[i], ffn2_w_up[i], ffn2_w_down[i])
        gate = jax.nn.sigmoid(rms_norm(h, ple_norm[i]) @ ple_w_gate[i])
        h = h + gate * (p[i].astype(h.dtype) @ ple_w_proj[i])
    return rms_norm(h, final_norm)


DA_HEADS = 4
DA_QK_DIM = 64
DA_V_DIM = 2 * DA_QK_DIM
DA_QK_WIDTH = DA_HEADS * 2 * DA_QK_DIM
DA_WIDTH = DA_HEADS * DA_V_DIM
ROPE_THETA = 500000.0
ROT_DIM = DA_QK_DIM // 4
Q_BLOCK = 128
HG_HEADS = 4
HG_K_DIM = 128
HG_V_DIM = 128
HG_K_WIDTH = HG_HEADS * HG_K_DIM
HG_V_WIDTH = HG_HEADS * HG_V_DIM
HG_CHUNK = 64
FFN_HIDDEN = -(-8 * D_MODEL // (3 * 256)) * 256
NORM_EPS = 1e-6
IN_SIZES = (DA_QK_WIDTH, DA_QK_WIDTH, DA_WIDTH,
            HG_K_WIDTH, HG_K_WIDTH, HG_K_WIDTH, HG_V_WIDTH, HG_V_WIDTH,
            D_MODEL, D_MODEL)
IN_WIDTH = sum(IN_SIZES)


def rmsnorm(x, gain):
    xf = x.astype(jnp.float32)
    y = xf * lax.rsqrt(jnp.mean(xf * xf, axis=-1, keepdims=True) + NORM_EPS)
    return (y * gain.astype(jnp.float32)).astype(x.dtype)

def split_columns(p):
    outs, start = [], 0
    for size in IN_SIZES:
        outs.append(p[..., start:start + size])
        start += size
    return outs

def rope_tables(positions):
    inv_freq = ROPE_THETA ** (-(jnp.arange(0, ROT_DIM, 2, dtype=jnp.float32) / ROT_DIM))
    ang = positions.astype(jnp.float32)[..., None] * inv_freq
    return jnp.cos(ang), jnp.sin(ang)

def apply_partial_rope(t, cos, sin):
    c = cos[:, :, None, None, :].astype(t.dtype)
    s = sin[:, :, None, None, :].astype(t.dtype)
    half = ROT_DIM // 2
    t1 = t[..., :half]
    t2 = t[..., half:ROT_DIM]
    rot = jnp.concatenate([t1 * c - t2 * s, t2 * c + t1 * s], axis=-1)
    return jnp.concatenate([rot, t[..., ROT_DIM:]], axis=-1)

def diff_attention(h_q, h_k, h_v, cos, sin, lam, norm_gain, layer):
    B, S, _ = h_q.shape
    q = h_q.reshape(B, S, DA_HEADS, 2, DA_QK_DIM)
    k = h_k.reshape(B, S, DA_HEADS, 2, DA_QK_DIM)
    v = h_v.reshape(B, S, DA_HEADS, DA_V_DIM)
    q = apply_partial_rope(q, cos, sin) * (DA_QK_DIM ** -0.5)
    k = apply_partial_rope(k, cos, sin)
    lam_init = 0.8 - 0.6 * math.exp(-0.3 * layer)
    l32 = lam.astype(jnp.float32)
    lam_full = (jnp.exp(jnp.sum(l32[0] * l32[1])) - jnp.exp(jnp.sum(l32[2] * l32[3]))
                + lam_init)
    nq = S // Q_BLOCK
    qb = q.reshape(B, nq, Q_BLOCK, DA_HEADS, 2, DA_QK_DIM).transpose(1, 0, 2, 3, 4, 5)

    def block(qi):
        s = jnp.einsum('bqhcd,bkhcd->bhcqk', qi, k).astype(jnp.float32)
        p = jax.nn.softmax(s, axis=-1)
        w = p[:, :, 0] - lam_full * p[:, :, 1]
        return jnp.einsum('bhqk,bkhv->bqhv', w.astype(v.dtype), v)

    o = lax.map(block, qb)
    o = o.transpose(1, 0, 2, 3, 4).reshape(B, S, DA_HEADS, DA_V_DIM)
    o = rmsnorm(o, norm_gain.reshape(DA_HEADS, DA_V_DIM)) * (1.0 - lam_init)
    return o.reshape(B, S, DA_WIDTH)

def hgrn_lower_bounds(lb_logits):
    p = jax.nn.softmax(lb_logits.astype(jnp.float32), axis=1)
    c = jnp.cumsum(p, axis=1)
    return c - c[:, :1]

def log_forget(z, lb):
    return jnp.logaddexp(jnp.log(lb), jnp.log1p(-lb) + jax.nn.log_sigmoid(z))

def chunk_scan(q, k, g, v):
    B, S, H, dk = q.shape
    dv = v.shape[-1]
    n = S // HG_CHUNK

    def to_chunks(t):
        return t.reshape(B, n, HG_CHUNK, H, t.shape[-1]).transpose(1, 0, 3, 2, 4)

    tril = jnp.tril(jnp.ones((HG_CHUNK, HG_CHUNK), dtype=bool))

    def step(state, inp):
        qc, kc, gc, vc = inp
        b = jnp.cumsum(gc, axis=2)
        inter = jnp.einsum('bhck,bhkv->bhcv', qc * jnp.exp(b), state)
        diff = b[:, :, :, None, :] - b[:, :, None, :, :]
        decay = jnp.exp(jnp.where(tril[:, :, None], diff, -jnp.inf))
        scores = jnp.einsum('bhtk,bhsk,bhtsk->bhts', qc, kc, decay)
        intra = jnp.einsum('bhts,bhsv->bhtv', scores, vc)
        b_last = b[:, :, -1, :]
        state = (jnp.exp(b_last)[..., None] * state
                 + jnp.einsum('bhck,bhcv->bhkv', kc * jnp.exp(b_last[:, :, None, :] - b), vc))
        return state, inter + intra

    s0 = jnp.zeros((B, H, dk, dv), jnp.float32)
    _, out = lax.scan(step, s0, (to_chunks(q), to_chunks(k), to_chunks(g), to_chunks(v)))
    return out.transpose(1, 0, 3, 2, 4).reshape(B, S, H, dv)

def hgrn2_bidirectional(h_q, h_ff, h_fb, h_i, h_g, lb_f, lb_b, norm_gain):
    B, S, _ = h_q.shape
    f32 = jnp.float32
    q = h_q.astype(f32).reshape(B, S, HG_HEADS, HG_K_DIM)
    v = h_i.astype(f32).reshape(B, S, HG_HEADS, HG_V_DIM)
    g_f = log_forget(h_ff.astype(f32).reshape(B, S, HG_HEADS, HG_K_DIM),
                     lb_f.reshape(HG_HEADS, HG_K_DIM))
    g_b = log_forget(h_fb.astype(f32).reshape(B, S, HG_HEADS, HG_K_DIM),
                     lb_b.reshape(HG_HEADS, HG_K_DIM))
    k_f = -jnp.expm1(g_f)
    k_b = -jnp.expm1(g_b)
    out_f = chunk_scan(q, k_f, g_f, v)
    out_b = chunk_scan(q[:, ::-1], k_b[:, ::-1], g_b[:, ::-1], v[:, ::-1])[:, ::-1]
    o = rmsnorm(out_f + out_b, norm_gain.reshape(HG_HEADS, HG_V_DIM))
    o = o * jax.nn.sigmoid(h_g.astype(f32).reshape(B, S, HG_HEADS, HG_V_DIM))
    return o.reshape(B, S, HG_V_WIDTH).astype(h_q.dtype)

def second_inputs(seed: int = 0) -> dict:
    key = jax.random.key(seed)
    ks = jax.random.split(key, 18)
    nrm = jax.random.normal
    f32 = jnp.float32
    x = nrm(ks[0], (BATCH, SEQ, D_MODEL), f32)
    offset = jax.random.randint(ks[1], (BATCH, 1), 0, 1024, dtype=jnp.int32)
    positions = offset + jnp.arange(SEQ, dtype=jnp.int32)[None, :]
    w_in = nrm(ks[2], (DEPTH, D_MODEL, IN_WIDTH), f32) * D_MODEL ** -0.5
    da_lambda = nrm(ks[3], (DEPTH, 4, DA_QK_DIM), f32) * 0.1
    da_norm = 1.0 + 0.02 * nrm(ks[4], (DEPTH, DA_WIDTH), f32)
    hg_lb_logits = 0.5 * nrm(ks[5], (2, DEPTH, HG_K_WIDTH), f32)
    hg_norm = 1.0 + 0.02 * nrm(ks[6], (DEPTH, HG_V_WIDTH), f32)
    w_a = nrm(ks[7], (DEPTH, DA_WIDTH, D_MODEL), f32) * DA_WIDTH ** -0.5
    w_b = nrm(ks[8], (DEPTH, HG_V_WIDTH, D_MODEL), f32) * HG_V_WIDTH ** -0.5
    w_o = nrm(ks[9], (DEPTH, D_MODEL, D_MODEL), f32) * D_MODEL ** -0.5
    attn_norm = 1.0 + 0.02 * nrm(ks[10], (DEPTH, D_MODEL), f32)
    ffn_norm = 1.0 + 0.02 * nrm(ks[11], (DEPTH, D_MODEL), f32)
    w_gate = nrm(ks[12], (DEPTH, D_MODEL, FFN_HIDDEN), f32) * D_MODEL ** -0.5
    w_up = nrm(ks[13], (DEPTH, D_MODEL, FFN_HIDDEN), f32) * D_MODEL ** -0.5
    w_down = nrm(ks[14], (DEPTH, FFN_HIDDEN, D_MODEL), f32) * FFN_HIDDEN ** -0.5
    final_norm = 1.0 + 0.02 * nrm(ks[15], (D_MODEL,), f32)
    return {"x": x, "positions": positions, "w_in": w_in, "da_lambda": da_lambda,
            "da_norm": da_norm, "hg_lb_logits": hg_lb_logits, "hg_norm": hg_norm,
            "w_a": w_a, "w_b": w_b, "w_o": w_o, "attn_norm": attn_norm,
            "ffn_norm": ffn_norm, "w_gate": w_gate, "w_up": w_up, "w_down": w_down,
            "final_norm": final_norm}

def second_block(x, positions, w_in, da_lambda, da_norm, hg_lb_logits, hg_norm, w_a, w_b,
              w_o, attn_norm, ffn_norm, w_gate, w_up, w_down, final_norm):
    cos, sin = rope_tables(positions)
    lbs = hgrn_lower_bounds(hg_lb_logits)
    for layer in range(DEPTH):
        h = rmsnorm(x, attn_norm[layer])
        proj = h @ w_in[layer]
        (a_q, a_k, a_v, b_q, b_ff, b_fb, b_i, b_g, gate_a, gate_b) = split_columns(proj)
        y_a = diff_attention(a_q, a_k, a_v, cos, sin, da_lambda[layer], da_norm[layer],
                             layer) @ w_a[layer]
        y_b = hgrn2_bidirectional(b_q, b_ff, b_fb, b_i, b_g,
                                  lbs[0, layer].astype(x.dtype).astype(jnp.float32),
                                  lbs[1, layer].astype(x.dtype).astype(jnp.float32),
                                  hg_norm[layer]) @ w_b[layer]
        merged = jax.nn.sigmoid(gate_a) * y_a + jax.nn.sigmoid(gate_b) * y_b
        x = x + merged @ w_o[layer]
        h = rmsnorm(x, ffn_norm[layer])
        x = x + (jax.nn.silu(h @ w_gate[layer]) * (h @ w_up[layer])) @ w_down[layer]
    return rmsnorm(x, final_norm)


def setup_inputs(seed=0):
    out = dict(first_inputs(seed))
    for name, value in second_inputs(seed + 1).items():
        if name != "x":
            out[name + "_2"] = value
    return out


def reference(
    x, p, ffn1_norm, ffn1_w_gate, ffn1_w_up, ffn1_w_down, mix_norm, lru_w_in, lru_conv_w,
    lru_conv_b, lru_w_a, lru_b_a, lru_w_x, lru_b_x, lru_a_param, lru_w_out, pool_w, pool_b,
    pool_scale, ffn2_norm, ffn2_w_gate, ffn2_w_up, ffn2_w_down, ple_norm, ple_w_gate,
    ple_w_proj, final_norm, positions_2, w_in_2, da_lambda_2, da_norm_2, hg_lb_logits_2,
    hg_norm_2, w_a_2, w_b_2, w_o_2, attn_norm_2, ffn_norm_2, w_gate_2, w_up_2, w_down_2,
    final_norm_2,
):
    x = first_block(
        x, p, ffn1_norm, ffn1_w_gate, ffn1_w_up, ffn1_w_down, mix_norm, lru_w_in, lru_conv_w,
        lru_conv_b, lru_w_a, lru_b_a, lru_w_x, lru_b_x, lru_a_param, lru_w_out, pool_w, pool_b,
        pool_scale, ffn2_norm, ffn2_w_gate, ffn2_w_up, ffn2_w_down, ple_norm, ple_w_gate,
        ple_w_proj, final_norm,
    )
    return second_block(
        x, positions_2, w_in_2, da_lambda_2, da_norm_2, hg_lb_logits_2, hg_norm_2, w_a_2, w_b_2,
        w_o_2, attn_norm_2, ffn_norm_2, w_gate_2, w_up_2, w_down_2, final_norm_2,
    )


_drawn_inputs = setup_inputs


def setup_inputs(seed=0):
    import zlib

    import numpy as np

    out = dict(_drawn_inputs(seed))
    spreads = {}
    factors = {'lru_b_a': 24.319,
     'lru_b_x': 8.0,
     'da_norm_2': 4.692,
     'hg_norm_2': 7.232,
     'ffn_norm_2': 2.906,
     'final_norm_2': 8.271}
    for name, (base, spread) in spreads.items():
        noise = np.random.default_rng([zlib.crc32(name.encode()), seed]).standard_normal(out[name].shape)
        drawn = base * np.exp(spread * noise) if base else spread * noise
        out[name] = __import__('jax').numpy.asarray(drawn.astype(out[name].dtype))
    for name, factor in factors.items():
        out[name] = (out[name] * factor).astype(out[name].dtype)
    return out
```

```python
from contextlib import ExitStack

import numpy as np
import concourse.bass as bass
from concourse import mybir

F32 = mybir.dt.float32
F32R = mybir.dt.float32r
I32 = mybir.dt.int32
ALU = mybir.AluOpType
ACT = mybir.ActivationFunctionType
AX_X = mybir.AxisListType.X

P = 128
S = 256
T = S // P
D = 1024
KT = D // P
F = 2816
R = 1280
RT = R // P
HD = 80
GT = 5
EPS = 1e-6
BW = 2048
FC = 256
CH = F // FC
RAW = 3
RING = 3
AHEAD = 2
HEADS = 4
LEVELS = (128, 64, 32, 16, 8, 4, 2, 1)
POOL_WINDOWS = (2, 4, 8, 16)
ROT = 8
TWO_PI = 6.283185307179586
PI_HI, PI_MID = 6.28125, 0.0019350051879882812
PI_LO = TWO_PI - PI_HI - PI_MID
ROUND = 12582912.0
LAM_INIT = [0.8 - 0.6 * float(np.exp(-0.3 * l)) for l in range(2)]

XN = 0
SIL, PROD = 2048, 3072
SIG = 2048
PTOK = 8192
L_R = 0
L_XB = 2560
L_XC = L_XB + RT * (S + 3) + 2
L_GELU = L_XC + RT * S
L_IG = L_GELU + RT * S
L_T = L_IG + RT * S
BAND = L_T + GT * S
POOL_M, POOL_B, POOL_S = 4096, 6144, 7168
Z, Q_B, V_B, A_QK, A_V, G_B, GATE_A, GATE_B = 2048, 4096, 5120, 6144, 8192, 9216, 10240, 12288
LOGF, TMP, KK = 14336, 16384, 18432
NRM_DA, NRM_HG, LAM = 20480, 20992, 21504
SCRATCH = 22016
assert BAND + 2 * 2 * GT * 384 <= SCRATCH


def head_pieces():
    out = []
    for head in range(8):
        row = 0
        while row < HD:
            at = head * HD + row
            n = min(HD - row, P - at % P)
            out.append((head, row, at // P, at % P, n))
            row += n
    return out


def build(nc, a, out):
    ctx = ExitStack()

    def sb(name, shape, dt=F32):
        return ctx.enter_context(nc.sbuf_tensor(name, shape, dt))

    def sem(name):
        return ctx.enter_context(nc.semaphore(name))

    with ctx:
        raw = sb("raw", [P, RAW, BW])
        hi = sb("hi", [P, RING, BW], F32R)
        lo = sb("lo", [P, RING, BW], F32R)
        h = sb("h", [P, T, D])
        xTh = sb("xTh", [P, RT, S], F32R)
        xTl = sb("xTl", [P, RT, S], F32R)
        prod_hi = sb("prod_hi", [P, 2, 2, S], F32R)
        prod_lo = sb("prod_lo", [P, 2, 2, S], F32R)
        gain = sb("gain", [P, D])
        ident = sb("ident", [P, P])
        level_mask = sb("level_mask", [P, len(LEVELS), P], I32)
        scr = sb("scr", [P, SCRATCH])
        stat = sb("stat", [P, 64])
        conv_w = sb("conv_w", [P, 4, RT])
        lru_c = sb("lru_c", [P, 4, RT])
        cpos = sb("cpos", [P, 6, RT])
        eps = sb("eps", [P, 2])
        rope_in = sb("rope_in", [P, 2 * ROT])
        pos_i = sb("pos_i", [P, T], I32)
        rope = sb("rope", [P, 8, T, ROT])
        one_row = sb("one_row", [P, P])
        lbt = sb("lbt", [P, 12, 2, HEADS])

        psA = ctx.enter_context(nc.psum_tensor("psA", [P, 4, 512], F32))
        psD = ctx.enter_context(nc.psum_tensor("psD", [P, 4, 512], F32))

        def view(at, *shape):
            n = int(np.prod(shape))
            v = scr[:, at:at + n]
            names = "abcd"[:len(shape)]
            if len(shape) == 1:
                return v
            return v.rearrange(f"p ({' '.join(names)}) -> p {' '.join(names)}", **dict(zip(names[1:], shape[1:])))

        xn = view(XN, T, D)
        sil, prod = view(SIL, 2, 2 * S), view(PROD, 2, 2 * S)

        raw_landed = [sem(f"raw_landed{i}") for i in range(RAW)]
        hi_ready, lo_ready, block_used = sem("hi_ready"), sem("lo_ready"), sem("block_used")
        x_loaded, consts_loaded, gain_loaded = sem("x_loaded"), sem("consts_loaded"), sem("gain_loaded")
        band_zeroed, band_loaded = sem("band_zeroed"), sem("band_loaded")
        p_loaded, pool_loaded, mix_loaded = sem("p_loaded"), sem("pool_loaded"), sem("mix_loaded")
        lb_loaded = sem("lb_loaded")
        h_ready, ssq_ready, rms_ready, xn_ready = sem("h_ready"), sem("ssq_ready"), sem("rms_ready"), sem("xn_ready")
        turned, xTh_ready, xT_ready = sem("turned"), sem("xTh_ready"), sem("xT_ready")
        silu_ready, prod_ready = sem("silu_ready"), sem("prod_ready")
        prod_hi_ready, prod_lo_ready = sem("prod_hi_ready"), sem("prod_lo_ready")
        dve_step, act_step = sem("dve_step"), sem("act_step")
        eps_ready, cpos_exp, cpos_ready = sem("eps_ready"), sem("cpos_exp"), sem("cpos_ready")
        xb_ready, xc_ready, gates_done, gates_ready = sem("xb_ready"), sem("xc_ready"), sem("gates_done"), sem("gates_ready")
        tanh_ready, decay_ready, ratio_ready, mult_ready = sem("tanh_ready"), sem("decay_ready"), sem("ratio_ready"), sem("mult_ready")
        gelu_ready, y_ready, sig_ready = sem("gelu_ready"), sem("y_ready"), sem("sig_ready")
        angles_ready, rope_ready = sem("angles_ready"), sem("rope_ready")
        proj_evac = sem("proj_evac")
        absz_ready, soft_ready, kk_ready = sem("absz_ready"), sem("soft_ready"), sem("kk_ready")
        lb_in, lb_out = sem("lb_in"), sem("lb_out")
        decay_in, decay_out = sem("decay_in"), sem("decay_out")
        scaled_ready, pair_done, pair_taken = sem("scaled_ready"), sem("pair_done"), sem("pair_taken")
        rec_done, rec_square, rec_sum, rec_rms, rec_ready = sem("rec_done"), sem("rec_square"), sem("rec_sum"), sem("rec_rms"), sem("rec_ready")
        roped, qk_turned, qkT_ready = sem("roped"), sem("qk_turned"), sem("qkT_ready")
        scores_done, max_ready, exp_ready, w_ready = sem("scores_done"), sem("max_ready"), sem("exp_ready"), sem("w_ready")
        w_turned, wT_ready, att_done = sem("w_turned"), sem("wT_ready"), sem("att_done")
        att_square, att_sum, att_rms, att_ready = sem("att_square"), sem("att_sum"), sem("att_rms"), sem("att_ready")
        lam_in, lam_exp = sem("lam_in"), sem("lam_exp")
        merged = sem("merged")
        stored = sem("stored")

        def columns(w, c, n=FC):
            return w[:, c * n:(c + 1) * n].rearrange("(k p) f -> p k f", p=P)

        def rows(w, c):
            return w[c * 2 * P:(c + 1) * 2 * P, :].rearrange("(k p) n -> p k n", p=P)

        def dst(n, src):
            k = src.shape[1]
            return raw[:, n % RAW, :].rearrange("p (k f) -> p k f", k=k)

        plan = []
        for i in range(2):
            plan += [("norm", a["ffn1_norm"][i]), ("ffn", a["ffn1_w_gate"][i], a["ffn1_w_up"][i], a["ffn1_w_down"][i], 0.5)]
            plan += [("norm", a["mix_norm"][i]), ("lru",)] if i == 0 else [("pool", a["mix_norm"][i])]
            plan += [("norm", a["ffn2_norm"][i]), ("ffn", a["ffn2_w_gate"][i], a["ffn2_w_up"][i], a["ffn2_w_down"][i], 0.5)]
            plan += [("norm", a["ple_norm"][i]), ("ple", i)]
        plan += [("rescale", a["final_norm"])]
        for l in range(2):
            plan += [("norm", a["attn_norm_2"][l]), ("mix", l)]
            plan += [("norm", a["ffn_norm_2"][l]), ("ffn", a["w_gate_2"][l], a["w_up_2"][l], a["w_down_2"][l], 1.0)]
        plan += [("rescale", a["final_norm_2"])]
        BLOCKS = {"norm": 0, "rescale": 0, "ffn": 3 * CH, "lru": 2 * R // FC + R // (2 * P), "pool": 1, "ple": KT // 2 + 1,
                  "mix": 6 * D // FC + 8}
        CONSTS = 13
        TOTAL = sum(BLOCKS[s[0]] for s in plan)
        gains = [s[1] for s in plan if s[0] in ("norm", "pool", "rescale")]
        PROJ = [6 * 2 + b for b in range(2)]
        FF, FB, QB, IB, AQ, AK, AV, GB_ = 8, 10, 6, 12, 0, 2, 4, 14
        PROJ = [(c + j, c) for c in (FF, FB, QB, IB, AQ, AK, AV, GB_) for j in range(2)]
        PROJ += [(16 + j, 16) for j in range(4)] + [(20 + j, 20) for j in range(4)]

        block = ctx.enter_context(nc.Block())

        @block.sync
        def _(sp):
            n = 0

            def load(n_at, n, src):
                if isinstance(n_at, int):
                    if n_at >= RAW:
                        sp.wait_ge(lo_ready, n_at - RAW + 1)
                else:
                    sp.wait_ge(lo_ready, n_at - (RAW - 1))
                sp.dma_start(dst(n, src), src).then_inc(raw_landed[n % RAW], 16)

            for stage in plan:
                kind = stage[0]
                if kind == "ffn":
                    _, wg, wu, wd, _ = stage
                    for src in (columns(wg, 0), columns(wu, 0), columns(wg, 1), columns(wu, 1), rows(wd, 0)):
                        load(n, n, src)
                        n += 1
                    with sp.Fori(0, (CH - 3) // 2) as j:
                        for e in range(2):
                            up = wg[:, bass.ds((2 * j + (e + 2)) * FC, FC)], wu[:, bass.ds((2 * j + (e + 2)) * FC, FC)]
                            down = wd[bass.ds((2 * j + (e + 1)) * FC, FC), :]
                            for b, src in enumerate([x.rearrange("(k p) f -> p k f", p=P) for x in (*up, down)]):
                                load(6 * j + (n + 3 * e + b), n + 3 * e + b, src)
                    n += 3 * (CH - 3)
                    for src in (columns(wg, CH - 1), columns(wu, CH - 1), rows(wd, CH - 2), rows(wd, CH - 1)):
                        load(n, n, src)
                        n += 1
                    continue
                srcs = []
                if kind == "lru":
                    w_in = a["lru_w_in"][0]
                    half = R // FC
                    srcs = [columns(w_in, half + c) for c in range(half)] + [columns(w_in, c) for c in range(half)]
                    srcs += [rows(a["lru_w_out"][0], c) for c in range(R // (2 * P))]
                if kind == "pool":
                    src = a["pool_w"][0].rearrange("g (k p) d -> p (g k) d", p=P)
                    srcs = [src]
                if kind == "ple":
                    srcs = [rows(a["ple_w_gate"][stage[1]], c) for c in range(KT // 2)] + [rows(a["ple_w_proj"][stage[1]], 0)]
                if kind == "mix":
                    l = stage[1]
                    srcs = [columns(a["w_in_2"][l], c) for c, _ in PROJ]
                    srcs += [rows(a["w_a_2"][l], c) for c in range(2)] + [rows(a["w_b_2"][l], c) for c in range(2)]
                    srcs += [rows(a["w_o_2"][l], c) for c in range(4)]
                for src in srcs:
                    load(n, n, src)
                    n += 1
            assert n == TOTAL
            updates = 2 * (1 + sum(s[0] in ("ffn", "lru", "pool", "ple", "mix", "rescale") for s in plan))
            sp.wait_ge(h_ready, updates)
            sp.dma_start(out.rearrange("b (t p) d -> p (b t) d", p=P), h[:]).then_inc(stored, 16)
            sp.wait_ge(stored, 16)

        @block.gpsimd
        def _(pool):
            band = view(BAND, 2, 2, GT, 384)
            pool.memset(scr[:, BAND:BAND + 2 * 2 * GT * 384], 0.0).then_inc(band_zeroed, 1)
            pool.dma_start(h[:], a["x"].rearrange("b (t p) d -> p (b t) d", p=P)).then_inc(x_loaded, 16)
            pool.dma_start(gain[:], gains[0].rearrange("(o d) -> o d", o=1).broadcast_to([P, D])).then_inc(gain_loaded, 16)
            for t_, src in ((ident[:], a["c_ident"]), (level_mask[:], a["c_level"]), (rope_in[:], a["c_freq"]),
                            (pos_i[:], a["positions_2"].rearrange("b (t p) -> p (b t)", p=P)),
                            (conv_w[:], a["lru_conv_w"][0].rearrange("k (f p) -> p k f", p=P)),
                            (lru_c[:, 0, :], a["lru_conv_b"][0].rearrange("(f p) -> p f", p=P)),
                            (lru_c[:, 1, :], a["lru_b_a"][0].rearrange("(f p) -> p f", p=P)),
                            (lru_c[:, 2, :], a["lru_b_x"][0].rearrange("(f p) -> p f", p=P)),
                            (lru_c[:, 3, :], a["lru_a_param"][0].rearrange("(f p) -> p f", p=P)),
                            *((lbt[:, l, e, :], a["hg_lb_logits_2"][e, l, :].rearrange("(f p) -> p f", p=P)) for l in range(2) for e in range(2))):
                pool.dma_start(t_, src, allow_slow_non_contiguous=True).then_inc(consts_loaded, 16)
            pool.wait_ge(band_zeroed, 1)
            for m, w in enumerate((a["lru_w_a"][0], a["lru_w_x"][0])):
                for head, row, tile, part, cnt in head_pieces():
                    col = head * HD - (tile - 1) * P
                    for g in range(2):
                        pool.dma_start(band[part:part + cnt, m, g, tile, col:col + HD],
                                       w[8 * g + head, row:row + cnt, :]).then_inc(band_loaded, 16)
            normed = updates = 0
            for stage in plan:
                kind = stage[0]
                if kind in ("norm", "pool", "rescale"):
                    normed += 1
                    if normed < len(gains):
                        pool.wait_ge(xn_ready, 2 * normed)
                        pool.dma_start(gain[:], gains[normed].rearrange("(o d) -> o d", o=1).broadcast_to([P, D])).then_inc(gain_loaded, 16)
                if kind in ("ffn", "lru", "pool", "ple", "mix", "rescale"):
                    updates += 1
                if kind == "lru":
                    pool.wait_ge(h_ready, 2 * updates + 2)
                    pool.dma_start(view(POOL_M, T, 4, S), a["c_pool"]).then_inc(pool_loaded, 16)
                    pool.dma_start(view(POOL_B, D), a["pool_b"].broadcast_to([P, D])).then_inc(pool_loaded, 16)
                    pool.dma_start(view(POOL_S, D), a["pool_scale"].broadcast_to([P, D])).then_inc(pool_loaded, 16)
                if kind == "lru" or kind == "ple" and stage[1] == 0:
                    i = 0 if kind == "lru" else 1
                    pool.wait_ge(h_ready, 2 * updates + 2)
                    pool.dma_start(view(PTOK, T, S), a["p"][i].rearrange("b (t p) d -> p (b t) d", p=P)).then_inc(p_loaded, 16)
                if kind == "lru" or kind == "mix" and stage[1] == 0:
                    l = 0 if kind == "lru" else 1
                    pool.wait_ge(h_ready, 2 * updates + 2)
                    pool.dma_start(view(NRM_DA, 512), a["da_norm_2"][l].rearrange("(o d) -> o d", o=1).broadcast_to([P, 512])).then_inc(mix_loaded, 16)
                    pool.dma_start(view(NRM_HG, 512), a["hg_norm_2"][l].rearrange("(o d) -> o d", o=1).broadcast_to([P, 512])).then_inc(mix_loaded, 16)
                    pool.dma_start(view(LAM, 256), a["da_lambda_2"][l].rearrange("(o i) d -> o (i d)", o=1).broadcast_to([P, 256])).then_inc(mix_loaded, 16)

        def norm_piece(t):
            ps = psA[:, 2 * t:2 * t + 2, :].rearrange("p b (k s) -> p (b k) s", k=4)
            return ps, (slice(0, KT), slice(t * P, (t + 1) * P))

        def pool_piece(t):
            ps = psA[:, 2 * t:2 * t + 2, :].rearrange("p b (k s) -> p (b k) s", k=2)
            return ps, (slice(4 * t, 4 * t + 4), slice(0, S))

        def ple_piece():
            return psD[:, 0, :].rearrange("p (k s) -> p k s", k=2), (slice(8, 10), slice(0, S))

        def merge_piece(t):
            ps = psD[:, 2 * t:2 * t + 2, :].rearrange("p b (k s) -> p (b k) s", k=4)
            return ps, (slice(0, KT), slice(t * P, (t + 1) * P))

        def rec_piece():
            return psD[:, 0:2, :].rearrange("p b (k s) -> p (b k) s", k=2), (slice(4, 8), slice(0, S))

        def att_piece():
            return psD[:, 2:4, :].rearrange("p b (k s) -> p (b k) s", k=2), (slice(0, 4), slice(0, S))

        def halves(v, m):
            return v.rearrange("p (n e m) -> p n e m", e=2, m=m)

        def span(v):
            return v.rearrange("p a b -> p (a b)")

        @block.scalar
        def _(act):
            st = {"split": 0, "norm": 0, "updates": 0, "piece": 0, "ffn": 0, "step": 0}

            def step(ins):
                ins.then_inc(act_step, 1)
                st["step"] += 1

            def settle():
                act.wait_ge(act_step, st["step"])

            def split(n_at, n):
                if isinstance(n_at, int):
                    act.wait_ge(raw_landed[n % RAW], 16 * (n // RAW + 1))
                    if n >= RING:
                        act.wait_ge(block_used, n - RING + 1)
                else:
                    act.wait_ge(raw_landed[n % RAW], 32 * n_at + 16 * (n // RAW + 1))
                    act.wait_ge(block_used, 6 * n_at + (n - RING + 1))
                act.activation(hi[:, n % RING, :], raw[:, n % RAW, :], ACT.Copy).then_inc(hi_ready, 1)

            def split_to(n):
                while st["split"] <= min(n + AHEAD, TOTAL - 1):
                    split(st["split"], st["split"])
                    st["split"] += 1

            def piece(src, to, wait=None):
                st["piece"] += 1
                if wait is None:
                    act.wait_ge(turned, st["turned"])
                act.activation(xTh[:, to[0], to[1]], src, ACT.Copy).then_inc(xTh_ready, 1)

            st["turned"] = 0

            def norm_stats():
                for t in range(T):
                    act.wait_ge(h_ready, 2 * st["updates"] + 1 + t)
                    act.activation(xn[:, t, :], h[:, t, :], ACT.Square, accum_out=stat[:, t:t + 1]).then_inc(ssq_ready, 1)
                st["norm"] += 1
                act.wait_ge(ssq_ready, 2 * st["norm"])
                act.activation(stat[:, 2:4], stat[:, 0:2], ACT.Sqrt, bias=eps[:, 0:1], scale=1.0 / D).then_inc(rms_ready, 1)

            act.wait_ge(x_loaded, 16)
            act.wait_ge(eps_ready, 2)
            n = 0
            act.wait_ge(cpos_exp, 1)
            act.activation(cpos[:, 1, :], cpos[:, 0, :], ACT.Exp, scale=-1.0).then_inc(cpos_exp, 1)
            act.wait_ge(angles_ready, 1)
            act.activation(rope[:, 0, :, :], rope[:, 4, :, :], ACT.Sin).then_inc(rope_ready, 1)
            act.activation(rope[:, 1, :, :], rope[:, 5, :, :], ACT.Sin).then_inc(rope_ready, 1)
            act.wait_ge(lb_in, 1)
            act.activation(lbt[:, 4, :, :], lbt[:, 3, :, :], ACT.Exp, scale=-1.0).then_inc(lb_out, 1)
            act.wait_ge(lb_out, 1)
            act.activation(lbt[:, 5, :, :], lbt[:, 4, :, :], ACT.Ln, bias=eps[:, 1:2]).then_inc(lb_out, 1)
            act.activation(lbt[:, 6, :, :], lbt[:, 2, :, :], ACT.Sigmoid, scale=-1.0).then_inc(lb_out, 1)

            for stage in plan:
                kind = stage[0]
                if kind == "norm":
                    split_to(n - 1)
                    norm_stats()
                    for t in range(T):
                        st["turned"] += 1
                        piece(*norm_piece(t))
                if kind == "rescale":
                    split_to(n - 1)
                    norm_stats()
                    st["updates"] += 1
                if kind == "pool":
                    split_to(n - 1)
                    norm_stats()
                    for t in range(T):
                        st["turned"] += 1
                        piece(*pool_piece(t))
                    split_to(n)
                    n += 1
                    st["updates"] += 1
                if kind == "ffn":
                    def gated(c_at, c, used):
                        act.wait_ge(block_used, used)
                        act.activation(sil[:, c % 2, :], psA[:, c % 2, :], ACT.Silu).then_inc(silu_ready, 1)
                        act.wait_ge(prod_ready, c_at + 1)
                        act.activation(span(prod_hi[:, c % 2]), prod[:, c % 2, :], ACT.Copy).then_inc(prod_hi_ready, 1)

                    c0 = st["ffn"] * CH
                    for b in range(5):
                        split_to(n)
                        if b in (1, 3):
                            gated(c0 + b // 2, b // 2, n + 1)
                        n += 1
                    with act.Fori(0, (CH - 3) // 2) as j:
                        for b in range(6):
                            split(j, n + b + AHEAD)
                            if b % 3 == 1:
                                gated(2 * j + (c0 + 2 + b // 3), b // 3, 6 * j + (n + b + 1))
                    n += 3 * (CH - 3)
                    st["split"] += 3 * (CH - 3)
                    for b in range(4):
                        split_to(n)
                        if b == 1:
                            gated(c0 + CH - 1, CH - 1, n + 1)
                        n += 1
                    st["ffn"] += 1
                    st["updates"] += 1
                if kind == "lru":
                    half = R // FC
                    xb = view(L_XB, RT, S + 3) if (RT * (S + 3)) else None
                    gelu = view(L_GELU, RT, S)
                    r, ig, th = view(L_R, RT, S), view(L_IG, RT, S), view(L_T, GT, S)
                    ratio = view(L_XB, RT, S)

                    def recurrent_gates(g):
                        for m in range(GT):
                            ft = g * GT + m
                            act.wait_ge(gates_done, ft + 1)
                            act.activation(r[:, ft, :], psD[:, ft % 4, 0:S], ACT.Sigmoid, bias=lru_c[:, 1, ft:ft + 1]).then_inc(gates_ready, 1)
                            act.activation(ig[:, ft, :], psD[:, ft % 4, S:2 * S], ACT.Sigmoid, bias=lru_c[:, 2, ft:ft + 1]).then_inc(gates_ready, 1)
                        if g:
                            act.wait_ge(ratio_ready, g)
                        act.wait_ge(cpos_ready, 2)
                        act.wait_ge(gates_ready, 2 * GT * (g + 1))
                        for m in range(GT):
                            ft = g * GT + m
                            act.activation(th[:, m, :], r[:, ft, :], ACT.Tanh, scale=cpos[:, 4, ft:ft + 1]).then_inc(tanh_ready, 1)

                    def recurrent_decay(g):
                        act.wait_ge(tanh_ready, GT * (g + 1))
                        for m in range(GT):
                            ft = g * GT + m
                            act.activation(r[:, ft, :], r[:, ft, :], ACT.Exp, scale=cpos[:, 5, ft:ft + 1]).then_inc(decay_ready, 1)
                        act.wait_ge(ratio_ready, g + 1)
                        v = ratio[:, g * GT:(g + 1) * GT, :]
                        act.activation(v, v, ACT.Sqrt, scale=2.0).then_inc(mult_ready, 1)

                    for i in range(2 * half):
                        split_to(n)
                        act.wait_ge(block_used, n + 1)
                        ps = psA[:, i % 4, :].rearrange("p (f s) -> p f s", f=2)
                        if i < half:
                            act.activation(xb[:, 2 * i:2 * i + 2, 3:S + 3], ps, ACT.Copy).then_inc(xb_ready, 1)
                        else:
                            i2 = 2 * (i - half)
                            act.activation(gelu[:, i2:i2 + 2, :], ps, ACT.Gelu_apprx_tanh).then_inc(gelu_ready, 1)
                        n += 1
                        if i == half:
                            recurrent_gates(0)
                        if i == half + 1:
                            recurrent_gates(1)
                        if i in (half + 2, half + 3):
                            recurrent_decay(i - half - 2)
                    for g in range(2):
                        act.wait_ge(y_ready, g + 1)
                        act.wait_ge(block_used, n)
                        piece(view(L_XC, RT, S)[:, g * GT:(g + 1) * GT, :], (slice(g * GT, (g + 1) * GT), slice(0, S)), wait="y")
                    for i in range(R // (2 * P)):
                        split_to(n)
                        n += 1
                    st["updates"] += 1
                if kind == "ple":
                    st["turned"] += 1
                    piece(*ple_piece())
                    for i in range(KT // 2 + 1):
                        split_to(n)
                        n += 1
                    sig = view(SIG, T, D)
                    for t in range(T):
                        act.wait_ge(block_used, n - 1)
                        act.activation(sig[:, t, :], span(psD[:, 2 * t:2 * t + 2, :]), ACT.Sigmoid).then_inc(sig_ready, 1)
                    st["updates"] += 1
                if kind == "mix":
                    l = stage[1]
                    z2 = view(Z, 2 * HEADS * S)
                    tmp2, e2 = view(TMP, 2 * HEADS * S), view(LOGF, 2 * HEADS * S)

                    def soft(nth):
                        act.wait_ge(absz_ready, nth)
                        step(act.activation(tmp2, tmp2, ACT.Exp, scale=-1.0))
                        settle()
                        act.activation(tmp2, tmp2, ACT.Ln, bias=eps[:, 1:2]).then_inc(soft_ready, 1)

                    def level(i):
                        act.wait_ge(decay_in, len(LEVELS) * l + i + 1)
                        act.activation(e2, e2, ACT.Exp).then_inc(decay_out, 1)

                    for i, (c, first) in enumerate(PROJ):
                        split_to(n)
                        act.wait_ge(block_used, n + 1)
                        j = c - first
                        ps = psA[:, i % 4, :].rearrange("p (f s) -> p f s", f=2)
                        if first in (FF, FB, QB):
                            at = {FF: Z, FB: Z + 1024, QB: Q_B}[first] + 512 * j
                            to, fn = view(at, 2, S), ACT.Copy
                        else:
                            at, wide, fn = {AQ: (A_QK, 512, ACT.Copy), AK: (A_QK + 1024, 512, ACT.Copy), AV: (A_V, 512, ACT.Copy),
                                            IB: (V_B, 512, ACT.Copy), GB_: (G_B, 512, ACT.Sigmoid),
                                            16: (GATE_A, D, ACT.Sigmoid), 20: (GATE_B, D, ACT.Sigmoid)}[first]
                            to = view(at, T, wide)[:, :, j * FC:(j + 1) * FC]
                        act.activation(to, ps, fn).then_inc(proj_evac, 1)
                        n += 1
                        if i == 3:
                            soft(1 + l)
                            act.wait_ge(proj_evac, len(PROJ) * l + 4)
                            act.activation(view(KK, 2 * HEADS * S), z2, ACT.Sigmoid, scale=-1.0).then_inc(kk_ready, 1)
                            if l:
                                soft(3)
                        if i >= 5 and i % 2 == 1 and (i - 5) // 2 < len(LEVELS):
                            level((i - 5) // 2)
                    act.wait_ge(rec_done, l + 1)
                    act.activation(tmp2[:, 0:T * 512], span(psD[:, 2:4, :]), ACT.Square).then_inc(rec_square, 1)
                    act.wait_ge(rec_sum, l + 1)
                    act.activation(stat[:, 24:32], stat[:, 16:24], ACT.Sqrt, bias=eps[:, 0:1], scale=1.0 / P).then_inc(rec_rms, 1)
                    st["turned"] += 1
                    piece(*rec_piece())
                    act.wait_ge(lam_in, l + 1)
                    act.activation(stat[:, 42:44], stat[:, 40:42], ACT.Exp).then_inc(lam_exp, 1)
                    act.wait_ge(qk_turned, l + 1)
                    act.activation(view(Z, 2048), span(psA[:, :, :]), ACT.Copy).then_inc(qkT_ready, 1)
                    prob = view(LOGF, 8, S)
                    for t in range(T):
                        k = T * l + t
                        act.wait_ge(max_ready, k + 1)
                        for e in range(8):
                            act.activation(prob[:, e, :], span(psD[:, :, :])[:, e * S:(e + 1) * S], ACT.Exp, bias=stat[:, 48 + e:49 + e],
                                           scale=0.125, accum_out=stat[:, 56 + e:57 + e]).then_inc(exp_ready, 1)
                        act.wait_ge(w_turned, k + 1)
                        act.activation(view(KK + 1024, 1024), span(psA[:, 0:2, :]), ACT.Copy).then_inc(wT_ready, 1)
                    act.wait_ge(att_done, T * (l + 1))
                    act.activation(tmp2[:, 0:T * 512], span(psA[:, 2:4, :]), ACT.Square).then_inc(att_square, 1)
                    act.wait_ge(att_sum, l + 1)
                    act.activation(stat[:, 24:32], stat[:, 16:24], ACT.Sqrt, bias=eps[:, 0:1], scale=1.0 / P).then_inc(att_rms, 1)
                    st["turned"] += 1
                    piece(*att_piece())
                    for i in range(4):
                        split_to(n)
                        n += 1
                    for t in range(T):
                        st["turned"] += 1
                        piece(*merge_piece(t))
                    for i in range(4):
                        split_to(n)
                        n += 1
                    st["updates"] += 1

        @block.vector
        def _(dve):
            st = {"split": 0, "norm": 0, "updates": 0, "piece": 0, "ffn": 0, "step": 0, "pair": 0}

            def step(ins):
                ins.then_inc(dve_step, 1)
                st["step"] += 1

            def settle():
                dve.wait_ge(dve_step, st["step"])

            def split(n_at, n):
                dve.wait_ge(hi_ready, n_at if n_at is not None else n + 1)
                dve.tensor_tensor(lo[:, n % RING, :], raw[:, n % RAW, :], hi[:, n % RING, :].bitcast(F32), ALU.subtract).then_inc(lo_ready, 1)

            def split_to(n):
                while st["split"] <= min(n + AHEAD, TOTAL - 1):
                    split(None, st["split"])
                    st["split"] += 1

            def piece(src, to):
                st["piece"] += 1
                dve.wait_ge(xTh_ready, st["piece"])
                dve.tensor_tensor(xTl[:, to[0], to[1]], src, xTh[:, to[0], to[1]].bitcast(F32), ALU.subtract).then_inc(xT_ready, 1)

            def inverse_root(n0, n1, mean, root, v, inv, t_):
                step(dve.reciprocal(stat[:, inv:inv + n1], stat[:, root:root + n1]))
                step(dve.tensor_scalar(stat[:, v:v + n1], stat[:, mean:mean + n1], 1.0 / n0, EPS, ALU.mult, ALU.add))
                settle()
                step(dve.tensor_tensor(stat[:, t_:t_ + n1], stat[:, inv:inv + n1], stat[:, inv:inv + n1], ALU.mult))
                settle()
                step(dve.tensor_tensor(stat[:, t_:t_ + n1], stat[:, t_:t_ + n1], stat[:, v:v + n1], ALU.mult))
                settle()
                step(dve.tensor_scalar(stat[:, t_:t_ + n1], stat[:, t_:t_ + n1], -0.5, 1.5, ALU.mult, ALU.add))
                settle()
                step(dve.tensor_tensor(stat[:, inv:inv + n1], stat[:, inv:inv + n1], stat[:, t_:t_ + n1], ALU.mult))
                settle()

            def norm_rows(to):
                st["norm"] += 1
                dve.wait_ge(rms_ready, st["norm"])
                inverse_root(D, 2, 0, 2, 4, 6, 8)
                dve.wait_ge(gain_loaded, 16 * st["norm"])
                for t in range(T):
                    dve.scalar_tensor_tensor(to[:, t, :], h[:, t, :], stat[:, 6 + t:7 + t], gain[:], ALU.mult, ALU.mult).then_inc(xn_ready, 1)

            def head_norm(src, sq, k_sq, sum_sem, rms_sem, nrm, scale, gate, to):
                dve.wait_ge(k_sq[0], k_sq[1])
                dve.tensor_reduce(stat[:, 16:24], sq.rearrange("p (e v) -> p e v", v=P), AX_X, ALU.add).then_inc(sum_sem, 1)
                dve.wait_ge(rms_sem, k_sq[1])
                inverse_root(P, 8, 16, 24, 32, 8, 16 if False else 0)
                view3 = lambda v: v.rearrange("p (e v) -> p e v", v=P)
                step(dve.tensor_tensor(view3(to), view3(src), stat[:, 8:16].unsqueeze(2).broadcast_to([P, 8, P]), ALU.mult))
                settle()
                rows_ = lambda v: v.rearrange("p (t f) -> p t f", t=T)
                wide = scr[:, nrm:nrm + 512].unsqueeze(1).broadcast_to([P, T, 512])
                return rows_, wide

            dve.memset(eps[:, 0:1], EPS).then_inc(eps_ready, 1)
            dve.memset(eps[:, 1:2], 1.0).then_inc(eps_ready, 1)
            step(dve.memset(one_row[:], 1.0))
            dve.wait_ge(consts_loaded, 16 * CONSTS)
            dve.scalar_tensor_tensor(cpos[:, 0, :], lru_c[:, 3, :], -1.0, lru_c[:, 3, :], ALU.mult, ALU.max).then_inc(cpos_exp, 1)
            step(dve.tensor_copy(stat[:, 10:12], pos_i[:]))
            settle()
            for t in range(T):
                step(dve.tensor_scalar(rope[:, 2, t, :], rope_in[:, 0:ROT], stat[:, 10 + t:11 + t], None, ALU.mult))
            settle()
            for shift, to in ((0.0, 4), (0.25, 5)):
                step(dve.tensor_scalar(rope[:, 3, :, :], rope[:, 2, :, :], 1.0 / TWO_PI, shift, ALU.mult, ALU.add))
                settle()
                step(dve.tensor_scalar(rope[:, 3, :, :], rope[:, 3, :, :], ROUND, None, ALU.add))
                settle()
                step(dve.tensor_scalar(rope[:, 3, :, :], rope[:, 3, :, :], ROUND, None, ALU.subtract))
                settle()
                step(dve.scalar_tensor_tensor(rope[:, to, :, :], rope[:, 3, :, :], -PI_HI, rope[:, 2, :, :], ALU.mult, ALU.add))
                settle()
                step(dve.scalar_tensor_tensor(rope[:, to, :, :], rope[:, 3, :, :], -PI_MID, rope[:, to, :, :], ALU.mult, ALU.add))
                settle()
                step(dve.scalar_tensor_tensor(rope[:, to, :, :], rope[:, 3, :, :], -PI_LO, rope[:, to, :, :], ALU.mult, ALU.add))
                settle()
                if to == 5:
                    step(dve.tensor_scalar(rope[:, to, :, :], rope[:, to, :, :], TWO_PI / 4, None, ALU.add))
                    settle()
                last = dve.tensor_scalar(rope[:, to, :, :], rope[:, to, :, :], 3.1415925, -3.1415925, ALU.min, ALU.max)
                if to == 4:
                    step(last)
                    settle()
                else:
                    last.then_inc(angles_ready, 1)
            dve.wait_ge(cpos_exp, 2)
            step(dve.tensor_scalar(cpos[:, 2, :], cpos[:, 1, :], 2.0, None, ALU.add))
            settle()
            step(dve.reciprocal(cpos[:, 3, :], cpos[:, 2, :]))
            settle()
            step(dve.tensor_tensor(cpos[:, 1, :], cpos[:, 1, :], cpos[:, 3, :], ALU.mult))
            settle()
            step(dve.tensor_tensor(cpos[:, 2, :], cpos[:, 1, :], cpos[:, 1, :], ALU.mult))
            settle()
            step(dve.tensor_scalar(cpos[:, 3, :], cpos[:, 2, :], 1.0 / 17, None, ALU.mult))
            settle()
            for odd in (15, 13, 11, 9, 7, 5, 3):
                step(dve.scalar_tensor_tensor(cpos[:, 3, :], cpos[:, 3, :], 1.0 / odd, cpos[:, 2, :], ALU.add, ALU.mult))
                settle()
            step(dve.scalar_tensor_tensor(cpos[:, 3, :], cpos[:, 3, :], 1.0, cpos[:, 1, :], ALU.add, ALU.mult))
            step(dve.tensor_scalar(cpos[:, 0, :], lru_c[:, 3, :], -1.0, 0.0, ALU.mult, ALU.max))
            settle()
            step(dve.scalar_tensor_tensor(cpos[:, 2, :], cpos[:, 3, :], 2.0, cpos[:, 0, :], ALU.mult, ALU.add))
            settle()
            dve.tensor_scalar(cpos[:, 4, :], cpos[:, 2, :], 8.0, None, ALU.mult).then_inc(cpos_ready, 1)
            dve.tensor_scalar(cpos[:, 5, :], cpos[:, 2, :], -8.0, None, ALU.mult).then_inc(cpos_ready, 1)
            step(dve.tensor_tensor(lbt[:, 2], lbt[:, 1], lbt[:, 0], ALU.subtract))
            settle()
            dve.scalar_tensor_tensor(lbt[:, 3], lbt[:, 2], -1.0, lbt[:, 2], ALU.mult, ALU.max).then_inc(lb_in, 1)
            dve.wait_ge(lb_out, 3)
            step(dve.scalar_tensor_tensor(lbt[:, 7], lbt[:, 2], 0.0, lbt[:, 5], ALU.min, ALU.subtract))
            step(dve.tensor_scalar(lbt[:, 8], lbt[:, 2], -1.0, 0.0, ALU.mult, ALU.min))
            settle()
            step(dve.tensor_tensor(lbt[:, 9], lbt[:, 8], lbt[:, 5], ALU.subtract))
            dve.wait_ge(x_loaded, 16)
            for t in range(T):
                dve.memset(stat[:, 12 + t:13 + t], 0.0).then_inc(h_ready, 1)
            settle()

            n = 0
            for stage in plan:
                kind = stage[0]
                if kind == "norm":
                    split_to(n - 1)
                    norm_rows(xn)
                    for t in range(T):
                        piece(*norm_piece(t))
                if kind == "rescale":
                    split_to(n - 1)
                    norm_rows(h)
                    dve.wait_ge(xn_ready, 2 * st["norm"])
                    for t in range(T):
                        dve.memset(stat[:, 12 + t:13 + t], 0.0).then_inc(h_ready, 1)
                    st["updates"] += 1
                if kind == "pool":
                    split_to(n - 1)
                    norm_rows(xn)
                    for t in range(T):
                        piece(*pool_piece(t))
                    split_to(n)
                    n += 1
                    dve.wait_ge(block_used, n)
                    dve.wait_ge(pool_loaded, 48)
                    for t in range(T):
                        y = xn[:, t, :]
                        step(dve.tensor_tensor(y, span(psD[:, 2 * t:2 * t + 2, :]), view(POOL_B, D), ALU.add))
                        settle()
                        step(dve.tensor_tensor(y, y, view(POOL_S, D), ALU.mult))
                        settle()
                        dve.tensor_tensor(h[:, t, :], h[:, t, :], y, ALU.add).then_inc(h_ready, 1)
                    st["updates"] += 1
                if kind == "ffn":
                    def gated(c_at, c):
                        dve.wait_ge(silu_ready, c_at)
                        dve.tensor_tensor(prod[:, c % 2, :], sil[:, c % 2, :], psA[:, 2 + c % 2, :], ALU.mult).then_inc(prod_ready, 1)
                        dve.wait_ge(prod_hi_ready, c_at)
                        dve.tensor_tensor(span(prod_lo[:, c % 2]), prod[:, c % 2, :], span(prod_hi[:, c % 2]).bitcast(F32), ALU.subtract).then_inc(prod_lo_ready, 1)

                    c0 = st["ffn"] * CH
                    for b in range(5):
                        split_to(n)
                        if b in (1, 3):
                            gated(c0 + b // 2 + 1, b // 2)
                        n += 1
                    with dve.Fori(0, (CH - 3) // 2) as j:
                        for b in range(6):
                            split(6 * j + (n + b + AHEAD + 1), n + b + AHEAD)
                            if b % 3 == 1:
                                gated(2 * j + (c0 + 3 + b // 3), b // 3)
                    n += 3 * (CH - 3)
                    st["split"] += 3 * (CH - 3)
                    for b in range(4):
                        split_to(n)
                        if b == 1:
                            gated(c0 + CH, CH - 1)
                        n += 1
                    dve.wait_ge(block_used, n)
                    for t in range(T):
                        dve.scalar_tensor_tensor(h[:, t, :], span(psD[:, 2 * t:2 * t + 2, :]), stage[4], h[:, t, :],
                                                 ALU.mult, ALU.add).then_inc(h_ready, 1)
                    st["ffn"] += 1
                    st["updates"] += 1
                if kind == "lru":
                    half = R // FC
                    xb, xc = view(L_XB, RT, S + 3), view(L_XC, RT, S)
                    r, ig, th = view(L_R, RT, S), view(L_IG, RT, S), view(L_T, GT, S)
                    gelu, ratio = view(L_GELU, RT, S), view(L_XB, RT, S)

                    step(dve.memset(xb[:, :, 0:3], 0.0))
                    settle()

                    def convolve(i):
                        dve.wait_ge(xb_ready, i + 1)
                        fts = (2 * i, 2 * i + 1)
                        for ft in fts:
                            step(dve.tensor_scalar(xc[:, ft, :], xb[:, ft, 0:S], conv_w[:, 0, ft:ft + 1], lru_c[:, 0, ft:ft + 1], ALU.mult, ALU.add))
                        for k in range(1, 4):
                            settle()
                            for ft in fts:
                                ins = dve.scalar_tensor_tensor(xc[:, ft, :], xb[:, ft, k:k + S], conv_w[:, k, ft:ft + 1], xc[:, ft, :], ALU.mult, ALU.add)
                                if k < 3:
                                    step(ins)
                                else:
                                    ins.then_inc(xc_ready, 1)

                    def ratios(g):
                        v, t_ = ratio[:, g * GT:(g + 1) * GT, :], th[:, :, :]
                        dve.wait_ge(tanh_ready, GT * (g + 1))
                        step(dve.tensor_scalar(v, t_, 1.0, None, ALU.add))
                        settle()
                        step(dve.reciprocal(v, v))
                        settle()
                        dve.tensor_tensor(v, v, t_, ALU.mult).then_inc(ratio_ready, 1)
                        gs = slice(g * GT, (g + 1) * GT)
                        dve.wait_ge(gates_ready, 2 * GT * (g + 1))
                        step(dve.tensor_tensor(ig[:, gs, :], ig[:, gs, :], xc[:, gs, :], ALU.mult))

                    def recur(g):
                        gs = slice(g * GT, (g + 1) * GT)
                        dve.wait_ge(mult_ready, g + 1)
                        settle()
                        step(dve.tensor_tensor(ig[:, gs, :], ig[:, gs, :], ratio[:, gs, :], ALU.mult))
                        settle()
                        dve.wait_ge(decay_ready, GT * (g + 1))
                        for ft in range(g * GT, (g + 1) * GT):
                            step(dve.tensor_tensor_scan(ig[:, ft, :], r[:, ft, :], ig[:, ft, :], 0.0, ALU.mult, ALU.add))
                        settle()

                    for i in range(2 * half):
                        split_to(n)
                        if i < half:
                            convolve(i)
                        if i in (half, half + 1):
                            ratios(i - half)
                        if i in (half + 2, half + 3):
                            recur(i - half - 2)
                        n += 1
                    dve.wait_ge(gelu_ready, half)
                    for g in range(2):
                        gs = slice(g * GT, (g + 1) * GT)
                        dve.tensor_tensor(xc[:, gs, :], ig[:, gs, :], gelu[:, gs, :], ALU.mult).then_inc(y_ready, 1)
                    for g in range(2):
                        gs = slice(g * GT, (g + 1) * GT)
                        piece(xc[:, gs, :], (gs, slice(0, S)))
                    for i in range(R // (2 * P)):
                        split_to(n)
                        n += 1
                    dve.wait_ge(block_used, n)
                    for t in range(T):
                        dve.tensor_tensor(h[:, t, :], span(psD[:, 2 * t:2 * t + 2, :]), h[:, t, :], ALU.add).then_inc(h_ready, 1)
                    st["updates"] += 1
                if kind == "ple":
                    piece(*ple_piece())
                    for i in range(KT // 2 + 1):
                        split_to(n)
                        n += 1
                    sig = view(SIG, T, D)
                    for t in range(T):
                        dve.wait_ge(sig_ready, 2 * stage[1] + t + 1)
                        dve.wait_ge(block_used, n)
                        step(dve.tensor_tensor(sig[:, t, :], sig[:, t, :], span(psA[:, 2 * t:2 * t + 2, :]), ALU.mult))
                    settle()
                    for t in range(T):
                        dve.tensor_tensor(h[:, t, :], h[:, t, :], sig[:, t, :], ALU.add).then_inc(h_ready, 1)
                    st["updates"] += 1
                if kind == "mix":
                    l = stage[1]
                    HS = HEADS * S
                    z2, tmp2, e2, kk2 = (view(at, 2 * HS) for at in (Z, TMP, LOGF, KK))
                    bf, bb = view(Z, HS), view(Z + HS, HS)
                    near, cross = view(XN, 8, P), view(XN + 1024, 8, P)

                    def log_forget():
                        dve.wait_ge(proj_evac, len(PROJ) * l + 4)
                        dve.scalar_tensor_tensor(tmp2, z2, -1.0, z2, ALU.mult, ALU.max).then_inc(absz_ready, 1)
                        dve.wait_ge(soft_ready, 1 + l)
                        step(dve.scalar_tensor_tensor(e2, z2, 0.0, tmp2, ALU.min, ALU.subtract))
                        settle()
                        if l:
                            e4, t4 = e2.rearrange("p (c s) -> p c s", s=S), tmp2.rearrange("p (c s) -> p c s", s=S)
                            for c in range(2 * HEADS):
                                d_, hh = c // HEADS, c % HEADS
                                step(dve.tensor_scalar(e4[:, c, :], e4[:, c, :], lbt[:, 9, d_, hh:hh + 1], None, ALU.add))
                            settle()
                            for c in range(2 * HEADS):
                                d_, hh = c // HEADS, c % HEADS
                                step(dve.tensor_scalar(t4[:, c, :], e4[:, c, :], lbt[:, 7, d_, hh:hh + 1], None, ALU.subtract))
                            settle()
                            for c in range(2 * HEADS):
                                d_, hh = c // HEADS, c % HEADS
                                step(dve.tensor_scalar(e4[:, c, :], e4[:, c, :], lbt[:, 7, d_, hh:hh + 1], None, ALU.max))
                            settle()
                            dve.scalar_tensor_tensor(tmp2, tmp2, -1.0, tmp2, ALU.mult, ALU.max).then_inc(absz_ready, 1)
                            dve.wait_ge(soft_ready, 3)
                            step(dve.tensor_tensor(e2, e2, tmp2, ALU.add))
                            settle()
                        dve.wait_ge(kk_ready, l + 1)
                        if l:
                            k4 = kk2.rearrange("p (c s) -> p c s", s=S)
                            for c in range(2 * HEADS):
                                d_, hh = c // HEADS, c % HEADS
                                step(dve.tensor_scalar(k4[:, c, :], k4[:, c, :], lbt[:, 6, d_, hh:hh + 1], None, ALU.mult))
                        for c in range(2 * HEADS):
                            f, b = slice(c * P, (c + 1) * P), slice(HS + c * P, HS + (c + 1) * P)
                            step(dve.tensor_tensor_scan(z2[:, f], one_row[:], e2[:, f], 0.0, ALU.mult, ALU.add))
                            step(dve.tensor_tensor_scan(z2[:, b][:, ::-1], one_row[:], e2[:, b][:, ::-1], 0.0, ALU.mult, ALU.add))
                        settle()

                    def diagonal():
                        step(dve.tensor_tensor(tmp2[:, HS:2 * HS], kk2[:, 0:HS], kk2[:, HS:2 * HS], ALU.add))
                        settle()
                        dve.tensor_copy(tmp2[:, 0:HS], view(Q_B, HS)).then_inc(scaled_ready, 1)

                    def exponents(i):
                        m = LEVELS[i]
                        eq, ek, f, b = (halves(v, m) for v in (e2[:, 0:HS], e2[:, HS:2 * HS], bf, bb))
                        nb = HS // (2 * m)
                        f_end = f[:, :, 0, m - 1:m].broadcast_to([P, nb, m])
                        b_end = b[:, :, 1, 0:1].broadcast_to([P, nb, m])
                        if m == P:
                            step(dve.tensor_copy(eq[:, :, 1, :], f[:, :, 1, :]))
                            step(dve.tensor_copy(eq[:, :, 0, :], b[:, :, 0, :]))
                        else:
                            step(dve.tensor_tensor(eq[:, :, 1, :], f[:, :, 1, :], f_end, ALU.subtract))
                            step(dve.tensor_tensor(eq[:, :, 0, :], b[:, :, 0, :], b_end, ALU.subtract))
                        step(dve.tensor_tensor(ek[:, :, 0, :], f_end, f[:, :, 0, :], ALU.subtract))
                        step(dve.tensor_tensor(ek[:, :, 1, :], b_end, b[:, :, 1, :], ALU.subtract))
                        settle()
                        dve.memset(stat[:, 14:15], 0.0).then_inc(decay_in, 1)

                    def scaled(i):
                        m = LEVELS[i]
                        dve.wait_ge(decay_out, len(LEVELS) * l + i + 1)
                        dve.wait_ge(pair_done, (len(LEVELS) + 1) * l + i + 1)
                        step(dve.tensor_tensor(tmp2[:, 0:HS], view(Q_B, HS), e2[:, 0:HS], ALU.mult))
                        ek, kf, kb, to = (halves(v, m) for v in (e2[:, HS:2 * HS], kk2[:, 0:HS], kk2[:, HS:2 * HS], tmp2[:, HS:2 * HS]))
                        step(dve.tensor_tensor(to[:, :, 0, :], kf[:, :, 0, :], ek[:, :, 0, :], ALU.mult))
                        step(dve.tensor_tensor(to[:, :, 1, :], kb[:, :, 1, :], ek[:, :, 1, :], ALU.mult))
                        settle()
                        dve.memset(stat[:, 15:16], 0.0).then_inc(scaled_ready, 1)

                    def take(i):
                        bank = (i + 1) % 2
                        ps = span(psD[:, 2 * bank:2 * bank + 2, :]).rearrange("p (e s) -> p e s", s=P)
                        dve.wait_ge(pair_done, (len(LEVELS) + 1) * l + i + 2)
                        if i < 0:
                            ins = dve.tensor_copy(near, ps)
                        elif LEVELS[i] == P:
                            ins = dve.tensor_copy(cross, ps)
                        else:
                            dve.wait_ge(pair_taken, (len(LEVELS) + 1) * l + i + 1)
                            ins = dve.copy_predicated(near, level_mask[:, i, :].unsqueeze(1).broadcast_to([P, 8, P]), ps)
                        ins.then_inc(pair_taken, 1)

                    for i, (c, first) in enumerate(PROJ):
                        split_to(n)
                        n += 1
                        if i == 3:
                            log_forget()
                        if i == 5:
                            dve.wait_ge(proj_evac, len(PROJ) * l + 6)
                            diagonal()
                        if i >= 5 and i % 2 == 1 and (i - 5) // 2 < len(LEVELS):
                            exponents((i - 5) // 2)
                        if i >= 6 and i % 2 == 0 and (i - 6) // 2 < len(LEVELS):
                            take((i - 6) // 2 - 1)
                            scaled((i - 6) // 2)
                    take(len(LEVELS) - 1)
                    rec, o = view(LOGF, T * 512), span(psD[:, 2:4, :])
                    rows_, wide = head_norm(o, tmp2[:, 0:T * 512], (rec_square, l + 1), rec_sum, rec_rms, NRM_HG, 1.0, None, rec)
                    dve.wait_ge(mix_loaded, 48 * (l + 1))
                    step(dve.tensor_tensor(rows_(rec), rows_(rec), wide, ALU.mult))
                    settle()
                    dve.wait_ge(proj_evac, len(PROJ) * l + 16)
                    dve.tensor_tensor(rec, rec, view(G_B, T * 512), ALU.mult).then_inc(rec_ready, 1)
                    piece(*rec_piece())
                    lam = view(LAM, 4, 64)
                    for e in range(2):
                        step(dve.tensor_tensor(lam[:, 2 * e, :], lam[:, 2 * e, :], lam[:, 2 * e + 1, :], ALU.mult))
                    settle()
                    for e in range(2):
                        step(dve.tensor_reduce(stat[:, 40 + e:41 + e], lam[:, 2 * e, :], AX_X, ALU.add))
                    settle()
                    dve.memset(stat[:, 14:15], 0.0).then_inc(lam_in, 1)
                    dve.wait_ge(rope_ready, 2)
                    dve.wait_ge(proj_evac, len(PROJ) * l + 14)
                    qk = view(A_QK, 2, T, 512)
                    t1s, t2s = view(KK, T, 2, 8, ROT), view(KK + 256, T, 2, 8, ROT)
                    for t in range(T):
                        x1 = qk[:, :, t, :].rearrange("p e (g d) -> p e g d", d=64)[:, :, :, 0:ROT]
                        x2 = qk[:, :, t, :].rearrange("p e (g d) -> p e g d", d=64)[:, :, :, ROT:2 * ROT]
                        sin, cos = (rope[:, e, t, :].unsqueeze(1).unsqueeze(1).broadcast_to([P, 2, 8, ROT]) for e in (0, 1))
                        u, v, w, y = (view(KK + 128 * (4 * t + e), 2, 8, ROT) for e in range(4))
                        step(dve.tensor_tensor(u, x1, cos, ALU.mult))
                        step(dve.tensor_tensor(v, x2, sin, ALU.mult))
                        step(dve.tensor_tensor(w, x2, cos, ALU.mult))
                        step(dve.tensor_tensor(y, x1, sin, ALU.mult))
                        settle()
                        dve.tensor_tensor(x1, u, v, ALU.subtract).then_inc(roped, 1)
                        dve.tensor_tensor(x2, w, y, ALU.add).then_inc(roped, 1)
                    dve.wait_ge(lam_exp, l + 1)
                    step(dve.scalar_tensor_tensor(stat[:, 44:45], stat[:, 42:43], LAM_INIT[l], stat[:, 43:44], ALU.add, ALU.subtract))
                    settle()
                    step(dve.tensor_scalar(stat[:, 45:46], stat[:, 44:45], -1.0, None, ALU.mult))
                    settle()
                    prob, w4 = view(LOGF, 8, S), view(TMP, HEADS, S)
                    for t in range(T):
                        k = T * l + t
                        dve.wait_ge(scores_done, k + 1)
                        if t:
                            dve.wait_ge(exp_ready, 8 * k)
                        step(dve.tensor_reduce(stat[:, 32:40], span(psD[:, :, :]).rearrange("p (e s) -> p e s", s=S), AX_X, ALU.max))
                        settle()
                        dve.tensor_scalar(stat[:, 48:56], stat[:, 32:40], -0.125, None, ALU.mult).then_inc(max_ready, 1)
                        dve.wait_ge(exp_ready, 8 * (k + 1))
                        step(dve.reciprocal(stat[:, 16:24], stat[:, 56:64]))
                        settle()
                        step(dve.tensor_scalar(stat[:, 24:28], stat[:, 20:24], stat[:, 45:46], None, ALU.mult))
                        settle()
                        if t:
                            dve.wait_ge(w_turned, k)
                        for hh in range(HEADS):
                            step(dve.tensor_scalar(w4[:, hh, :], prob[:, hh, :], stat[:, 16 + hh:17 + hh], None, ALU.mult))
                        settle()
                        for hh in range(HEADS):
                            dve.scalar_tensor_tensor(w4[:, hh, :], prob[:, 4 + hh, :], stat[:, 24 + hh:25 + hh], w4[:, hh, :],
                                                     ALU.mult, ALU.add).then_inc(w_ready, 1)
                    att, o = view(LOGF, T * 512), span(psA[:, 2:4, :])
                    rows_, wide = head_norm(o, tmp2[:, 0:T * 512], (att_square, l + 1), att_sum, att_rms, NRM_DA, 1.0, None, att)
                    dve.scalar_tensor_tensor(rows_(att), rows_(att), 1.0 - LAM_INIT[l], wide, ALU.mult, ALU.mult).then_inc(att_ready, 1)
                    piece(*att_piece())
                    for i in range(4):
                        split_to(n)
                        n += 1
                    mrg, ga, gb = xn, view(GATE_A, T, D), view(GATE_B, T, D)
                    dve.wait_ge(proj_evac, len(PROJ) * (l + 1))
                    dve.wait_ge(block_used, n)
                    for t in range(T):
                        step(dve.tensor_tensor(mrg[:, t, :], ga[:, t, :], span(psD[:, 2 * t:2 * t + 2, :]), ALU.mult))
                        step(dve.tensor_tensor(gb[:, t, :], gb[:, t, :], span(psA[:, 2 * t:2 * t + 2, :]), ALU.mult))
                    settle()
                    for t in range(T):
                        dve.tensor_tensor(mrg[:, t, :], mrg[:, t, :], gb[:, t, :], ALU.add).then_inc(merged, 1)
                    for t in range(T):
                        piece(*merge_piece(t))
                    for i in range(4):
                        split_to(n)
                        n += 1
                    dve.wait_ge(block_used, n)
                    for t in range(T):
                        dve.tensor_tensor(h[:, t, :], span(psA[:, 2 * t:2 * t + 2, :]), h[:, t, :], ALU.add).then_inc(h_ready, 1)
                    st["updates"] += 1

        @block.tensor
        def _(pe):
            st = {"norm": 0, "piece": 0, "ffn": 0}

            def features(n_at, n, to, ready=None):
                pe.wait_ge(lo_ready, n_at)
                w_hi = hi[:, n % RING, :].rearrange("p (k f) -> p k f", f=FC)
                w_lo = lo[:, n % RING, :].rearrange("p (k f) -> p k f", f=FC)
                for f in range(2):
                    fs = slice(f * P, (f + 1) * P)
                    for k in range(KT):
                        for e, (w, x) in enumerate(((w_hi, xTh), (w_hi, xTl), (w_lo, xTh))):
                            last = pe.matmul(to[:, f * S:(f + 1) * S], w[:, k, fs], x[:, k, :], start=(k == 0 and e == 0),
                                             stop=(k == KT - 1 and e == 2))
                last.then_inc(block_used, 1)

            def tokens(n_at, n, to):
                pe.wait_ge(lo_ready, n_at)
                w_hi = hi[:, n % RING, :].rearrange("p (k f) -> p k f", f=FC)
                w_lo = lo[:, n % RING, :].rearrange("p (k f) -> p k f", f=FC)
                for t in range(T):
                    ts = slice(t * P, (t + 1) * P)
                    for k in range(KT):
                        for e, (x, w) in enumerate(((xTh, w_hi), (xTh, w_lo), (xTl, w_hi))):
                            last = pe.matmul(to[:, t * FC:(t + 1) * FC], x[:, k, ts], w[:, k, :], start=(k == 0 and e == 0),
                                             stop=(k == KT - 1 and e == 2))
                last.then_inc(block_used, 1)

            def contract(n_at, n, x_hi, x_lo, to, first, final):
                pe.wait_ge(lo_ready, n_at)
                w_hi = hi[:, n % RING, :].rearrange("p (k f) -> p k f", f=D)
                w_lo = lo[:, n % RING, :].rearrange("p (k f) -> p k f", f=D)
                for k in range(2):
                    for t in range(T):
                        ts = slice(t * P, (t + 1) * P)
                        for e, (x, w) in enumerate(((x_hi, w_hi), (x_hi, w_lo), (x_lo, w_hi))):
                            for c in range(2):
                                last = pe.matmul(to[:, 2 * t + c, :], x[:, k, ts], w[:, k, c * 512:(c + 1) * 512],
                                                 start=(first and k == 0 and e == 0), stop=(final and k == 1 and e == 2))
                last.then_inc(block_used, 1)

            def xT_pieces(k):
                st["piece"] += k
                pe.wait_ge(xT_ready, st["piece"])

            def turn(to, src, cols):
                pass

            pe.wait_ge(consts_loaded, 16 * CONSTS)
            n = 0
            for stage in plan:
                kind = stage[0]
                if kind == "norm":
                    for t in range(T):
                        pe.wait_ge(xn_ready, 2 * st["norm"] + t + 1)
                        for k in range(KT):
                            last = pe.transpose(psA[:, 2 * t + k // 4, (k % 4) * P:(k % 4 + 1) * P],
                                                xn[:, t, k * P:(k + 1) * P], ident[:])
                        last.then_inc(turned, 1)
                    st["norm"] += 1
                    xT_pieces(T)
                if kind == "rescale":
                    st["norm"] += 1
                if kind == "pool":
                    mean = view(POOL_M, T, 4, S)
                    pe.wait_ge(pool_loaded, 48)
                    pe.wait_ge(xn_ready, 2 * st["norm"] + 2)
                    for k in range(KT):
                        to = psA[:, k // 2, (k % 2) * S:(k % 2 + 1) * S]
                        pe.matmul(to, xn[:, 0, k * P:(k + 1) * P], mean[:, 0, k // 2, :], start=True, stop=False)
                        last = pe.matmul(to[:, P:S], xn[:, 1, k * P:(k + 1) * P], mean[:, 1, k // 2, P:S], start=False, stop=True)
                        if k % 4 == 3:
                            last.then_inc(turned, 1)
                    st["norm"] += 1
                    xT_pieces(T)
                    pe.wait_ge(lo_ready, n + 1)
                    w_hi, w_lo = (v[:, n % RING, :].rearrange("p (k f) -> p k f", f=FC) for v in (hi, lo))
                    for t in range(T):
                        for g in range(4):
                            to = psD[:, 2 * t + g // 2, (g % 2) * FC:(g % 2 + 1) * FC]
                            for k in range(2):
                                for e, (x, w) in enumerate(((xTh, w_hi), (xTh, w_lo), (xTl, w_hi))):
                                    last = pe.matmul(to, x[:, 2 * g + k, t * P:(t + 1) * P], w[:, 2 * g + k, :],
                                                     start=(k == 0 and e == 0), stop=(k == 1 and e == 2))
                    last.then_inc(block_used, 1)
                    n += 1
                if kind == "ffn":
                    c0 = st["ffn"] * CH

                    def down(n_at, n, c_at, c, first=False, final=False):
                        pe.wait_ge(prod_lo_ready, c_at)
                        contract(n_at, n, prod_hi[:, c % 2], prod_lo[:, c % 2], psD, first, final)

                    features(n + 1, n, psA[:, 0, :])
                    features(n + 2, n + 1, psA[:, 2, :])
                    features(n + 3, n + 2, psA[:, 1, :])
                    features(n + 4, n + 3, psA[:, 3, :])
                    down(n + 5, n + 4, c0 + 1, 0, first=True)
                    n += 5
                    with pe.Fori(0, (CH - 3) // 2) as j:
                        for e in range(2):
                            pe.wait_ge(prod_ready, 2 * j + (c0 + e + 1))
                            features(6 * j + (n + 3 * e + 1), n + 3 * e, psA[:, e, :])
                            features(6 * j + (n + 3 * e + 2), n + 3 * e + 1, psA[:, 2 + e, :])
                            down(6 * j + (n + 3 * e + 3), n + 3 * e + 2, 2 * j + (c0 + e + 2), 1 + e)
                    n += 3 * (CH - 3)
                    pe.wait_ge(prod_ready, c0 + CH - 2)
                    features(n + 1, n, psA[:, 0, :])
                    features(n + 2, n + 1, psA[:, 2, :])
                    down(n + 3, n + 2, c0 + CH - 1, CH - 2)
                    down(n + 4, n + 3, c0 + CH, CH - 1, final=True)
                    n += 4
                    st["ffn"] += 1
                if kind == "lru":
                    half = R // FC
                    band, xc = view(BAND, 2, 2, GT, 384), view(L_XC, RT, S)

                    def recurrent_gates(g):
                        pe.wait_ge(xc_ready, GT * (g + 1))
                        for m in range(GT):
                            ft = g * GT + m
                            if ft >= 4:
                                pe.wait_ge(gates_ready, 2 * (ft - 3))
                            for e in range(2):
                                ks = [k for k in (m - 1, m, m + 1) if 0 <= k < GT]
                                for k in ks:
                                    last = pe.matmul(psD[:, ft % 4, e * S:(e + 1) * S], band[:, e, g, k, (m - k + 1) * P:(m - k + 2) * P],
                                                     xc[:, g * GT + k, :], start=(k == ks[0]), stop=(k == ks[-1]))
                            last.then_inc(gates_done, 1)

                    for i in range(2 * half):
                        if 4 <= i < 4 + half:
                            pe.wait_ge(xb_ready, i - 3)
                        elif i >= 4 + half:
                            pe.wait_ge(gelu_ready, i - 3 - half)
                        features(n + 1, n, psA[:, i % 4, :])
                        n += 1
                        if i == half:
                            pe.wait_ge(band_loaded, 16 * 2 * 2 * len(head_pieces()))
                            recurrent_gates(0)
                        if i == half + 1:
                            recurrent_gates(1)
                    xT_pieces(2)
                    nk = R // (2 * P)
                    for i in range(nk):
                        contract(n + 1, n, xTh[:, 2 * i:2 * i + 2], xTl[:, 2 * i:2 * i + 2], psD, i == 0, i == nk - 1)
                        n += 1
                if kind == "ple":
                    pe.wait_ge(p_loaded, 16 * (stage[1] + 1))
                    rows_p = view(PTOK, T, S)
                    for t in range(T):
                        for k in range(2):
                            last = pe.transpose(psD[:, 0, k * S + t * P:k * S + (t + 1) * P], rows_p[:, t, k * P:(k + 1) * P], ident[:])
                    last.then_inc(turned, 1)
                    xT_pieces(1)
                    for i in range(KT // 2):
                        contract(n + 1, n, xTh[:, 2 * i:2 * i + 2], xTl[:, 2 * i:2 * i + 2], psD, i == 0, i == KT // 2 - 1)
                        n += 1
                    contract(n + 1, n, xTh[:, 8:10], xTl[:, 8:10], psA, True, True)
                    n += 1
                if kind == "mix":
                    l = stage[1]
                    HS = HEADS * S
                    tmp2 = view(TMP, 2, HEADS, S)
                    near, cross = view(XN, 8, P), view(XN + 1024, 8, P)

                    def pair(i):
                        k0 = (len(LEVELS) + 1) * l
                        pe.wait_ge(scaled_ready, k0 + i + 2)
                        if i >= 1:
                            pe.wait_ge(pair_taken, k0 + i)
                        bank = (i + 1) % 2
                        ps = span(psD[:, 2 * bank:2 * bank + 2, :]).rearrange("p (e s) -> p e s", s=P)
                        for hh in range(HEADS):
                            for e in range(T):
                                te = 1 - e if i >= 0 and LEVELS[i] == P else e
                                last = pe.matmul(ps[:, 2 * hh + e, :], tmp2[:, 1, hh, e * P:(e + 1) * P], tmp2[:, 0, hh, te * P:(te + 1) * P],
                                                 start=True, stop=True)
                        last.then_inc(pair_done, 1)

                    for i, (c, first) in enumerate(PROJ):
                        if i >= 4:
                            pe.wait_ge(proj_evac, len(PROJ) * l + i - 3)
                        (features if first in (FF, FB, QB) else tokens)(n + 1, n, psA[:, i % 4, :])
                        n += 1
                        if i == 6:
                            pair(-1)
                        if i >= 7 and i % 2 == 1 and (i - 7) // 2 < len(LEVELS):
                            pair((i - 7) // 2)
                    pe.wait_ge(pair_taken, (len(LEVELS) + 1) * (l + 1))
                    v_b = view(V_B, T, 512)
                    for t in range(T):
                        for hh in range(HEADS):
                            to = psD[:, 2 + t, hh * P:(hh + 1) * P]
                            pe.matmul(to, near[:, 2 * hh + t, :], v_b[:, t, hh * P:(hh + 1) * P], start=True, stop=False)
                            last = pe.matmul(to, cross[:, 2 * hh + 1 - t, :], v_b[:, 1 - t, hh * P:(hh + 1) * P], start=False, stop=True)
                    last.then_inc(rec_done, 1)
                    pe.wait_ge(rec_ready, l + 1)
                    rec = view(LOGF, T, 512)
                    for t in range(T):
                        for k in range(HEADS):
                            last = pe.transpose(psD[:, k // 2, (k % 2) * S + t * P:(k % 2) * S + (t + 1) * P], rec[:, t, k * P:(k + 1) * P], ident[:])
                    last.then_inc(turned, 1)
                    pe.wait_ge(roped, 4 * (l + 1))
                    pe.wait_ge(proj_evac, len(PROJ) * (l + 1))
                    qk, qkT = view(A_QK, 2, T, 512), view(Z, 2, HEADS, S)
                    for e in range(2):
                        for t in range(T):
                            for hh in range(HEADS):
                                c = HEADS * e + hh
                                last = pe.transpose(psA[:, c // 2, (c % 2) * S + t * P:(c % 2) * S + (t + 1) * P],
                                                    qk[:, e, t, hh * P:(hh + 1) * P], ident[:])
                    last.then_inc(qk_turned, 1)
                    pe.wait_ge(qkT_ready, l + 1)
                    xT_pieces(1)
                    w4, wT, v_a = view(TMP, HEADS, S), view(KK + 1024, HEADS, T, P), view(A_V, T, 512)
                    for t in range(T):
                        k = T * l + t
                        if t:
                            pe.wait_ge(exp_ready, 8 * k)
                        for e in range(2):
                            for hh in range(HEADS):
                                at = (e * HEADS + hh) * S
                                last = pe.matmul(span(psD[:, :, :])[:, at:at + S], qkT[64 * e:64 * e + 64, 0, hh, t * P:(t + 1) * P],
                                                 qkT[64 * e:64 * e + 64, 1, hh, :], start=True, stop=True)
                        last.then_inc(scores_done, 1)
                        pe.wait_ge(w_ready, HEADS * (k + 1))
                        if t:
                            pe.wait_ge(wT_ready, k)
                        for hh in range(HEADS):
                            for e in range(T):
                                last = pe.transpose(span(psA[:, 0:2, :])[:, (T * hh + e) * P:(T * hh + e + 1) * P], w4[:, hh, e * P:(e + 1) * P], ident[:])
                        last.then_inc(w_turned, 1)
                        pe.wait_ge(wT_ready, k + 1)
                        for hh in range(HEADS):
                            for e in range(T):
                                last = pe.matmul(psA[:, 2 + t, hh * P:(hh + 1) * P], wT[:, hh, e, :], v_a[:, e, hh * P:(hh + 1) * P],
                                                 start=(e == 0), stop=(e == T - 1))
                        last.then_inc(att_done, 1)
                    pe.wait_ge(att_ready, l + 1)
                    att = view(LOGF, T, 512)
                    for t in range(T):
                        for k in range(HEADS):
                            last = pe.transpose(psD[:, 2 + k // 2, (k % 2) * S + t * P:(k % 2) * S + (t + 1) * P], att[:, t, k * P:(k + 1) * P], ident[:])
                    last.then_inc(turned, 1)
                    xT_pieces(1)
                    for i in range(2):
                        contract(n + 1, n, xTh[:, 2 * i:2 * i + 2], xTl[:, 2 * i:2 * i + 2], psD, i == 0, i == 1)
                        n += 1
                    for i in range(2):
                        contract(n + 1, n, xTh[:, 4 + 2 * i:6 + 2 * i], xTl[:, 4 + 2 * i:6 + 2 * i], psA, i == 0, i == 1)
                        n += 1
                    for t in range(T):
                        pe.wait_ge(merged, T * l + t + 1)
                        for k in range(KT):
                            last = pe.transpose(psD[:, 2 * t + k // 4, (k % 4) * P:(k % 4 + 1) * P], xn[:, t, k * P:(k + 1) * P], ident[:])
                        last.then_inc(turned, 1)
                    xT_pieces(T)
                    for i in range(KT // 2):
                        contract(n + 1, n, xTh[:, 2 * i:2 * i + 2], xTl[:, 2 * i:2 * i + 2], psA, i == 0, i == KT // 2 - 1)
                        n += 1
            assert n == TOTAL


_INS = ["x", "p", "ffn1_norm", "ffn1_w_gate", "ffn1_w_up", "ffn1_w_down", "mix_norm", "lru_w_in", "lru_conv_w", "lru_conv_b",
        "lru_w_a", "lru_b_a", "lru_w_x", "lru_b_x", "lru_a_param", "lru_w_out", "pool_w", "pool_b", "pool_scale", "ffn2_norm",
        "ffn2_w_gate", "ffn2_w_up", "ffn2_w_down", "ple_norm", "ple_w_gate", "ple_w_proj", "final_norm", "positions_2", "w_in_2",
        "da_lambda_2", "da_norm_2", "hg_lb_logits_2", "hg_norm_2", "w_a_2", "w_b_2", "w_o_2", "attn_norm_2", "ffn_norm_2",
        "w_gate_2", "w_up_2", "w_down_2", "final_norm_2"]


def shape_constants():
    i = np.arange(P)
    level = np.zeros((P, len(LEVELS), P), np.int32)
    for e, m in enumerate(LEVELS):
        level[:, e, :] = (i[:, None] // m != i[None, :] // m) & (i[:, None] // (2 * m) == i[None, :] // (2 * m))
    pool = np.zeros((P, T, len(POOL_WINDOWS), S), np.float32)
    s = np.arange(S)
    for t in range(T):
        tok = t * P + i[:, None]
        for g, win in enumerate(POOL_WINDOWS):
            inside = (tok <= s[None, :]) & (tok > s[None, :] - win)
            pool[:, t, g, :] = inside / np.minimum(s[None, :] + 1, win).astype(np.float32) - (tok == s[None, :])
    freq = np.float32(500000.0) ** (-(np.arange(0, 2 * ROT, 2, dtype=np.float32) / np.float32(2 * ROT)))
    freq = np.tile(np.concatenate([freq, freq]).astype(np.float32), (P, 1))
    return {"c_ident": np.eye(P, dtype=np.float32), "c_level": level, "c_pool": pool, "c_freq": freq}


def kernel(**inputs):
    import concourse.bacc as bacc
    from concourse.bass_utils import run_bass_kernel_spmd

    nc = bacc.Bacc("TRN2", target_bir_lowering=False, num_devices=1)
    arrays, aps = {}, {}
    for name, v in [(k, inputs[k]) for k in _INS] + list(shape_constants().items()):
        v = np.ascontiguousarray(v)
        arrays[f"in_{name}"] = v
        aps[name] = nc.dram_tensor(f"in_{name}", v.shape, mybir.dt.from_np(v.dtype), kind="ExternalInput").ap()
    out = nc.dram_tensor("out_0", (1, S, D), F32, kind="ExternalOutput").ap()
    build(nc, aps, out)
    r = run_bass_kernel_spmd(nc, [arrays], core_ids=[0])
    return r.results[0]["out_0"]
```

```python
from contextlib import ExitStack

import numpy as np
import concourse.bass as bass
from concourse import mybir

F32 = mybir.dt.float32
F32R = mybir.dt.float32r
I32 = mybir.dt.int32
U8 = mybir.dt.uint8
ALU = mybir.AluOpType
ACT = mybir.ActivationFunctionType
AX_X = mybir.AxisListType.X

P = 128
S = 256
T = S // P
D = 1024
KT = D // P
F = 2816
R = 1280
RT = R // P
HD = 80
GT = 5
EPS = 1e-6
BW = 2048
FC = 256
CH = F // FC
RAW = 3
RING = 3
AHEAD = 2
HEADS = 4
LEVELS = (128, 64, 32, 16, 8, 4, 2, 1)
POOL_WINDOWS = (2, 4, 8, 16)
ROT = 8
TWO_PI = 6.283185307179586
PI_HI, PI_MID = 6.28125, 0.0019350051879882812
PI_LO = TWO_PI - PI_HI - PI_MID
ROUND = 12582912.0
LAM_INIT = [0.8 - 0.6 * float(np.exp(-0.3 * l)) for l in range(2)]

XN = 0
SIL, PROD = 2048, 3072
SIG = 2048
PTOK = 8192
L_R = 0
L_XB = 2560
L_XC = L_XB + RT * (S + 3) + 2
L_GELU = L_XC + RT * S
L_IG = L_GELU + RT * S
L_T = L_IG + RT * S
BAND = L_T + GT * S
POOL_M, POOL_B, POOL_S = 4096, 6144, 7168
Z, Q_B, V_B, A_QK, A_V, G_B, GATE_A, GATE_B = 2048, 4096, 5120, 6144, 8192, 9216, 10240, 12288
LOGF, TMP, KK = 14336, 16384, 18432
NRM_DA, NRM_HG, LAM = 20480, 20992, 21504
ATT = 21760
PROB, W_ATT, W_T = A_QK, A_QK + 1024, A_QK + 1536
QK_T = GATE_B
SCRATCH = 22784
assert BAND + 2 * 2 * GT * 384 <= SCRATCH


def head_pieces():
    out = []
    for head in range(8):
        row = 0
        while row < HD:
            at = head * HD + row
            n = min(HD - row, P - at % P)
            out.append((head, row, at // P, at % P, n))
            row += n
    return out


def build(nc, a, out):
    ctx = ExitStack()

    def sb(name, shape, dt=F32):
        return ctx.enter_context(nc.sbuf_tensor(name, shape, dt))

    def sem(name):
        return ctx.enter_context(nc.semaphore(name))

    with ctx:
        raw = sb("raw", [P, RAW, BW])
        hi = sb("hi", [P, RING, BW], F32R)
        lo = sb("lo", [P, RING, BW], F32R)
        h = sb("h", [P, T, D])
        xTh = sb("xTh", [P, RT, S], F32R)
        xTl = sb("xTl", [P, RT, S], F32R)
        prod_hi = sb("prod_hi", [P, 2, 2, S], F32R)
        prod_lo = sb("prod_lo", [P, 2, 2, S], F32R)
        gain = sb("gain", [P, D])
        ident = sb("ident", [P, P])
        level_mask = sb("level_mask", [P, len(LEVELS), P], U8)
        scr = sb("scr", [P, SCRATCH])
        stat = sb("stat", [P, 96])
        conv_w = sb("conv_w", [P, 4, RT])
        lru_c = sb("lru_c", [P, 4, RT])
        cpos = sb("cpos", [P, 6, RT])
        eps = sb("eps", [P, 2])
        rope_in = sb("rope_in", [P, 2 * ROT])
        pos_i = sb("pos_i", [P, T], I32)
        rope = sb("rope", [P, 8, T, ROT])
        one_row = sb("one_row", [P, P])
        lbt = sb("lbt", [P, 12, 2, HEADS])

        psA = ctx.enter_context(nc.psum_tensor("psA", [P, 4, 512], F32))
        psD = ctx.enter_context(nc.psum_tensor("psD", [P, 4, 512], F32))

        def view(at, *shape):
            n = int(np.prod(shape))
            v = scr[:, at:at + n]
            names = "abcd"[:len(shape)]
            if len(shape) == 1:
                return v
            return v.rearrange(f"p ({' '.join(names)}) -> p {' '.join(names)}", **dict(zip(names[1:], shape[1:])))

        xn = view(XN, T, D)
        tmp_att = view(PROB, T * 512)
        level_words = view(POOL_M, len(LEVELS), P).bitcast(I32)
        sil, prod = view(SIL, 2, 2 * S), view(PROD, 2, 2 * S)

        raw_landed = [sem(f"raw_landed{i}") for i in range(RAW)]
        hi_ready, lo_ready, block_used = sem("hi_ready"), sem("lo_ready"), sem("block_used")
        x_loaded, consts_loaded, gain_loaded = sem("x_loaded"), sem("consts_loaded"), sem("gain_loaded")
        band_zeroed, band_loaded = sem("band_zeroed"), sem("band_loaded")
        p_loaded, pool_loaded, mix_loaded = sem("p_loaded"), sem("pool_loaded"), sem("mix_loaded")
        ident_loaded, first_gain_loaded = sem("ident_loaded"), sem("first_gain_loaded")
        h_ready, ssq_ready, rms_ready, xn_ready = sem("h_ready"), sem("ssq_ready"), sem("rms_ready"), sem("xn_ready")
        turned, xTh_ready, xT_ready = sem("turned"), sem("xTh_ready"), sem("xT_ready")
        silu_ready, prod_ready = sem("silu_ready"), sem("prod_ready")
        prod_hi_ready, prod_lo_ready = sem("prod_hi_ready"), sem("prod_lo_ready")
        dve_step, act_step = sem("dve_step"), sem("act_step")
        eps_ready, cpos_exp, cpos_ready = sem("eps_ready"), sem("cpos_exp"), sem("cpos_ready")
        xb_ready, xc_ready, gates_done, gates_ready = sem("xb_ready"), sem("xc_ready"), sem("gates_done"), sem("gates_ready")
        tanh_ready, decay_ready, ratio_ready, mult_ready = sem("tanh_ready"), sem("decay_ready"), sem("ratio_ready"), sem("mult_ready")
        gelu_ready, y_ready, sig_ready = sem("gelu_ready"), sem("y_ready"), sem("sig_ready")
        angles_ready, rope_ready = sem("angles_ready"), sem("rope_ready")
        proj_evac = sem("proj_evac")
        gap_ready, soft_ready, kk_ready = sem("gap_ready"), sem("soft_ready"), sem("kk_ready")
        lb_in, lb_out = sem("lb_in"), sem("lb_out")
        decay_in, decay_out = sem("decay_in"), sem("decay_out")
        scaled_ready, pair_done, pair_taken = sem("scaled_ready"), sem("pair_done"), sem("pair_taken")
        rec_done, rec_square, rec_sum, rec_rms, rec_ready = sem("rec_done"), sem("rec_square"), sem("rec_sum"), sem("rec_rms"), sem("rec_ready")
        roped, qk_turned, qkT_ready = sem("roped"), sem("qk_turned"), sem("qkT_ready")
        scores_done, max_ready, exp_ready, w_ready = sem("scores_done"), sem("max_ready"), sem("exp_ready"), sem("w_ready")
        w_turned, wT_ready, att_done, att_rows = sem("w_turned"), sem("wT_ready"), sem("att_done"), sem("att_rows")
        att_square, att_sum, att_rms, att_ready = sem("att_square"), sem("att_sum"), sem("att_rms"), sem("att_ready")
        lam_in, lam_exp = sem("lam_in"), sem("lam_exp")
        merged, rows_done = sem("merged"), sem("rows_done")
        stored = sem("stored")

        def columns(w, c, n=FC):
            return w[:, c * n:(c + 1) * n].rearrange("(k p) f -> p k f", p=P)

        def rows(w, c):
            return w[c * 2 * P:(c + 1) * 2 * P, :].rearrange("(k p) n -> p k n", p=P)

        def dst(n, src):
            k = src.shape[1]
            return raw[:, n % RAW, :].rearrange("p (k f) -> p k f", k=k)

        plan = []
        for i in range(2):
            plan += [("norm", a["ffn1_norm"][i]), ("ffn", a["ffn1_w_gate"][i], a["ffn1_w_up"][i], a["ffn1_w_down"][i], 0.5)]
            plan += [("norm", a["mix_norm"][i]), ("lru",)] if i == 0 else [("pool", a["mix_norm"][i])]
            plan += [("norm", a["ffn2_norm"][i]), ("ffn", a["ffn2_w_gate"][i], a["ffn2_w_up"][i], a["ffn2_w_down"][i], 0.5)]
            plan += [("ple", a["ple_norm"][i], i)]
        plan += [("rescale", a["final_norm"])]
        for l in range(2):
            plan += [("norm", a["attn_norm_2"][l]), ("mix", l)]
            plan += [("norm", a["ffn_norm_2"][l]), ("ffn", a["w_gate_2"][l], a["w_up_2"][l], a["w_down_2"][l], 1.0)]
        plan += [("rescale", a["final_norm_2"])]
        BLOCKS = {"norm": 0, "rescale": 0, "ffn": 3 * CH, "lru": 2 * R // FC + R // (2 * P), "pool": 1, "ple": KT // 2 + 1,
                  "mix": 6 * D // FC + 8}
        CONSTS = 12
        TOTAL = sum(BLOCKS[s[0]] for s in plan)
        gains = [s[1] for s in plan if s[0] in ("norm", "pool", "rescale", "ple")]
        FF, FB, QB, IB, AQ, AK, AV, GB_ = 8, 10, 6, 12, 0, 2, 4, 14
        PROJ = [(c + j, c) for c in (FF, FB, QB, AQ, AK, AV, IB, GB_) for j in range(2)]
        PROJ += [(16 + j, 16) for j in range(4)] + [(20 + j, 20) for j in range(4)]
        NP, NL = len(PROJ), len(LEVELS)
        UNITS = 2 * T
        SOFTS = (2, 4)

        block = ctx.enter_context(nc.Block())

        @block.sync
        def _(sp):
            sp.dma_start(h[:], a["x"].rearrange("b (t p) d -> p (b t) d", p=P)).then_inc(x_loaded, 16)
            n = 0

            def load(n_at, n, src):
                if isinstance(n_at, int):
                    if n_at >= RAW:
                        sp.wait_ge(lo_ready, n_at - RAW + 1)
                else:
                    sp.wait_ge(lo_ready, n_at - (RAW - 1))
                sp.dma_start(dst(n, src), src).then_inc(raw_landed[n % RAW], 16)

            for stage, nxt in zip(plan, plan[1:] + [("end",)]):
                kind = stage[0]
                if kind == "ffn":
                    _, wg, wu, wd, _ = stage
                    for src in (columns(wg, 0), columns(wu, 0), columns(wg, 1), columns(wu, 1), rows(wd, 0)):
                        load(n, n, src)
                        n += 1
                    with sp.Fori(0, (CH - 3) // 2) as j:
                        for e in range(2):
                            up = wg[:, bass.ds((2 * j + (e + 2)) * FC, FC)], wu[:, bass.ds((2 * j + (e + 2)) * FC, FC)]
                            down = wd[bass.ds((2 * j + (e + 1)) * FC, FC), :]
                            for b, src in enumerate([x.rearrange("(k p) f -> p k f", p=P) for x in (*up, down)]):
                                load(6 * j + (n + 3 * e + b), n + 3 * e + b, src)
                    n += 3 * (CH - 3)
                    for src in (columns(wg, CH - 1), columns(wu, CH - 1), rows(wd, CH - 2), rows(wd, CH - 1)):
                        load(n, n, src)
                        n += 1
                    continue
                srcs = []
                if kind == "lru":
                    w_in = a["lru_w_in"][0]
                    half = R // FC
                    srcs = [columns(w_in, half + c) for c in range(half)] + [columns(w_in, c) for c in range(half)]
                    srcs += [rows(a["lru_w_out"][0], c) for c in range(R // (2 * P))]
                if kind == "pool":
                    src = a["pool_w"][0].rearrange("g (k p) d -> p (g k) d", p=P)
                    srcs = [src]
                if kind == "ple":
                    srcs = [rows(a["ple_w_proj"][stage[2]], 0)] + [rows(a["ple_w_gate"][stage[2]], c) for c in range(KT // 2)]
                if kind == "mix":
                    l = stage[1]
                    srcs = [columns(a["w_in_2"][l], c) for c, _ in PROJ]
                    srcs += [rows(a["w_a_2"][l], c) for c in range(2)] + [rows(a["w_b_2"][l], c) for c in range(2)]
                    srcs += [rows(a["w_o_2"][l], c) for c in range(4)]
                for src in srcs:
                    load(n, n, src)
                    n += 1
            assert n == TOTAL
            updates = 2 * (1 + sum(s[0] in ("ffn", "lru", "pool", "ple", "mix", "rescale") for s in plan))
            sp.wait_ge(h_ready, updates)
            sp.dma_start(out.rearrange("b (t p) d -> p (b t) d", p=P), h[:]).then_inc(stored, 16)
            sp.wait_ge(stored, 16)

        @block.gpsimd
        def _(pool):
            band = view(BAND, 2, 2, GT, 384)
            pool.memset(scr[:, BAND:BAND + 2 * 2 * GT * 384], 0.0).then_inc(band_zeroed, 1)
            for t_, src in ((level_words, a["c_level"]), (rope_in[:], a["c_freq"]),
                            (pos_i[:], a["positions_2"].rearrange("b (t p) -> p (b t)", p=P)),
                            (conv_w[:], a["lru_conv_w"][0].rearrange("k (f p) -> p k f", p=P)),
                            (lru_c[:, 0, :], a["lru_conv_b"][0].rearrange("(f p) -> p f", p=P)),
                            (lru_c[:, 1, :], a["lru_b_a"][0].rearrange("(f p) -> p f", p=P)),
                            (lru_c[:, 2, :], a["lru_b_x"][0].rearrange("(f p) -> p f", p=P)),
                            (lru_c[:, 3, :], a["lru_a_param"][0].rearrange("(f p) -> p f", p=P)),
                            *((lbt[:, l, e, :], a["hg_lb_logits_2"][e, l, :].rearrange("(f p) -> p f", p=P)) for l in range(2) for e in range(2))):
                pool.dma_start(t_, src, allow_slow_non_contiguous=True).then_inc(consts_loaded, 16)
            pool.wait_ge(band_zeroed, 1)
            for m, w in enumerate((a["lru_w_a"][0], a["lru_w_x"][0])):
                for head, row, tile, part, cnt in head_pieces():
                    col = head * HD - (tile - 1) * P
                    for g in range(2):
                        pool.dma_start(band[part:part + cnt, m, g, tile, col:col + HD],
                                       w[8 * g + head, row:row + cnt, :]).then_inc(band_loaded, 16)
            normed = updates = 0
            for stage, nxt in zip(plan, plan[1:] + [("end",)]):
                kind = stage[0]
                if kind in ("norm", "pool", "rescale", "ple"):
                    normed += 1
                    if normed < len(gains):
                        pool.wait_ge(xn_ready, 2 * normed)
                        pool.dma_start(gain[:], gains[normed].rearrange("(o d) -> o d", o=1).broadcast_to([P, D])).then_inc(gain_loaded, 16)
                if kind in ("ffn", "lru", "pool", "ple", "mix", "rescale"):
                    updates += 1
                if kind == "lru":
                    pool.wait_ge(h_ready, 2 * updates + 2)
                    pool.dma_start(view(POOL_M, T, 4, S), a["c_pool"]).then_inc(pool_loaded, 16)
                    pool.dma_start(view(POOL_B, D), a["pool_b"].broadcast_to([P, D])).then_inc(pool_loaded, 16)
                    pool.dma_start(view(POOL_S, D), a["pool_scale"].broadcast_to([P, D])).then_inc(pool_loaded, 16)
                if kind == "lru" or kind == "ple" and stage[2] == 0:
                    i = 0 if kind == "lru" else 1
                    pool.wait_ge(h_ready, 2 * updates + 2)
                    pool.dma_start(view(PTOK, T, S), a["p"][i].rearrange("b (t p) d -> p (b t) d", p=P)).then_inc(p_loaded, 16)
                if kind == "lru" or kind == "mix" and stage[1] == 0:
                    l = 0 if kind == "lru" else 1
                    pool.wait_ge(h_ready, 2 * updates + 2)
                    pool.dma_start(view(NRM_DA, 512), a["da_norm_2"][l].rearrange("(o d) -> o d", o=1).broadcast_to([P, 512])).then_inc(mix_loaded, 16)
                    pool.dma_start(view(NRM_HG, 512), a["hg_norm_2"][l].rearrange("(o d) -> o d", o=1).broadcast_to([P, 512])).then_inc(mix_loaded, 16)
                    pool.dma_start(view(LAM, 256), a["da_lambda_2"][l].rearrange("(o i) d -> o (i d)", o=1).broadcast_to([P, 256])).then_inc(mix_loaded, 16)

        def norm_piece(t):
            ps = psA[:, 2 * t:2 * t + 2, :].rearrange("p b (k s) -> p (b k) s", k=4)
            return ps, (slice(0, KT), slice(t * P, (t + 1) * P))

        def pool_piece(t):
            ps = psA[:, 2 * t:2 * t + 2, :].rearrange("p b (k s) -> p (b k) s", k=2)
            return ps, (slice(4 * t, 4 * t + 4), slice(0, S))

        def ple_piece():
            return psA[:, 1, :].rearrange("p (k s) -> p k s", k=2), (slice(8, 10), slice(0, S))

        def merge_piece(t):
            ps = psD[:, 2 * t:2 * t + 2, :].rearrange("p b (k s) -> p (b k) s", k=4)
            return ps, (slice(0, KT), slice(t * P, (t + 1) * P))

        def rec_piece():
            return psD[:, 0:2, :].rearrange("p b (k s) -> p (b k) s", k=2), (slice(4, 8), slice(0, S))

        def att_piece():
            return psA[:, 2:4, :].rearrange("p b (k s) -> p (b k) s", k=2), None

        x_att = [v[:, :, :, :].rearrange("p c f s -> p (c f) s") for v in (prod_hi, prod_lo)]

        def halves(v, m):
            return v.rearrange("p (n e m) -> p n e m", e=2, m=m)

        def span(v):
            return v.rearrange("p a b -> p (a b)")

        @block.scalar
        def _(act):
            st = {"split": 0, "norm": 0, "updates": 0, "piece": 0, "ffn": 0, "step": 0, "rows": 0, "turned": 0}

            def step(ins):
                ins.then_inc(act_step, 1)
                st["step"] += 1

            def settle():
                act.wait_ge(act_step, st["step"])

            def split(n_at, n):
                if isinstance(n_at, int):
                    act.wait_ge(raw_landed[n % RAW], 16 * (n // RAW + 1))
                    if n >= RING:
                        act.wait_ge(block_used, n - RING + 1)
                else:
                    act.wait_ge(raw_landed[n % RAW], 32 * n_at + 16 * (n // RAW + 1))
                    act.wait_ge(block_used, 6 * n_at + (n - RING + 1))
                act.activation(hi[:, n % RING, :], raw[:, n % RAW, :], ACT.Copy).then_inc(hi_ready, 1)

            def split_to(n):
                while st["split"] <= min(n + AHEAD, TOTAL - 1):
                    split(st["split"], st["split"])
                    st["split"] += 1

            def piece(src, to, wait=None):
                st["piece"] += 1
                if wait is None:
                    st["turned"] += 1
                    act.wait_ge(turned, st["turned"])
                act.activation(xTh[:, to[0], to[1]] if to else x_att[0], src, ACT.Copy).then_inc(xTh_ready, 1)

            def norm_stats():
                for t in range(T):
                    act.wait_ge(h_ready, 2 * st["updates"] + 1 + t)
                    act.activation(xn[:, t, :], h[:, t, :], ACT.Square, accum_out=stat[:, t:t + 1]).then_inc(ssq_ready, 1)
                    act.wait_ge(ssq_ready, 2 * st["norm"] + t + 1)
                    act.activation(stat[:, 2 + t:3 + t], stat[:, t:t + 1], ACT.Sqrt, bias=eps[:, 0:1], scale=1.0 / D).then_inc(rms_ready, 1)
                st["norm"] += 1

            act.dma_start(gain[:], gains[0].rearrange("(o d) -> o d", o=1).broadcast_to([P, D])).then_inc(first_gain_loaded, 16)
            act.dma_start(ident[:], a["c_ident"]).then_inc(ident_loaded, 16)
            act.wait_ge(eps_ready, 2)
            n = 0
            def constants():
                act.wait_ge(cpos_exp, 1)
                act.activation(cpos[:, 1, :], cpos[:, 0, :], ACT.Exp, scale=-1.0).then_inc(cpos_exp, 1)
                act.wait_ge(angles_ready, 1)
                act.activation(rope[:, 0, :, :], rope[:, 4, :, :], ACT.Sin).then_inc(rope_ready, 1)
                act.activation(rope[:, 1, :, :], rope[:, 5, :, :], ACT.Sin).then_inc(rope_ready, 1)
                act.wait_ge(lb_in, 1)
                act.activation(lbt[:, 4, :, :], lbt[:, 3, :, :], ACT.Exp, scale=-1.0).then_inc(lb_out, 1)
                act.wait_ge(lb_out, 1)
                act.activation(lbt[:, 5, :, :], lbt[:, 4, :, :], ACT.Ln, bias=eps[:, 1:2]).then_inc(lb_out, 1)
                act.activation(lbt[:, 6, :, :], lbt[:, 2, :, :], ACT.Sigmoid, scale=-1.0).then_inc(lb_out, 1)

            for stage, nxt in zip(plan, plan[1:] + [("end",)]):
                kind = stage[0]
                if kind == "norm":
                    split_to(n - 1)
                    norm_stats()
                    for t in range(T):
                        piece(*norm_piece(t))
                if kind == "rescale":
                    split_to(n - 1)
                    norm_stats()
                    st["updates"] += 1
                if kind == "pool":
                    split_to(n - 1)
                    norm_stats()
                    for t in range(T):
                        piece(*pool_piece(t))
                    split_to(n)
                    n += 1
                    st["updates"] += 1
                if kind == "ffn":
                    def gated(c_at, c, used):
                        act.wait_ge(block_used, used)
                        act.activation(sil[:, c % 2, :], psA[:, c % 2, :], ACT.Silu).then_inc(silu_ready, 1)
                        act.wait_ge(prod_ready, c_at + 1)
                        act.activation(span(prod_hi[:, c % 2]), prod[:, c % 2, :], ACT.Copy).then_inc(prod_hi_ready, 1)

                    c0 = st["ffn"] * CH
                    for b in range(5):
                        split_to(n)
                        if b in (1, 3):
                            gated(c0 + b // 2, b // 2, n + 1)
                        n += 1
                    with act.Fori(0, (CH - 3) // 2) as j:
                        for b in range(6):
                            split(j, n + b + AHEAD)
                            if b % 3 == 1:
                                gated(2 * j + (c0 + 2 + b // 3), b // 3, 6 * j + (n + b + 1))
                    n += 3 * (CH - 3)
                    st["split"] += 3 * (CH - 3)
                    for b in range(4):
                        split_to(n)
                        if b == 1:
                            gated(c0 + CH - 1, CH - 1, n + 1)
                        if b == 2 and nxt[0] == "ple":
                            piece(*ple_piece())
                        if b == 2 and st["ffn"] == 0:
                            constants()
                        n += 1
                    st["ffn"] += 1
                    st["rows"] += 1
                    st["updates"] += 1
                if kind == "lru":
                    half = R // FC
                    xb = view(L_XB, RT, S + 3) if (RT * (S + 3)) else None
                    gelu = view(L_GELU, RT, S)
                    r, ig, th = view(L_R, RT, S), view(L_IG, RT, S), view(L_T, GT, S)
                    ratio = view(L_XB, RT, S)

                    def recurrent_gates(g):
                        for m in range(GT):
                            ft = g * GT + m
                            act.wait_ge(gates_done, ft + 1)
                            act.activation(r[:, ft, :], psD[:, ft % 4, 0:S], ACT.Sigmoid, bias=lru_c[:, 1, ft:ft + 1]).then_inc(gates_ready, 1)
                            act.activation(ig[:, ft, :], psD[:, ft % 4, S:2 * S], ACT.Sigmoid, bias=lru_c[:, 2, ft:ft + 1]).then_inc(gates_ready, 1)
                        if g:
                            act.wait_ge(ratio_ready, g)
                        act.wait_ge(cpos_ready, 2)
                        act.wait_ge(gates_ready, 2 * GT * (g + 1))
                        for m in range(GT):
                            ft = g * GT + m
                            act.activation(th[:, m, :], r[:, ft, :], ACT.Tanh, scale=cpos[:, 4, ft:ft + 1]).then_inc(tanh_ready, 1)

                    def recurrent_decay(g):
                        act.wait_ge(tanh_ready, GT * (g + 1))
                        for m in range(GT):
                            ft = g * GT + m
                            act.activation(r[:, ft, :], r[:, ft, :], ACT.Exp, scale=cpos[:, 5, ft:ft + 1]).then_inc(decay_ready, 1)
                        act.wait_ge(ratio_ready, g + 1)
                        v = ratio[:, g * GT:(g + 1) * GT, :]
                        act.activation(v, v, ACT.Sqrt, scale=2.0).then_inc(mult_ready, 1)

                    for i in range(2 * half):
                        split_to(n)
                        act.wait_ge(block_used, n + 1)
                        ps = psA[:, i % 4, :].rearrange("p (f s) -> p f s", f=2)
                        if i < half:
                            act.activation(xb[:, 2 * i:2 * i + 2, 3:S + 3], ps, ACT.Copy).then_inc(xb_ready, 1)
                        else:
                            i2 = 2 * (i - half)
                            act.activation(gelu[:, i2:i2 + 2, :], ps, ACT.Gelu_apprx_tanh).then_inc(gelu_ready, 1)
                        n += 1
                        if i == half:
                            recurrent_gates(0)
                        if i == half + 1:
                            recurrent_gates(1)
                        if i in (half + 2, half + 3):
                            recurrent_decay(i - half - 2)
                    for g in range(2):
                        act.wait_ge(y_ready, g + 1)
                        act.wait_ge(block_used, n)
                        piece(view(L_XC, RT, S)[:, g * GT:(g + 1) * GT, :], (slice(g * GT, (g + 1) * GT), slice(0, S)), wait="y")
                    for i in range(R // (2 * P)):
                        split_to(n)
                        n += 1
                    st["rows"] += 1
                    st["updates"] += 1
                if kind == "ple":
                    split_to(n)
                    norm_stats()
                    for t in range(T):
                        piece(*merge_piece(t))
                    for i in range(KT // 2 + 1):
                        split_to(n)
                        n += 1
                    sig = view(SIG, T, D)
                    st["rows"] += 1
                    for t in range(T):
                        if t == 0:
                            act.wait_ge(rows_done, st["rows"])
                        else:
                            act.wait_ge(block_used, n)
                        act.activation(sig[:, t, :], span(psD[:, 2 * t:2 * t + 2, :]), ACT.Sigmoid).then_inc(sig_ready, 1)
                    st["updates"] += 1
                if kind == "mix":
                    l = stage[1]
                    HS = HEADS * S
                    n0 = n
                    z2, tmp2, e2, kk2 = (view(at, 2 * HS) for at in (Z, TMP, LOGF, KK))
                    near, cross = view(XN, 8, P), view(XN + 1024, 8, P)
                    pairs = psD[:, 0:2, :].rearrange("p b (e s) -> p (b e) s", s=P)
                    prob = view(PROB, 4, S)

                    def soft(d, src):
                        to = tmp2[:, d * HS:(d + 1) * HS]
                        step(act.activation(to, src, ACT.Abs))
                        settle()
                        step(act.activation(to, to, ACT.Exp, scale=-1.0))
                        settle()
                        act.activation(to, to, ACT.Ln, bias=eps[:, 1:2]).then_inc(soft_ready, 1)

                    def level(i):
                        act.wait_ge(decay_in, NL * l + i + 1)
                        act.activation(e2, e2, ACT.Exp).then_inc(decay_out, 1)

                    def take(i):
                        act.wait_ge(pair_done, (NL + 1) * l + i + 2)
                        act.activation(near if i < 0 else cross, pairs, ACT.Copy).then_inc(pair_taken, 1)

                    def exponentials(u):
                        k = UNITS * l + u
                        act.wait_ge(max_ready, k + 1)
                        if k:
                            act.wait_ge(w_ready, 2 * k)
                        for e in range(4):
                            ps = psA[:, 2 + e // 2, (e % 2) * S:(e % 2 + 1) * S]
                            act.activation(prob[:, e, :], ps, ACT.Exp, bias=stat[:, 48 + e:49 + e], scale=0.125,
                                           accum_out=stat[:, 56 + e:57 + e]).then_inc(exp_ready, 1)

                    def weights_turned(u):
                        act.wait_ge(w_turned, UNITS * l + u + 1)
                        act.activation(view(W_T, 512), psD[:, 2, :], ACT.Copy).then_inc(wT_ready, 1)

                    def rows_out(u):
                        act.wait_ge(att_done, UNITS * l + u + 1)
                        act.activation(view(ATT, T, 512)[:, u // 2, (u % 2) * S:(u % 2 + 1) * S], psD[:, 3, 0:S], ACT.Copy).then_inc(att_rows, 1)

                    for i, (c, first) in enumerate(PROJ):
                        split_to(n)
                        act.wait_ge(block_used, n + 1)
                        j = c - first
                        ps = psA[:, i % 2, :].rearrange("p (f s) -> p f s", f=2)
                        if first in (FF, FB, QB):
                            at = {FF: Z, FB: Z + 1024, QB: Q_B}[first] + 512 * j
                            to, fn = view(at, 2, S), ACT.Copy
                        else:
                            at, wide, fn = {AQ: (A_QK, 512, ACT.Copy), AK: (A_QK + 1024, 512, ACT.Copy), AV: (A_V, 512, ACT.Copy),
                                            IB: (V_B, 512, ACT.Copy), GB_: (G_B, 512, ACT.Tanh),
                                            16: (GATE_A, D, ACT.Tanh), 20: (GATE_B, D, ACT.Tanh)}[first]
                            to = view(at, T, wide)[:, :, j * FC:(j + 1) * FC]
                        act.activation(to, ps, fn, scale=0.5 if fn == ACT.Tanh else 1.0).then_inc(proj_evac, 1)
                        n += 1
                        if i in (1, 3):
                            d = i // 2
                            act.wait_ge(proj_evac, NP * l + i + 1)
                            soft(d, z2[:, d * HS:(d + 1) * HS])
                            act.activation(kk2[:, d * HS:(d + 1) * HS], z2[:, d * HS:(d + 1) * HS], ACT.Sigmoid, scale=-1.0).then_inc(kk_ready, 1)
                        if i in (2, 4) and l:
                            d = i // 2 - 1
                            act.wait_ge(gap_ready, d + 1)
                            soft(d, tmp2[:, d * HS:(d + 1) * HS])
                        if i == 7:
                            take(-1)
                        if i == 9:
                            take(0)
                        if i % 2 == 0 and 0 <= (i - 6) // 2 < NL:
                            level((i - 6) // 2)
                        if i in (9, 11):
                            e = (i - 9) // 2
                            act.wait_ge(qk_turned, 2 * l + e + 1)
                            act.activation(view(QK_T + 1024 * e, 1024), span(psA[:, 2:4, :]), ACT.Copy).then_inc(qkT_ready, 1)
                        if i == 10:
                            act.wait_ge(lam_in, l + 1)
                            act.activation(stat[:, 42:44], stat[:, 40:42], ACT.Exp).then_inc(lam_exp, 1)
                        for u in range(UNITS):
                            if i == 12 + 2 * u:
                                exponentials(u)
                            if i == 14 + 2 * u:
                                weights_turned(u)
                            if i == 15 + 2 * u:
                                rows_out(u)
                        if i == 21:
                            act.wait_ge(att_rows, UNITS * (l + 1))
                            act.activation(tmp_att, view(ATT, T * 512), ACT.Square).then_inc(att_square, 1)
                        if i == 22:
                            act.wait_ge(att_sum, l + 1)
                            act.activation(stat[:, 24:32], stat[:, 16:24], ACT.Sqrt, bias=eps[:, 0:1], scale=1.0 / P).then_inc(att_rms, 1)
                    piece(*att_piece())
                    split_to(n)
                    act.wait_ge(rec_done, l + 1)
                    act.activation(tmp2[:, 0:T * 512], span(psD[:, 0:2, :]), ACT.Square).then_inc(rec_square, 1)
                    act.wait_ge(rec_sum, l + 1)
                    act.activation(stat[:, 24:32], stat[:, 16:24], ACT.Sqrt, bias=eps[:, 0:1], scale=1.0 / P).then_inc(rec_rms, 1)
                    split_to(n + 1)
                    piece(*rec_piece())
                    for i in range(4):
                        split_to(n)
                        n += 1
                    for t in range(T):
                        piece(*merge_piece(t))
                    for i in range(4):
                        split_to(n)
                        n += 1
                    st["rows"] += 3
                    st["updates"] += 1

        @block.vector
        def _(dve):
            st = {"split": 0, "norm": 0, "updates": 0, "piece": 0, "ffn": 0, "step": 0, "rows": 0}

            def step(ins):
                ins.then_inc(dve_step, 1)
                st["step"] += 1

            def settle():
                dve.wait_ge(dve_step, st["step"])

            def split(n_at, n):
                dve.wait_ge(hi_ready, n_at if n_at is not None else n + 1)
                dve.tensor_tensor(lo[:, n % RING, :], raw[:, n % RAW, :], hi[:, n % RING, :].bitcast(F32), ALU.subtract).then_inc(lo_ready, 1)

            def split_to(n):
                while st["split"] <= min(n + AHEAD, TOTAL - 1):
                    split(None, st["split"])
                    st["split"] += 1

            def piece(src, to):
                st["piece"] += 1
                dve.wait_ge(xTh_ready, st["piece"])
                x_hi, x_lo = (xTh[:, to[0], to[1]], xTl[:, to[0], to[1]]) if to else x_att
                dve.tensor_tensor(x_lo, src, x_hi.bitcast(F32), ALU.subtract).then_inc(xT_ready, 1)

            def inverse_root(count, width, mean, root, v, inv, t_):
                at = lambda c: stat[:, c:c + width]
                step(dve.tensor_scalar(at(v), at(mean), 1.0 / count, EPS, ALU.mult, ALU.add))
                step(dve.reciprocal(at(inv), at(root)))
                settle()
                step(dve.tensor_tensor(at(t_), at(inv), at(inv), ALU.mult))
                settle()
                step(dve.tensor_tensor(at(t_), at(t_), at(v), ALU.mult))
                settle()
                step(dve.tensor_scalar(at(t_), at(t_), -0.5, 1.5, ALU.mult, ALU.add))
                settle()
                step(dve.tensor_tensor(at(inv), at(inv), at(t_), ALU.mult))
                settle()

            def summed(t, n):
                if t == 0:
                    st["rows"] += 1
                    dve.wait_ge(rows_done, st["rows"])
                else:
                    dve.wait_ge(block_used, n)

            def norm_rows(to):
                st["norm"] += 1
                for t in range(T):
                    dve.wait_ge(rms_ready, T * (st["norm"] - 1) + t + 1)
                    inverse_root(D, 1, t, 2 + t, 4 + t, 6 + t, 8 + t)
                    if st["norm"] == 1:
                        dve.wait_ge(first_gain_loaded, 16)
                    else:
                        dve.wait_ge(gain_loaded, 16 * (st["norm"] - 1))
                    dve.scalar_tensor_tensor(to[:, t, :], h[:, t, :], stat[:, 6 + t:7 + t], gain[:], ALU.mult, ALU.mult).then_inc(xn_ready, 1)

            def head_norm(src, squares, square_ready, nth, sum_ready, root_ready, nrm, factor, to):
                heads = lambda v: v.rearrange("p (e v) -> p e v", v=P)
                dve.wait_ge(square_ready, nth)
                dve.tensor_reduce(stat[:, 16:24], heads(squares), AX_X, ALU.add).then_inc(sum_ready, 1)
                dve.wait_ge(root_ready, nth)
                inverse_root(P, 8, 16, 24, 32, 80, 88)
                step(dve.tensor_tensor(heads(to), heads(src), stat[:, 80:88].unsqueeze(2).broadcast_to([P, 8, P]), ALU.mult))
                settle()
                dve.wait_ge(mix_loaded, 48 * nth)
                rows_ = to.rearrange("p (t f) -> p t f", t=T)
                gains_ = scr[:, nrm:nrm + 512].unsqueeze(1).broadcast_to([P, T, 512])
                return dve.scalar_tensor_tensor(rows_, rows_, factor, gains_, ALU.mult, ALU.mult)

            dve.memset(eps[:, 0:1], EPS).then_inc(eps_ready, 1)
            dve.memset(eps[:, 1:2], 1.0).then_inc(eps_ready, 1)
            step(dve.memset(one_row[:], 1.0))

            def constants():
                dve.wait_ge(consts_loaded, 16 * CONSTS)
                step(dve.tensor_copy(level_mask[:], level_words))
                dve.scalar_tensor_tensor(cpos[:, 0, :], lru_c[:, 3, :], -1.0, lru_c[:, 3, :], ALU.mult, ALU.max).then_inc(cpos_exp, 1)
                step(dve.tensor_copy(stat[:, 10:12], pos_i[:]))
                settle()
                for t in range(T):
                    step(dve.tensor_scalar(rope[:, 2, t, :], rope_in[:, 0:ROT], stat[:, 10 + t:11 + t], None, ALU.mult))
                settle()
                for shift, to in ((0.0, 4), (0.25, 5)):
                    step(dve.tensor_scalar(rope[:, 3, :, :], rope[:, 2, :, :], 1.0 / TWO_PI, shift, ALU.mult, ALU.add))
                    settle()
                    step(dve.tensor_scalar(rope[:, 3, :, :], rope[:, 3, :, :], ROUND, None, ALU.add))
                    settle()
                    step(dve.tensor_scalar(rope[:, 3, :, :], rope[:, 3, :, :], ROUND, None, ALU.subtract))
                    settle()
                    step(dve.scalar_tensor_tensor(rope[:, to, :, :], rope[:, 3, :, :], -PI_HI, rope[:, 2, :, :], ALU.mult, ALU.add))
                    settle()
                    step(dve.scalar_tensor_tensor(rope[:, to, :, :], rope[:, 3, :, :], -PI_MID, rope[:, to, :, :], ALU.mult, ALU.add))
                    settle()
                    step(dve.scalar_tensor_tensor(rope[:, to, :, :], rope[:, 3, :, :], -PI_LO, rope[:, to, :, :], ALU.mult, ALU.add))
                    settle()
                    if to == 5:
                        step(dve.tensor_scalar(rope[:, to, :, :], rope[:, to, :, :], TWO_PI / 4, None, ALU.add))
                        settle()
                    last = dve.tensor_scalar(rope[:, to, :, :], rope[:, to, :, :], 3.1415925, -3.1415925, ALU.min, ALU.max)
                    if to == 4:
                        step(last)
                        settle()
                    else:
                        last.then_inc(angles_ready, 1)
                dve.wait_ge(cpos_exp, 2)
                step(dve.tensor_scalar(cpos[:, 2, :], cpos[:, 1, :], 2.0, None, ALU.add))
                settle()
                step(dve.reciprocal(cpos[:, 3, :], cpos[:, 2, :]))
                settle()
                step(dve.tensor_tensor(cpos[:, 1, :], cpos[:, 1, :], cpos[:, 3, :], ALU.mult))
                settle()
                step(dve.tensor_tensor(cpos[:, 2, :], cpos[:, 1, :], cpos[:, 1, :], ALU.mult))
                settle()
                step(dve.tensor_scalar(cpos[:, 3, :], cpos[:, 2, :], 1.0 / 17, None, ALU.mult))
                settle()
                for odd in (15, 13, 11, 9, 7, 5, 3):
                    step(dve.scalar_tensor_tensor(cpos[:, 3, :], cpos[:, 3, :], 1.0 / odd, cpos[:, 2, :], ALU.add, ALU.mult))
                    settle()
                step(dve.scalar_tensor_tensor(cpos[:, 3, :], cpos[:, 3, :], 1.0, cpos[:, 1, :], ALU.add, ALU.mult))
                step(dve.tensor_scalar(cpos[:, 0, :], lru_c[:, 3, :], -1.0, 0.0, ALU.mult, ALU.max))
                settle()
                step(dve.scalar_tensor_tensor(cpos[:, 2, :], cpos[:, 3, :], 2.0, cpos[:, 0, :], ALU.mult, ALU.add))
                settle()
                dve.tensor_scalar(cpos[:, 4, :], cpos[:, 2, :], 8.0, None, ALU.mult).then_inc(cpos_ready, 1)
                dve.tensor_scalar(cpos[:, 5, :], cpos[:, 2, :], -8.0, None, ALU.mult).then_inc(cpos_ready, 1)
                step(dve.tensor_tensor(lbt[:, 2], lbt[:, 1], lbt[:, 0], ALU.subtract))
                settle()
                dve.scalar_tensor_tensor(lbt[:, 3], lbt[:, 2], -1.0, lbt[:, 2], ALU.mult, ALU.max).then_inc(lb_in, 1)
                dve.wait_ge(lb_out, 3)
                step(dve.scalar_tensor_tensor(lbt[:, 7], lbt[:, 2], 0.0, lbt[:, 5], ALU.min, ALU.subtract))
                step(dve.tensor_scalar(lbt[:, 8], lbt[:, 2], -1.0, 0.0, ALU.mult, ALU.min))
                settle()
                step(dve.tensor_tensor(lbt[:, 9], lbt[:, 8], lbt[:, 5], ALU.subtract))
                settle()

            dve.wait_ge(x_loaded, 16)
            for t in range(T):
                dve.memset(stat[:, 12 + t:13 + t], 0.0).then_inc(h_ready, 1)
            settle()

            n = 0
            for stage, nxt in zip(plan, plan[1:] + [("end",)]):
                kind = stage[0]
                if kind == "norm":
                    split_to(n - 1)
                    norm_rows(xn)
                    for t in range(T):
                        piece(*norm_piece(t))
                if kind == "rescale":
                    split_to(n - 1)
                    norm_rows(h)
                    dve.wait_ge(xn_ready, 2 * st["norm"])
                    for t in range(T):
                        dve.memset(stat[:, 12 + t:13 + t], 0.0).then_inc(h_ready, 1)
                    st["updates"] += 1
                if kind == "pool":
                    split_to(n - 1)
                    norm_rows(xn)
                    for t in range(T):
                        piece(*pool_piece(t))
                    split_to(n)
                    n += 1
                    dve.wait_ge(block_used, n)
                    dve.wait_ge(pool_loaded, 48)
                    for t in range(T):
                        y = xn[:, t, :]
                        step(dve.tensor_tensor(y, span(psD[:, 2 * t:2 * t + 2, :]), view(POOL_B, D), ALU.add))
                        settle()
                        step(dve.tensor_tensor(y, y, view(POOL_S, D), ALU.mult))
                        settle()
                        dve.tensor_tensor(h[:, t, :], h[:, t, :], y, ALU.add).then_inc(h_ready, 1)
                    st["updates"] += 1
                if kind == "ffn":
                    def gated(c_at, c):
                        dve.wait_ge(silu_ready, c_at)
                        dve.tensor_tensor(prod[:, c % 2, :], sil[:, c % 2, :], psA[:, 2 + c % 2, :], ALU.mult).then_inc(prod_ready, 1)
                        dve.wait_ge(prod_hi_ready, c_at)
                        dve.tensor_tensor(span(prod_lo[:, c % 2]), prod[:, c % 2, :], span(prod_hi[:, c % 2]).bitcast(F32), ALU.subtract).then_inc(prod_lo_ready, 1)

                    c0 = st["ffn"] * CH
                    for b in range(5):
                        split_to(n)
                        if b in (1, 3):
                            gated(c0 + b // 2 + 1, b // 2)
                        n += 1
                    with dve.Fori(0, (CH - 3) // 2) as j:
                        for b in range(6):
                            split(6 * j + (n + b + AHEAD + 1), n + b + AHEAD)
                            if b % 3 == 1:
                                gated(2 * j + (c0 + 3 + b // 3), b // 3)
                    n += 3 * (CH - 3)
                    st["split"] += 3 * (CH - 3)
                    for b in range(4):
                        split_to(n)
                        if b == 1:
                            gated(c0 + CH, CH - 1)
                        if b == 2 and nxt[0] == "ple":
                            piece(*ple_piece())
                        if b == 2 and st["ffn"] == 0:
                            constants()
                        n += 1
                    for t in range(T):
                        summed(t, n)
                        dve.scalar_tensor_tensor(h[:, t, :], span(psD[:, 2 * t:2 * t + 2, :]), stage[4], h[:, t, :],
                                                 ALU.mult, ALU.add).then_inc(h_ready, 1)
                    st["ffn"] += 1
                    st["updates"] += 1
                if kind == "lru":
                    half = R // FC
                    xb, xc = view(L_XB, RT, S + 3), view(L_XC, RT, S)
                    r, ig, th = view(L_R, RT, S), view(L_IG, RT, S), view(L_T, GT, S)
                    gelu, ratio = view(L_GELU, RT, S), view(L_XB, RT, S)

                    step(dve.memset(xb[:, :, 0:3], 0.0))
                    settle()

                    def convolve(i):
                        dve.wait_ge(xb_ready, i + 1)
                        fts = (2 * i, 2 * i + 1)
                        for ft in fts:
                            step(dve.tensor_scalar(xc[:, ft, :], xb[:, ft, 0:S], conv_w[:, 0, ft:ft + 1], lru_c[:, 0, ft:ft + 1], ALU.mult, ALU.add))
                        for k in range(1, 4):
                            settle()
                            for ft in fts:
                                ins = dve.scalar_tensor_tensor(xc[:, ft, :], xb[:, ft, k:k + S], conv_w[:, k, ft:ft + 1], xc[:, ft, :], ALU.mult, ALU.add)
                                if k < 3:
                                    step(ins)
                                else:
                                    ins.then_inc(xc_ready, 1)

                    def ratios(g):
                        v, t_ = ratio[:, g * GT:(g + 1) * GT, :], th[:, :, :]
                        dve.wait_ge(tanh_ready, GT * (g + 1))
                        step(dve.tensor_scalar(v, t_, 1.0, None, ALU.add))
                        settle()
                        step(dve.reciprocal(v, v))
                        settle()
                        dve.tensor_tensor(v, v, t_, ALU.mult).then_inc(ratio_ready, 1)
                        gs = slice(g * GT, (g + 1) * GT)
                        dve.wait_ge(gates_ready, 2 * GT * (g + 1))
                        step(dve.tensor_tensor(ig[:, gs, :], ig[:, gs, :], xc[:, gs, :], ALU.mult))

                    def recur(g):
                        gs = slice(g * GT, (g + 1) * GT)
                        dve.wait_ge(mult_ready, g + 1)
                        settle()
                        step(dve.tensor_tensor(ig[:, gs, :], ig[:, gs, :], ratio[:, gs, :], ALU.mult))
                        settle()
                        dve.wait_ge(decay_ready, GT * (g + 1))
                        for ft in range(g * GT, (g + 1) * GT):
                            step(dve.tensor_tensor_scan(ig[:, ft, :], r[:, ft, :], ig[:, ft, :], 0.0, ALU.mult, ALU.add))
                        settle()

                    for i in range(2 * half):
                        split_to(n)
                        if i < half:
                            convolve(i)
                        if i in (half, half + 1):
                            ratios(i - half)
                        if i in (half + 2, half + 3):
                            recur(i - half - 2)
                        n += 1
                    dve.wait_ge(gelu_ready, half)
                    for g in range(2):
                        gs = slice(g * GT, (g + 1) * GT)
                        dve.tensor_tensor(xc[:, gs, :], ig[:, gs, :], gelu[:, gs, :], ALU.mult).then_inc(y_ready, 1)
                    for g in range(2):
                        gs = slice(g * GT, (g + 1) * GT)
                        piece(xc[:, gs, :], (gs, slice(0, S)))
                    for i in range(R // (2 * P)):
                        split_to(n)
                        n += 1
                    for t in range(T):
                        summed(t, n)
                        dve.tensor_tensor(h[:, t, :], span(psD[:, 2 * t:2 * t + 2, :]), h[:, t, :], ALU.add).then_inc(h_ready, 1)
                    st["updates"] += 1
                if kind == "ple":
                    split_to(n)
                    norm_rows(xn)
                    for t in range(T):
                        piece(*merge_piece(t))
                    for i in range(KT // 2 + 1):
                        split_to(n)
                        n += 1
                    sig = view(SIG, T, D)
                    st["rows"] += 1
                    for t in range(T):
                        dve.wait_ge(sig_ready, 2 * stage[2] + t + 1)
                        step(dve.tensor_tensor(sig[:, t, :], sig[:, t, :], span(psA[:, 2 * t:2 * t + 2, :]), ALU.mult))
                        settle()
                        dve.tensor_tensor(h[:, t, :], h[:, t, :], sig[:, t, :], ALU.add).then_inc(h_ready, 1)
                    st["updates"] += 1
                if kind == "mix":
                    l = stage[1]
                    HS = HEADS * S
                    z2, tmp2, e2, kk2 = (view(at, 2 * HS) for at in (Z, TMP, LOGF, KK))
                    bf, bb = view(Z, HS), view(Z + HS, HS)
                    near = view(XN, 8, P)
                    pairs = psD[:, 0:2, :].rearrange("p b (e s) -> p (b e) s", s=P)
                    heads = lambda v, d: [v[:, d * HS + c * S:d * HS + (c + 1) * S] for c in range(HEADS)]

                    def log_sigmoid(d):
                        ds = slice(d * HS, (d + 1) * HS)
                        dve.wait_ge(soft_ready, (2 * d + 1) if l == 0 and d == 0 else (SOFTS[0] + 2 * d + 1 if l else d + 1))
                        step(dve.scalar_tensor_tensor(e2[:, ds], z2[:, ds], 0.0, tmp2[:, ds], ALU.min, ALU.subtract))
                        settle()
                        if l:
                            for c, v in enumerate(heads(e2, d)):
                                step(dve.tensor_scalar(v, v, lbt[:, 9, d, c:c + 1], None, ALU.add))
                            settle()
                            for c, (v, w) in enumerate(zip(heads(e2, d), heads(tmp2, d))):
                                step(dve.tensor_scalar(w, v, lbt[:, 7, d, c:c + 1], None, ALU.subtract))
                            settle()
                            dve.memset(stat[:, 14:15], 0.0).then_inc(gap_ready, 1)
                            for c, v in enumerate(heads(e2, d)):
                                step(dve.tensor_scalar(v, v, lbt[:, 7, d, c:c + 1], None, ALU.max))
                            settle()

                    def sums(d):
                        ds = slice(d * HS, (d + 1) * HS)
                        if l:
                            dve.wait_ge(soft_ready, SOFTS[0] + 2 * d + 2)
                            step(dve.tensor_tensor(e2[:, ds], e2[:, ds], tmp2[:, ds], ALU.add))
                            settle()
                        dve.wait_ge(kk_ready, 2 * l + d + 1)
                        if l:
                            for c, v in enumerate(heads(kk2, d)):
                                step(dve.tensor_scalar(v, v, lbt[:, 6, d, c:c + 1], None, ALU.mult))
                        way = slice(None, None, -1 if d else 1)
                        for c in range(2 * HEADS):
                            f = slice(d * HS + c * P, d * HS + (c + 1) * P)
                            step(dve.tensor_tensor_scan(z2[:, f][:, way], one_row[:], e2[:, f][:, way], 0.0, ALU.mult, ALU.add))
                        settle()

                    def diagonal():
                        dve.tensor_tensor(tmp2[:, HS:2 * HS], kk2[:, 0:HS], kk2[:, HS:2 * HS], ALU.add).then_inc(scaled_ready, 1)

                    def exponents(i):
                        m = LEVELS[i]
                        eq, ek, f, b = (halves(v, m) for v in (e2[:, 0:HS], e2[:, HS:2 * HS], bf, bb))
                        nb = HS // (2 * m)
                        f_end = f[:, :, 0, m - 1:m].broadcast_to([P, nb, m])
                        b_end = b[:, :, 1, 0:1].broadcast_to([P, nb, m])
                        if m == P:
                            step(dve.tensor_copy(eq[:, :, 1, :], f[:, :, 1, :]))
                            step(dve.tensor_copy(eq[:, :, 0, :], b[:, :, 0, :]))
                        else:
                            step(dve.tensor_tensor(eq[:, :, 1, :], f[:, :, 1, :], f_end, ALU.subtract))
                            step(dve.tensor_tensor(eq[:, :, 0, :], b[:, :, 0, :], b_end, ALU.subtract))
                        step(dve.tensor_tensor(ek[:, :, 0, :], f_end, f[:, :, 0, :], ALU.subtract))
                        step(dve.tensor_tensor(ek[:, :, 1, :], b_end, b[:, :, 1, :], ALU.subtract))
                        settle()
                        dve.memset(stat[:, 14:15], 0.0).then_inc(decay_in, 1)

                    def scaled(i):
                        m = LEVELS[i]
                        dve.wait_ge(decay_out, NL * l + i + 1)
                        dve.wait_ge(pair_done, (NL + 1) * l + i + 1)
                        step(dve.tensor_tensor(tmp2[:, 0:HS], view(Q_B, HS), e2[:, 0:HS], ALU.mult))
                        ek, kf, kb, to = (halves(v, m) for v in (e2[:, HS:2 * HS], kk2[:, 0:HS], kk2[:, HS:2 * HS], tmp2[:, HS:2 * HS]))
                        step(dve.tensor_tensor(to[:, :, 0, :], kf[:, :, 0, :], ek[:, :, 0, :], ALU.mult))
                        step(dve.tensor_tensor(to[:, :, 1, :], kb[:, :, 1, :], ek[:, :, 1, :], ALU.mult))
                        settle()
                        dve.memset(stat[:, 15:16], 0.0).then_inc(scaled_ready, 1)

                    def take(i):
                        dve.wait_ge(pair_done, (NL + 1) * l + i + 2)
                        dve.copy_predicated(near, level_mask[:, i, :].unsqueeze(1).broadcast_to([P, 8, P]), pairs).then_inc(pair_taken, 1)

                    def rotate(e):
                        dve.wait_ge(proj_evac, NP * l + 8 + 2 * e)
                        dve.wait_ge(rope_ready, 2)
                        x4 = view(A_QK + 1024 * e, T, 8, 64)
                        x1, x2 = x4[:, :, :, 0:ROT], x4[:, :, :, ROT:2 * ROT]
                        sin, cos = (rope[:, j, :, :].unsqueeze(2).broadcast_to([P, T, 8, ROT]) for j in (0, 1))
                        u, v, w, y = (view(ATT + 128 * j, T, 8, ROT) for j in range(4))
                        step(dve.tensor_tensor(u, x1, cos, ALU.mult))
                        step(dve.tensor_tensor(v, x2, sin, ALU.mult))
                        step(dve.tensor_tensor(w, x2, cos, ALU.mult))
                        step(dve.tensor_tensor(y, x1, sin, ALU.mult))
                        settle()
                        dve.tensor_tensor(x1, u, v, ALU.subtract).then_inc(roped, 1)
                        dve.tensor_tensor(x2, w, y, ALU.add).then_inc(roped, 1)

                    def mix_lambda_in():
                        dve.wait_ge(mix_loaded, 48 * (l + 1))
                        lam = view(LAM, 4, 64)
                        for e in range(2):
                            step(dve.tensor_tensor(lam[:, 2 * e, :], lam[:, 2 * e, :], lam[:, 2 * e + 1, :], ALU.mult))
                        settle()
                        for e in range(2):
                            step(dve.tensor_reduce(stat[:, 40 + e:41 + e], lam[:, 2 * e, :], AX_X, ALU.add))
                        settle()
                        dve.memset(stat[:, 14:15], 0.0).then_inc(lam_in, 1)

                    def mix_lambda_out():
                        dve.wait_ge(lam_exp, l + 1)
                        step(dve.scalar_tensor_tensor(stat[:, 44:45], stat[:, 42:43], LAM_INIT[l], stat[:, 43:44], ALU.add, ALU.subtract))
                        settle()
                        step(dve.tensor_scalar(stat[:, 45:46], stat[:, 44:45], -1.0, None, ALU.mult))
                        settle()

                    prob, w_att = view(PROB, 4, S), view(W_ATT, 2, S)

                    def maxima(u):
                        k = UNITS * l + u
                        dve.wait_ge(scores_done, k + 1)
                        step(dve.tensor_reduce(stat[:, 64:68], psA[:, 2:4, :].rearrange("p b (e s) -> p (b e) s", s=S), AX_X, ALU.max))
                        settle()
                        dve.tensor_scalar(stat[:, 48:52], stat[:, 64:68], -0.125, None, ALU.mult).then_inc(max_ready, 1)

                    def attention_weights(u):
                        k = UNITS * l + u
                        dve.wait_ge(exp_ready, 4 * (k + 1))
                        step(dve.reciprocal(stat[:, 68:72], stat[:, 56:60]))
                        settle()
                        step(dve.tensor_scalar(stat[:, 72:74], stat[:, 70:72], stat[:, 45:46], None, ALU.mult))
                        if k:
                            dve.wait_ge(w_turned, k)
                        for hh in range(2):
                            step(dve.tensor_scalar(w_att[:, hh, :], prob[:, hh, :], stat[:, 68 + hh:69 + hh], None, ALU.mult))
                        settle()
                        for hh in range(2):
                            dve.scalar_tensor_tensor(w_att[:, hh, :], prob[:, 2 + hh, :], stat[:, 72 + hh:73 + hh], w_att[:, hh, :],
                                                     ALU.mult, ALU.add).then_inc(w_ready, 1)

                    for i, (c, first) in enumerate(PROJ):
                        split_to(n)
                        n += 1
                        if i in (2, 4):
                            log_sigmoid(i // 2 - 1)
                        if i in (3, 5):
                            sums(i // 2 - 1)
                        if i == 6:
                            diagonal()
                        if i in (8, 10):
                            rotate((i - 8) // 2)
                        if i == 9:
                            mix_lambda_in()
                        if i == 11:
                            mix_lambda_out()
                        for u in range(UNITS):
                            if i == 12 + 2 * u:
                                maxima(u)
                            if i == 13 + 2 * u:
                                attention_weights(u)
                        if i % 2 == 0 and 0 <= (i - 6) // 2 < NL:
                            exponents((i - 6) // 2)
                        if i % 2 == 1 and 0 <= (i - 7) // 2 < NL:
                            if i >= 11:
                                take((i - 7) // 2 - 1)
                            scaled((i - 7) // 2)
                        if i == 22:
                            att = view(ATT, T * 512)
                            head_norm(att, tmp_att, att_square, l + 1, att_sum, att_rms, NRM_DA, 1.0 - LAM_INIT[l], att).then_inc(att_ready, 1)
                    take(NL - 1)
                    piece(*att_piece())
                    split_to(n)
                    rec, o = view(LOGF, T * 512), span(psD[:, 0:2, :])
                    step(head_norm(o, tmp2[:, 0:T * 512], rec_square, l + 1, rec_sum, rec_rms, NRM_HG, 0.5, rec))
                    settle()
                    dve.scalar_tensor_tensor(rec, view(G_B, T * 512), 1.0, rec, ALU.add, ALU.mult).then_inc(rec_ready, 1)
                    split_to(n + 1)
                    piece(*rec_piece())
                    for i in range(4):
                        split_to(n)
                        n += 1
                    mrg, ga, gb = xn, view(GATE_A, T, D), view(GATE_B, T, D)
                    dve.wait_ge(proj_evac, NP * (l + 1))
                    dve.wait_ge(block_used, n - 2)
                    for t in range(T):
                        step(dve.scalar_tensor_tensor(mrg[:, t, :], ga[:, t, :], 1.0, span(psA[:, 2 * t:2 * t + 2, :]), ALU.add, ALU.mult))
                    for t in range(T):
                        if t == 0:
                            st["rows"] += 2
                            dve.wait_ge(rows_done, st["rows"])
                        else:
                            dve.wait_ge(block_used, n)
                        step(dve.scalar_tensor_tensor(gb[:, t, :], gb[:, t, :], 1.0, span(psD[:, 2 * t:2 * t + 2, :]), ALU.add, ALU.mult))
                        settle()
                        dve.tensor_tensor(mrg[:, t, :], mrg[:, t, :], gb[:, t, :], ALU.add).then_inc(merged, 1)
                    for t in range(T):
                        piece(*merge_piece(t))
                    for i in range(4):
                        split_to(n)
                        n += 1
                    for t in range(T):
                        summed(t, n)
                        dve.scalar_tensor_tensor(h[:, t, :], span(psA[:, 2 * t:2 * t + 2, :]), 0.5, h[:, t, :], ALU.mult, ALU.add).then_inc(h_ready, 1)
                    st["updates"] += 1

        @block.tensor
        def _(pe):
            st = {"norm": 0, "piece": 0, "ffn": 0}

            def features(n_at, n, to, ready=None):
                pe.wait_ge(lo_ready, n_at)
                w_hi = hi[:, n % RING, :].rearrange("p (k f) -> p k f", f=FC)
                w_lo = lo[:, n % RING, :].rearrange("p (k f) -> p k f", f=FC)
                for f in range(2):
                    fs = slice(f * P, (f + 1) * P)
                    for k in range(KT):
                        for e, (w, x) in enumerate(((w_hi, xTh), (w_hi, xTl), (w_lo, xTh))):
                            last = pe.matmul(to[:, f * S:(f + 1) * S], w[:, k, fs], x[:, k, :], start=(k == 0 and e == 0),
                                             stop=(k == KT - 1 and e == 2))
                last.then_inc(block_used, 1)

            def tokens(n_at, n, to):
                pe.wait_ge(lo_ready, n_at)
                w_hi = hi[:, n % RING, :].rearrange("p (k f) -> p k f", f=FC)
                w_lo = lo[:, n % RING, :].rearrange("p (k f) -> p k f", f=FC)
                for t in range(T):
                    ts = slice(t * P, (t + 1) * P)
                    for k in range(KT):
                        for e, (x, w) in enumerate(((xTh, w_hi), (xTh, w_lo), (xTl, w_hi))):
                            last = pe.matmul(to[:, t * FC:(t + 1) * FC], x[:, k, ts], w[:, k, :], start=(k == 0 and e == 0),
                                             stop=(k == KT - 1 and e == 2))
                last.then_inc(block_used, 1)

            def contract(n_at, n, x_hi, x_lo, to, first, final, signal=True):
                pe.wait_ge(lo_ready, n_at)
                w_hi = hi[:, n % RING, :].rearrange("p (k f) -> p k f", f=D)
                w_lo = lo[:, n % RING, :].rearrange("p (k f) -> p k f", f=D)
                for t in range(T):
                    ts = slice(t * P, (t + 1) * P)
                    for k in range(2):
                        for e, (x, w) in enumerate(((x_hi, w_hi), (x_hi, w_lo), (x_lo, w_hi))):
                            for c in range(2):
                                last = pe.matmul(to[:, 2 * t + c, :], x[:, k, ts], w[:, k, c * 512:(c + 1) * 512],
                                                 start=(first and k == 0 and e == 0), stop=(final and k == 1 and e == 2))
                    if final and signal and t == 0:
                        last.then_inc(rows_done, 1)
                last.then_inc(block_used, 1)

            def xT_pieces(k):
                st["piece"] += k
                pe.wait_ge(xT_ready, st["piece"])

            def turn(to, rows_, k, t):
                return pe.transpose(to, rows_[:, t, k * P:(k + 1) * P], ident[:])

            def turn_norm(ps):
                for t in range(T):
                    pe.wait_ge(xn_ready, 2 * st["norm"] + t + 1)
                    for k in range(KT):
                        last = turn(ps[:, 2 * t + k // 4, (k % 4) * P:(k % 4 + 1) * P], xn, k, t)
                    last.then_inc(turned, 1)
                st["norm"] += 1
                xT_pieces(T)

            pe.wait_ge(ident_loaded, 16)
            n = 0
            for stage, nxt in zip(plan, plan[1:] + [("end",)]):
                kind = stage[0]
                if kind == "norm":
                    turn_norm(psA)
                if kind == "rescale":
                    st["norm"] += 1
                if kind == "pool":
                    mean = view(POOL_M, T, 4, S)
                    pe.wait_ge(pool_loaded, 48)
                    pe.wait_ge(xn_ready, 2 * st["norm"] + 2)
                    for k in range(KT):
                        to = psA[:, k // 2, (k % 2) * S:(k % 2 + 1) * S]
                        pe.matmul(to, xn[:, 0, k * P:(k + 1) * P], mean[:, 0, k // 2, :], start=True, stop=False)
                        last = pe.matmul(to[:, P:S], xn[:, 1, k * P:(k + 1) * P], mean[:, 1, k // 2, P:S], start=False, stop=True)
                        if k % 4 == 3:
                            last.then_inc(turned, 1)
                    st["norm"] += 1
                    xT_pieces(T)
                    pe.wait_ge(lo_ready, n + 1)
                    w_hi, w_lo = (v[:, n % RING, :].rearrange("p (k f) -> p k f", f=FC) for v in (hi, lo))
                    for t in range(T):
                        for g in range(4):
                            to = psD[:, 2 * t + g // 2, (g % 2) * FC:(g % 2 + 1) * FC]
                            for k in range(2):
                                for e, (x, w) in enumerate(((xTh, w_hi), (xTh, w_lo), (xTl, w_hi))):
                                    last = pe.matmul(to, x[:, 2 * g + k, t * P:(t + 1) * P], w[:, 2 * g + k, :],
                                                     start=(k == 0 and e == 0), stop=(k == 1 and e == 2))
                    last.then_inc(block_used, 1)
                    n += 1
                if kind == "ffn":
                    c0 = st["ffn"] * CH

                    def down(n_at, n, c_at, c, first=False, final=False):
                        pe.wait_ge(prod_lo_ready, c_at)
                        contract(n_at, n, prod_hi[:, c % 2], prod_lo[:, c % 2], psD, first, final)

                    features(n + 1, n, psA[:, 0, :])
                    features(n + 2, n + 1, psA[:, 2, :])
                    features(n + 3, n + 2, psA[:, 1, :])
                    features(n + 4, n + 3, psA[:, 3, :])
                    down(n + 5, n + 4, c0 + 1, 0, first=True)
                    n += 5
                    with pe.Fori(0, (CH - 3) // 2) as j:
                        for e in range(2):
                            pe.wait_ge(prod_ready, 2 * j + (c0 + e + 1))
                            features(6 * j + (n + 3 * e + 1), n + 3 * e, psA[:, e, :])
                            features(6 * j + (n + 3 * e + 2), n + 3 * e + 1, psA[:, 2 + e, :])
                            down(6 * j + (n + 3 * e + 3), n + 3 * e + 2, 2 * j + (c0 + e + 2), 1 + e)
                    n += 3 * (CH - 3)
                    pe.wait_ge(prod_ready, c0 + CH - 2)
                    features(n + 1, n, psA[:, 0, :])
                    features(n + 2, n + 1, psA[:, 2, :])
                    down(n + 3, n + 2, c0 + CH - 1, CH - 2)
                    if nxt[0] == "ple":
                        pe.wait_ge(p_loaded, 16 * (nxt[2] + 1))
                        for t in range(T):
                            for k in range(2):
                                last = turn(psA[:, 1, k * S + t * P:k * S + (t + 1) * P], view(PTOK, T, S), k, t)
                        last.then_inc(turned, 1)
                    down(n + 4, n + 3, c0 + CH, CH - 1, final=True)
                    n += 4
                    st["ffn"] += 1
                if kind == "lru":
                    half = R // FC
                    band, xc = view(BAND, 2, 2, GT, 384), view(L_XC, RT, S)

                    def recurrent_gates(g):
                        pe.wait_ge(xc_ready, GT * (g + 1))
                        for m in range(GT):
                            ft = g * GT + m
                            if ft >= 4:
                                pe.wait_ge(gates_ready, 2 * (ft - 3))
                            for e in range(2):
                                ks = [k for k in (m - 1, m, m + 1) if 0 <= k < GT]
                                for k in ks:
                                    last = pe.matmul(psD[:, ft % 4, e * S:(e + 1) * S], band[:, e, g, k, (m - k + 1) * P:(m - k + 2) * P],
                                                     xc[:, g * GT + k, :], start=(k == ks[0]), stop=(k == ks[-1]))
                            last.then_inc(gates_done, 1)

                    for i in range(2 * half):
                        if 4 <= i < 4 + half:
                            pe.wait_ge(xb_ready, i - 3)
                        elif i >= 4 + half:
                            pe.wait_ge(gelu_ready, i - 3 - half)
                        features(n + 1, n, psA[:, i % 4, :])
                        n += 1
                        if i == half:
                            pe.wait_ge(band_loaded, 16 * 2 * 2 * len(head_pieces()))
                            recurrent_gates(0)
                        if i == half + 1:
                            recurrent_gates(1)
                    xT_pieces(2)
                    nk = R // (2 * P)
                    for i in range(nk):
                        contract(n + 1, n, xTh[:, 2 * i:2 * i + 2], xTl[:, 2 * i:2 * i + 2], psD, i == 0, i == nk - 1)
                        n += 1
                if kind == "ple":
                    xT_pieces(1)
                    contract(n + 1, n, xTh[:, 8:10], xTl[:, 8:10], psA, True, True, signal=False)
                    n += 1
                    turn_norm(psD)
                    for i in range(KT // 2):
                        contract(n + 1, n, xTh[:, 2 * i:2 * i + 2], xTl[:, 2 * i:2 * i + 2], psD, i == 0, i == KT // 2 - 1)
                        n += 1
                if kind == "mix":
                    l = stage[1]
                    HS = HEADS * S
                    tmp2, q_b, v_b, v_a = view(TMP, 2, HEADS, S), view(Q_B, HEADS, S), view(V_B, T, 512), view(A_V, T, 512)
                    near, cross = view(XN, 8, P), view(XN + 1024, 8, P)
                    qkT, w_att, wT = view(QK_T, 2, HEADS, S), view(W_ATT, 2, S), view(W_T, 2, T, P)

                    def pair(i):
                        k0 = (NL + 1) * l
                        pe.wait_ge(scaled_ready, k0 + i + 2)
                        if i >= 0:
                            pe.wait_ge(pair_taken, k0 + i + 1)
                        q = q_b if i < 0 else tmp2[:, 0]
                        ps = psD[:, 0:2, :].rearrange("p b (e s) -> p (b e) s", s=P)
                        for hh in range(HEADS):
                            for e in range(T):
                                te = 1 - e if i >= 0 and LEVELS[i] == P else e
                                last = pe.matmul(ps[:, 2 * hh + e, :], tmp2[:, 1, hh, e * P:(e + 1) * P], q[:, hh, te * P:(te + 1) * P],
                                                 start=True, stop=True)
                        last.then_inc(pair_done, 1)

                    def turn_heads(e):
                        pe.wait_ge(roped, 4 * l + 2 * e + 2)
                        if e:
                            pe.wait_ge(qkT_ready, 2 * l + 1)
                        for t in range(T):
                            for hh in range(HEADS):
                                last = turn(psA[:, 2 + hh // 2, (hh % 2) * S + t * P:(hh % 2) * S + (t + 1) * P], view(A_QK + 1024 * e, T, 512), hh, t)
                        last.then_inc(qk_turned, 1)

                    def scores(u):
                        t, k = u // 2, UNITS * l + u
                        pe.wait_ge(qkT_ready, 2 * l + 2)
                        if u:
                            pe.wait_ge(exp_ready, 4 * k)
                        for e in range(2):
                            cs = slice(64 * e, 64 * e + 64)
                            for j in range(2):
                                hh = 2 * (u % 2) + j
                                last = pe.matmul(psA[:, 2 + e, j * S:(j + 1) * S], qkT[cs, 0, hh, t * P:(t + 1) * P], qkT[cs, 1, hh, :],
                                                 start=True, stop=True)
                        last.then_inc(scores_done, 1)

                    def turn_weights(u):
                        k = UNITS * l + u
                        pe.wait_ge(w_ready, 2 * (k + 1))
                        if k:
                            pe.wait_ge(wT_ready, k)
                        for j in range(2):
                            for e in range(T):
                                last = turn(psD[:, 2, (T * j + e) * P:(T * j + e + 1) * P], w_att, e, j)
                        last.then_inc(w_turned, 1)

                    def attend(u):
                        k = UNITS * l + u
                        pe.wait_ge(wT_ready, k + 1)
                        if k:
                            pe.wait_ge(att_rows, k)
                        for j in range(2):
                            hh = 2 * (u % 2) + j
                            for e in range(T):
                                last = pe.matmul(psD[:, 3, j * P:(j + 1) * P], wT[:, j, e, :], v_a[:, e, hh * P:(hh + 1) * P],
                                                 start=(e == 0), stop=(e == T - 1))
                        last.then_inc(att_done, 1)

                    for i, (c, first) in enumerate(PROJ):
                        if i >= 2:
                            pe.wait_ge(proj_evac, NP * l + i - 1)
                        (features if first in (FF, FB, QB) else tokens)(n + 1, n, psA[:, i % 2, :])
                        n += 1
                        if i % 2 == 0 and 0 <= (i - 6) // 2 <= NL:
                            pair((i - 6) // 2 - 1)
                        if i in (8, 10):
                            turn_heads((i - 8) // 2)
                        for u in range(UNITS):
                            if i == 11 + 2 * u:
                                scores(u)
                            if i == 13 + 2 * u:
                                turn_weights(u)
                            if i == 14 + 2 * u:
                                attend(u)
                    pe.wait_ge(att_ready, l + 1)
                    for t in range(T):
                        for k in range(HEADS):
                            last = turn(psA[:, 2 + k // 2, (k % 2) * S + t * P:(k % 2) * S + (t + 1) * P], view(ATT, T, 512), k, t)
                    last.then_inc(turned, 1)
                    pe.wait_ge(pair_taken, (NL + 1) * (l + 1))
                    for t in range(T):
                        for hh in range(HEADS):
                            to = psD[:, t, hh * P:(hh + 1) * P]
                            pe.matmul(to, near[:, 2 * hh + t, :], v_b[:, t, hh * P:(hh + 1) * P], start=True, stop=False)
                            last = pe.matmul(to, cross[:, 2 * hh + 1 - t, :], v_b[:, 1 - t, hh * P:(hh + 1) * P], start=False, stop=True)
                    last.then_inc(rec_done, 1)
                    xT_pieces(1)
                    pe.wait_ge(proj_evac, NP * (l + 1))
                    for i in range(2):
                        contract(n + 1, n, x_att[0][:, 2 * i:2 * i + 2], x_att[1][:, 2 * i:2 * i + 2], psA, i == 0, i == 1)
                        n += 1
                    pe.wait_ge(rec_ready, l + 1)
                    for t in range(T):
                        for k in range(HEADS):
                            last = turn(psD[:, k // 2, (k % 2) * S + t * P:(k % 2) * S + (t + 1) * P], view(LOGF, T, 512), k, t)
                    last.then_inc(turned, 1)
                    xT_pieces(1)
                    for i in range(2):
                        contract(n + 1, n, xTh[:, 4 + 2 * i:6 + 2 * i], xTl[:, 4 + 2 * i:6 + 2 * i], psD, i == 0, i == 1)
                        n += 1
                    for t in range(T):
                        pe.wait_ge(merged, T * l + t + 1)
                        for k in range(KT):
                            last = turn(psD[:, 2 * t + k // 4, (k % 4) * P:(k % 4 + 1) * P], xn, k, t)
                        last.then_inc(turned, 1)
                    xT_pieces(T)
                    for i in range(KT // 2):
                        contract(n + 1, n, xTh[:, 2 * i:2 * i + 2], xTl[:, 2 * i:2 * i + 2], psA, i == 0, i == KT // 2 - 1)
                        n += 1
            assert n == TOTAL


_INS = ["x", "p", "ffn1_norm", "ffn1_w_gate", "ffn1_w_up", "ffn1_w_down", "mix_norm", "lru_w_in", "lru_conv_w", "lru_conv_b",
        "lru_w_a", "lru_b_a", "lru_w_x", "lru_b_x", "lru_a_param", "lru_w_out", "pool_w", "pool_b", "pool_scale", "ffn2_norm",
        "ffn2_w_gate", "ffn2_w_up", "ffn2_w_down", "ple_norm", "ple_w_gate", "ple_w_proj", "final_norm", "positions_2", "w_in_2",
        "da_lambda_2", "da_norm_2", "hg_lb_logits_2", "hg_norm_2", "w_a_2", "w_b_2", "w_o_2", "attn_norm_2", "ffn_norm_2",
        "w_gate_2", "w_up_2", "w_down_2", "final_norm_2"]


def shape_constants():
    i = np.arange(P)
    level = np.zeros((P, len(LEVELS), P), np.int32)
    for e, m in enumerate(LEVELS):
        level[:, e, :] = (i[:, None] // m != i[None, :] // m) & (i[:, None] // (2 * m) == i[None, :] // (2 * m))
    pool = np.zeros((P, T, len(POOL_WINDOWS), S), np.float32)
    s = np.arange(S)
    for t in range(T):
        tok = t * P + i[:, None]
        for g, win in enumerate(POOL_WINDOWS):
            inside = (tok <= s[None, :]) & (tok > s[None, :] - win)
            pool[:, t, g, :] = inside / np.minimum(s[None, :] + 1, win).astype(np.float32) - (tok == s[None, :])
    freq = np.float32(500000.0) ** (-(np.arange(0, 2 * ROT, 2, dtype=np.float32) / np.float32(2 * ROT)))
    freq = np.tile(np.concatenate([freq, freq]).astype(np.float32), (P, 1))
    return {"c_ident": np.eye(P, dtype=np.float32), "c_level": level, "c_pool": pool, "c_freq": freq}


def kernel(**inputs):
    import concourse.bacc as bacc
    from concourse.bass_utils import run_bass_kernel_spmd

    nc = bacc.Bacc("TRN2", target_bir_lowering=False, num_devices=1)
    arrays, aps = {}, {}
    for name, v in [(k, inputs[k]) for k in _INS] + list(shape_constants().items()):
        v = np.ascontiguousarray(v)
        arrays[f"in_{name}"] = v
        aps[name] = nc.dram_tensor(f"in_{name}", v.shape, mybir.dt.from_np(v.dtype), kind="ExternalInput").ap()
    out = nc.dram_tensor("out_0", (1, S, D), F32, kind="ExternalOutput").ap()
    build(nc, aps, out)
    r = run_bass_kernel_spmd(nc, [arrays], core_ids=[0])
    return r.results[0]["out_0"]
```

```python
from contextlib import ExitStack

import numpy as np
import concourse.bass as bass
from concourse import mybir

F32 = mybir.dt.float32
F32R = mybir.dt.float32r
I32 = mybir.dt.int32
U8 = mybir.dt.uint8
ALU = mybir.AluOpType
ACT = mybir.ActivationFunctionType
AX_X = mybir.AxisListType.X

P = 128
S = 256
T = S // P
D = 1024
KT = D // P
F = 2816
R = 1280
RT = R // P
HD = 80
GT = 5
EPS = 1e-6
BW = 2048
FC = 256
CH = F // FC
RAW = 3
RING = 3
AHEAD = 2
HEADS = 4
LEVELS = (128, 64, 32, 16, 8, 4, 2, 1)
POOL_WINDOWS = (2, 4, 8, 16)
ROT = 8
TWO_PI = 6.283185307179586
PI_HI, PI_MID = 6.28125, 0.0019350051879882812
PI_LO = TWO_PI - PI_HI - PI_MID
ROUND = 12582912.0
LAM_INIT = [0.8 - 0.6 * float(np.exp(-0.3 * l)) for l in range(2)]

XN = 0
SIL, PROD = 2048, 3072
SIG = 2048
PTOK = 8192
L_R = 0
L_XB = 2560
L_XC = L_XB + RT * (S + 3) + 2
L_GELU = L_XC + RT * S
L_IG = L_GELU + RT * S
BAND = L_IG + RT * S
POOL_M, POOL_B, POOL_S = 4096, 6144, 7168
Z, Q_B, V_B, A_QK, A_V, G_B, GATE_A, GATE_B = 2048, 4096, 5120, 6144, 8192, 9216, 10240, 12288
LOGF, TMP, KK = 14336, 16384, 18432
NRM_DA, NRM_HG, LAM = 20480, 20992, 21504
ATT = 21760
PROB, W_ATT, W_T = A_QK, A_QK + 1024, A_QK + 1536
K_SUM = GATE_A
QK_T = GATE_B
SQUARES, TURNER = 22016, 22528
SCRATCH = 22784
assert BAND + 2 * 2 * GT * 384 <= SCRATCH


def head_pieces():
    out = []
    for head in range(8):
        row = 0
        while row < HD:
            at = head * HD + row
            n = min(HD - row, P - at % P)
            out.append((head, row, at // P, at % P, n))
            row += n
    return out


def build(nc, a, out):
    ctx = ExitStack()

    def sb(name, shape, dt=F32):
        return ctx.enter_context(nc.sbuf_tensor(name, shape, dt))

    def sem(name):
        return ctx.enter_context(nc.semaphore(name))

    with ctx:
        raw = sb("raw", [P, RAW, BW])
        hi = sb("hi", [P, RING, BW], F32R)
        lo = sb("lo", [P, RING, BW], F32R)
        h = sb("h", [P, T, D])
        xTh = sb("xTh", [P, RT, S], F32R)
        xTl = sb("xTl", [P, RT, S], F32R)
        prod_hi = sb("prod_hi", [P, 2, 2, S], F32R)
        prod_lo = sb("prod_lo", [P, 2, 2, S], F32R)
        gain = sb("gain", [P, D])
        gain_col = sb("gain_col", [P, 12, KT])
        ident = sb("ident", [P, P])
        level_mask = sb("level_mask", [P, len(LEVELS), P], U8)
        scr = sb("scr", [P, SCRATCH])
        stat = sb("stat", [P, 112])
        conv_w = sb("conv_w", [P, 4, RT])
        lru_c = sb("lru_c", [P, 4, RT])
        cpos = sb("cpos", [P, 6, RT])
        eps = sb("eps", [P, 2])
        rope_in = sb("rope_in", [P, 2 * ROT])
        pos_i = sb("pos_i", [P, T], I32)
        rope = sb("rope", [P, 8, T, ROT])
        one_row = sb("one_row", [P, P])
        lbt = sb("lbt", [P, 12, 2, HEADS])

        psA = ctx.enter_context(nc.psum_tensor("psA", [P, 4, 512], F32))
        psD = ctx.enter_context(nc.psum_tensor("psD", [P, 4, 512], F32))

        def view(at, *shape):
            n = int(np.prod(shape))
            v = scr[:, at:at + n]
            names = "abcd"[:len(shape)]
            if len(shape) == 1:
                return v
            return v.rearrange(f"p ({' '.join(names)}) -> p {' '.join(names)}", **dict(zip(names[1:], shape[1:])))

        xn = view(XN, T, D)
        tmp_att = view(PROB, T * 512)
        level_words = view(POOL_M, len(LEVELS), P).bitcast(I32)
        turner = view(TURNER, T, P)
        squares = view(SQUARES, 512).bitcast(mybir.dt.bfloat16).rearrange("p (c d) -> p c d", c=2)
        sil, prod = view(SIL, 2, 2 * S), view(PROD, 2, 2 * S)

        raw_landed = [sem(f"raw_landed{i}") for i in range(RAW)]
        hi_ready, lo_ready, block_used = sem("hi_ready"), sem("lo_ready"), sem("block_used")
        x_loaded = [sem(f"x_loaded{t}") for t in range(T)]
        consts_loaded, gain_loaded = sem("consts_loaded"), sem("gain_loaded")
        band_zeroed, band_loaded = sem("band_zeroed"), sem("band_loaded")
        p_loaded, pool_loaded, mix_loaded = sem("p_loaded"), sem("pool_loaded"), sem("mix_loaded")
        ident_loaded, first_gain_loaded, gains_loaded, gains_turned, gains_ready = sem("ident_loaded"), sem("first_gain_loaded"), sem("gains_loaded"), sem("gains_turned"), sem("gains_ready")
        h_ready, ssq_ready, mean_ready, rms_ready = sem("h_ready"), sem("ssq_ready"), sem("mean_ready"), sem("rms_ready")
        hg_ready, turner_ready = sem("hg_ready"), sem("turner_ready")
        first_hi, first_lo = sem("first_hi"), sem("first_lo")
        turned, xTh_ready, xT_ready = sem("turned"), sem("xTh_ready"), sem("xT_ready")
        silu_ready, prod_ready = sem("silu_ready"), sem("prod_ready")
        prod_hi_ready, prod_lo_ready = sem("prod_hi_ready"), sem("prod_lo_ready")
        dve_step, act_step = sem("dve_step"), sem("act_step")
        eps_ready, cpos_exp, cpos_ready = sem("eps_ready"), sem("cpos_exp"), sem("cpos_ready")
        xb_ready, xc_ready, gates_done, gates_ready = sem("xb_ready"), sem("xc_ready"), sem("gates_done"), sem("gates_ready")
        tanh_ready, decay_ready, mult_ready = sem("tanh_ready"), sem("decay_ready"), sem("mult_ready")
        gate_in, rows_biased = sem("gate_in"), sem("rows_biased")
        gelu_ready, y_ready, sig_ready = sem("gelu_ready"), sem("y_ready"), sem("sig_ready")
        angles_ready, rope_ready = sem("angles_ready"), sem("rope_ready")
        proj_evac, forget_evac = sem("proj_evac"), sem("forget_evac")
        gap_ready, soft_ready, kk_ready = sem("gap_ready"), sem("soft_ready"), sem("kk_ready")
        lb_in, lb_out = sem("lb_in"), sem("lb_out")
        decay_in, decay_out = sem("decay_in"), sem("decay_out")
        scaled_ready, pair_done, pair_taken = sem("scaled_ready"), sem("pair_done"), sem("pair_taken")
        rec_done, rec_square, rec_sum, rec_rms, rec_ready = sem("rec_done"), sem("rec_square"), sem("rec_sum"), sem("rec_rms"), sem("rec_ready")
        roped, qk_turned, qkT_ready = sem("roped"), sem("qk_turned"), sem("qkT_ready")
        scores_done, max_ready, exp_ready, w_ready = sem("scores_done"), sem("max_ready"), sem("exp_ready"), sem("w_ready")
        w_turned, wT_ready, att_done, att_rows = sem("w_turned"), sem("wT_ready"), sem("att_done"), sem("att_rows")
        att_square, att_sum, att_rms, att_ready = sem("att_square"), sem("att_sum"), sem("att_rms"), sem("att_ready")
        lam_in, lam_exp = sem("lam_in"), sem("lam_exp")
        merged, rows_done = sem("merged"), sem("rows_done")
        stored = sem("stored")

        def columns(w, c, n=FC):
            return w[:, c * n:(c + 1) * n].rearrange("(k p) f -> p k f", p=P)

        def rows(w, c):
            return w[c * 2 * P:(c + 1) * 2 * P, :].rearrange("(k p) n -> p k n", p=P)

        def dst(n, src):
            k = src.shape[1]
            return raw[:, n % RAW, :].rearrange("p (k f) -> p k f", k=k)

        plan = []
        for i in range(2):
            plan += [("norm", a["ffn1_norm"][i]), ("ffn", a["ffn1_w_gate"][i], a["ffn1_w_up"][i], a["ffn1_w_down"][i], 0.5)]
            plan += [("norm", a["mix_norm"][i]), ("lru",)] if i == 0 else [("pool", a["mix_norm"][i])]
            plan += [("norm", a["ffn2_norm"][i]), ("ffn", a["ffn2_w_gate"][i], a["ffn2_w_up"][i], a["ffn2_w_down"][i], 0.5)]
            plan += [("ple", a["ple_norm"][i], i)]
        plan += [("rescale", a["final_norm"])]
        for l in range(2):
            plan += [("norm", a["attn_norm_2"][l]), ("mix", l)]
            plan += [("norm", a["ffn_norm_2"][l]), ("ffn", a["w_gate_2"][l], a["w_up_2"][l], a["w_down_2"][l], 1.0)]
        plan += [("rescale", a["final_norm_2"])]
        BLOCKS = {"norm": 0, "rescale": 0, "ffn": 3 * CH, "lru": 2 * R // FC + R // (2 * P), "pool": 1, "ple": KT // 2 + 1,
                  "mix": 6 * D // FC + 8}
        CONSTS = 12
        TOTAL = sum(BLOCKS[s[0]] for s in plan)
        gains = [s[1] for s in plan if s[0] in ("norm", "pool", "ple")]
        row_gains = [s[1] for s in plan if s[0] == "rescale"]
        gain_rows = scr[0:KT, POOL_B:POOL_B + P], scr[0:(len(gains) - 1) * KT, POOL_S:POOL_S + P]
        gain_cols = slice(0, 1), slice(1, len(gains))
        FF, FB, QB, IB, AQ, AK, AV, GB_ = 8, 10, 6, 12, 0, 2, 4, 14
        PROJ = [(c + j, c) for c in (FF, FB, QB, AQ, AK, AV, IB, GB_) for j in range(2)]
        PROJ += [(16 + j, 16) for j in range(4)] + [(20 + j, 20) for j in range(4)]
        NP, NL = len(PROJ), len(LEVELS)
        UNITS = 2 * T
        SOFTS = (2, 3)
        EXPONENTS, SCORES = (6, 7), (11, 11)
        FORGET = 4

        block = ctx.enter_context(nc.Block())

        @block.sync
        def _(sp):
            for t in range(T):
                sp.dma_start(h[:, t, :], a["x"][0, t * P:(t + 1) * P, :]).then_inc(x_loaded[t], 16)
            n = 0

            def load(n_at, n, src):
                if isinstance(n_at, int):
                    if n_at >= RAW:
                        sp.wait_ge(lo_ready, n_at - RAW + 1)
                else:
                    sp.wait_ge(lo_ready, n_at - (RAW - 1))
                sp.dma_start(dst(n, src), src).then_inc(raw_landed[n % RAW], 16)

            for stage, nxt in zip(plan, plan[1:] + [("end",)]):
                kind = stage[0]
                if kind == "ffn":
                    _, wg, wu, wd, _ = stage
                    for src in (columns(wg, 0), columns(wu, 0), columns(wg, 1), columns(wu, 1), rows(wd, 0)):
                        load(n, n, src)
                        n += 1
                    with sp.Fori(0, (CH - 3) // 2) as j:
                        for e in range(2):
                            up = wg[:, bass.ds((2 * j + (e + 2)) * FC, FC)], wu[:, bass.ds((2 * j + (e + 2)) * FC, FC)]
                            down = wd[bass.ds((2 * j + (e + 1)) * FC, FC), :]
                            for b, src in enumerate([x.rearrange("(k p) f -> p k f", p=P) for x in (*up, down)]):
                                load(6 * j + (n + 3 * e + b), n + 3 * e + b, src)
                    n += 3 * (CH - 3)
                    for src in (columns(wg, CH - 1), columns(wu, CH - 1), rows(wd, CH - 2), rows(wd, CH - 1)):
                        load(n, n, src)
                        n += 1
                    continue
                srcs = []
                if kind == "lru":
                    w_in = a["lru_w_in"][0]
                    half = R // FC
                    srcs = [columns(w_in, half + c) for c in range(half)] + [columns(w_in, c) for c in range(half)]
                    srcs += [rows(a["lru_w_out"][0], c) for c in range(R // (2 * P))]
                if kind == "pool":
                    src = a["pool_w"][0].rearrange("g (k p) d -> p (g k) d", p=P)
                    srcs = [src]
                if kind == "ple":
                    srcs = [rows(a["ple_w_proj"][stage[2]], 0)] + [rows(a["ple_w_gate"][stage[2]], c) for c in range(KT // 2)]
                if kind == "mix":
                    l = stage[1]
                    srcs = [columns(a["w_in_2"][l], c) for c, _ in PROJ]
                    srcs += [rows(a["w_a_2"][l], c) for c in range(2)] + [rows(a["w_b_2"][l], c) for c in range(2)]
                    srcs += [rows(a["w_o_2"][l], c) for c in range(4)]
                for src in srcs:
                    load(n, n, src)
                    n += 1
            assert n == TOTAL
            updates = sum(s[0] in ("ffn", "lru", "pool", "ple", "mix", "rescale") for s in plan)
            for t in range(T):
                sp.wait_ge(h_ready, 2 * T * updates + 2 * (t + 1))
                sp.dma_start(out[0, t * P:(t + 1) * P, :], h[:, t, :]).then_inc(stored, 16)
            sp.wait_ge(stored, 16 * T)

        @block.gpsimd
        def _(pool):
            band = view(BAND, 2, 2, GT, 384)
            pool.memset(scr[:, BAND:BAND + 2 * 2 * GT * 384], 0.0).then_inc(band_zeroed, 1)
            for i, g in enumerate(gains[1:]):
                pool.dma_start(gain_rows[1][i * KT:(i + 1) * KT, :], g.rearrange("(k p) -> k p", p=P)).then_inc(gains_loaded, 16)
            for t_, src in ((level_words, a["c_level"]), (rope_in[:], a["c_freq"]),
                            (pos_i[:], a["positions_2"].rearrange("b (t p) -> p (b t)", p=P)),
                            (conv_w[:], a["lru_conv_w"][0].rearrange("k (f p) -> p k f", p=P)),
                            (lru_c[:, 0, :], a["lru_conv_b"][0].rearrange("(f p) -> p f", p=P)),
                            (lru_c[:, 1, :], a["lru_b_a"][0].rearrange("(f p) -> p f", p=P)),
                            (lru_c[:, 2, :], a["lru_b_x"][0].rearrange("(f p) -> p f", p=P)),
                            (lru_c[:, 3, :], a["lru_a_param"][0].rearrange("(f p) -> p f", p=P)),
                            *((lbt[:, l, e, :], a["hg_lb_logits_2"][e, l, :].rearrange("(f p) -> p f", p=P)) for l in range(2) for e in range(2))):
                pool.dma_start(t_, src, allow_slow_non_contiguous=True).then_inc(consts_loaded, 16)
            pool.wait_ge(band_zeroed, 1)
            for m, w in enumerate((a["lru_w_a"][0], a["lru_w_x"][0])):
                for head, row, tile, part, cnt in head_pieces():
                    col = head * HD - (tile - 1) * P
                    for g in range(2):
                        pool.dma_start(band[part:part + cnt, m, g, tile, col:col + HD],
                                       w[8 * g + head, row:row + cnt, :]).then_inc(band_loaded, 16)
            if row_gains:
                pool.dma_start(gain[:], row_gains[0].rearrange("(o d) -> o d", o=1).broadcast_to([P, D])).then_inc(gain_loaded, 16)
            rescaled = updates = 0
            for stage, nxt in zip(plan, plan[1:] + [("end",)]):
                kind = stage[0]
                if kind == "rescale":
                    pool.wait_ge(gain_loaded, 16 * (rescaled + 1))
                    for t in range(T):
                        for c in range(2):
                            pool.wait_ge(h_ready, 2 * T * updates + 2 * t + c + 1)
                            cs = slice(512 * c, 512 * (c + 1))
                            pool.tensor_tensor(xn[:, t, cs], h[:, t, cs], gain[:, cs], ALU.mult).then_inc(hg_ready, 1)
                    rescaled += 1
                    if rescaled < len(row_gains):
                        pool.wait_ge(hg_ready, 2 * T * rescaled)
                        pool.dma_start(gain[:], row_gains[rescaled].rearrange("(o d) -> o d", o=1).broadcast_to([P, D])).then_inc(gain_loaded, 16)
                if kind == "pool":
                    pool.wait_ge(pool_loaded, 48)
                    pool.tensor_tensor(view(POOL_B, D), view(POOL_B, D), view(POOL_S, D), ALU.mult).then_inc(rows_biased, 1)
                    pool.wait_ge(rows_biased, 1)
                    pool.wait_ge(h_ready, 2 * T * (updates + 1))
                    for t in range(T):
                        pool.tensor_tensor(xn[:, t, :], h[:, t, :], view(POOL_B, D), ALU.add).then_inc(rows_biased, 1)
                if kind in ("ffn", "lru", "pool", "ple", "mix", "rescale"):
                    updates += 1
                if kind == "lru":
                    pool.wait_ge(h_ready, 2 * T * (updates + 1))
                    pool.dma_start(view(POOL_M, T, 4, S), a["c_pool"]).then_inc(pool_loaded, 16)
                    pool.dma_start(view(POOL_B, D), a["pool_b"].broadcast_to([P, D])).then_inc(pool_loaded, 16)
                    pool.dma_start(view(POOL_S, D), a["pool_scale"].broadcast_to([P, D])).then_inc(pool_loaded, 16)
                if kind == "lru" or kind == "ple" and stage[2] == 0:
                    i = 0 if kind == "lru" else 1
                    pool.wait_ge(h_ready, 2 * T * (updates + 1))
                    pool.dma_start(view(PTOK, T, S), a["p"][i].rearrange("b (t p) d -> p (b t) d", p=P)).then_inc(p_loaded, 16)
                if kind == "lru" or kind == "mix" and stage[1] == 0:
                    l = 0 if kind == "lru" else 1
                    pool.wait_ge(h_ready, 2 * T * (updates + 1))
                    pool.dma_start(view(NRM_DA, 512), a["da_norm_2"][l].rearrange("(o d) -> o d", o=1).broadcast_to([P, 512])).then_inc(mix_loaded, 16)
                    pool.dma_start(view(NRM_HG, 512), a["hg_norm_2"][l].rearrange("(o d) -> o d", o=1).broadcast_to([P, 512])).then_inc(mix_loaded, 16)
                    pool.dma_start(view(LAM, 256), a["da_lambda_2"][l].rearrange("(o i) d -> o (i d)", o=1).broadcast_to([P, 256])).then_inc(mix_loaded, 16)

        def halves_of(ps, t):
            return [(ps[:, j, :].rearrange("p (k s) -> p k s", k=4), (slice(4 * j, 4 * j + 4), slice(t * P, (t + 1) * P)))
                    for j in range(2)]

        def quarters_of(ps, t):
            return [(ps[:, q, 0:2 * P].rearrange("p (k s) -> p k s", k=2), (slice(2 * q, 2 * q + 2), slice(t * P, (t + 1) * P)))
                    for q in range(4)]

        norm_pieces = halves_of(psA, 0) + quarters_of(psD, 1)
        ple_pieces = halves_of(psD, 0) + halves_of(psD[:, 2:4], 1)
        merge_pieces = halves_of(psA, 0) + halves_of(psA[:, 2:4], 1)
        pool_pieces = [(psA[:, q, :].rearrange("p (k s) -> p k s", k=2), (slice(2 * q, 2 * q + 2), slice(0, S))) for q in range(4)]

        def ple_piece():
            return psA[:, 1, :].rearrange("p (k s) -> p k s", k=2), (slice(8, 10), slice(0, S))

        rec_pieces = [(psD[:, c, :].rearrange("p (k s) -> p k s", k=2), (slice(4 + 2 * c, 6 + 2 * c), slice(0, S))) for c in range(2)]
        att_pieces = [(psA[:, 2 + c, :].rearrange("p (k s) -> p k s", k=2), c) for c in range(2)]

        SSQ, MEAN_A, ROOT, MEAN, INV, STEP, NEG, RSTD, SPARE = 0, 4, 6, 96, 98, 100, 102, 104, 106
        half_of = (slice(0, 512), slice(512, D))
        col = lambda c: stat[:, c:c + 1]

        def halves(v, m):
            return v.rearrange("p (n e m) -> p n e m", e=2, m=m)

        def span(v):
            return v.rearrange("p a b -> p (a b)")

        @block.scalar
        def _(act):
            st = {"split": 0, "norm": 0, "updates": 0, "piece": 0, "ffn": 0, "step": 0, "rows": 0, "turned": 0, "gate": None, "gain": 0}

            def step(ins):
                ins.then_inc(act_step, 1)
                st["step"] += 1

            def settle():
                act.wait_ge(act_step, st["step"])

            def split(n_at, n):
                if isinstance(n_at, int):
                    act.wait_ge(raw_landed[n % RAW], 16 * (n // RAW + 1))
                    if n >= RING:
                        act.wait_ge(block_used, n - RING + 1)
                else:
                    act.wait_ge(raw_landed[n % RAW], 32 * n_at + 16 * (n // RAW + 1))
                    act.wait_ge(block_used, 6 * n_at + (n - RING + 1))
                act.activation(hi[:, n % RING, :], raw[:, n % RAW, :], ACT.Copy).then_inc(hi_ready, 1)

            def split_first(c):
                cs = slice(c * BW // 2, (c + 1) * BW // 2)
                act.wait_ge(raw_landed[0], 16)
                act.activation(hi[:, 0, cs], raw[:, 0, cs], ACT.Copy).then_inc((first_hi, hi_ready)[c], 1)
                st["split"] = c

            def split_through(n):
                while st["split"] <= min(n, TOTAL - 1):
                    split(st["split"], st["split"])
                    st["split"] += 1

            def split_to(n):
                split_through(n + AHEAD)

            def piece(src, to, turns=True, nth=None):
                st["piece"] += 1
                if turns:
                    st["turned"] += 1
                    act.wait_ge(turned, st["turned"])
                x_hi = prod_hi[:, to] if isinstance(to, int) else xTh[:, to[0], to[1]]
                if nth is None:
                    last = act.activation(x_hi, src, ACT.Copy)
                else:
                    act.wait_ge(gains_ready, min(nth + 1, 2))
                    for j in range(src.shape[1]):
                        last = act.activation(x_hi[:, j, :], src[:, j, :], ACT.Copy, scale=gain_col[:, nth, to[0].start + j:to[0].start + j + 1])
                last.then_inc(xTh_ready, 1)

            def norm_stats():
                k, gate = st["norm"], st["gate"]
                st["norm"], st["gate"] = k + 1, None
                if gate:
                    for t, c in ((0, 0), (0, 1), (1, 0)):
                        gate(t, c)
                else:
                    act.activation(col(SPARE), eps[:, 1:2], ACT.Sqrt)
                for t in range(T):
                    for c in range(2):
                        act.wait_ge(h_ready, 2 * T * st["updates"] + 2 * t + c + 1)
                        act.activation(squares[:, c, :], h[:, t, half_of[c]], ACT.Square, accum_out=col(SSQ + 2 * t + c)).then_inc(ssq_ready, 1)
                        if c == 0:
                            act.wait_ge(ssq_ready, 2 * T * k + 2 * t + 1)
                            act.activation(col(MEAN_A + t), col(SSQ + 2 * t), ACT.Identity, bias=eps[:, 0:1], scale=1.0 / D).then_inc(mean_ready, 1)
                    if gate and t == 0:
                        gate(1, 1)
                    act.wait_ge(ssq_ready, 2 * T * k + 2 * t + 2)
                    act.wait_ge(mean_ready, T * k + t + 1)
                    act.activation(col(ROOT + t), col(SSQ + 2 * t + 1), ACT.Sqrt, bias=col(MEAN_A + t), scale=1.0 / D).then_inc(rms_ready, 1)

            act.dma_start(ident[:], a["c_ident"]).then_inc(ident_loaded, 16)
            act.dma_start(gain_rows[0], gains[0].rearrange("(k p) -> k p", p=P)).then_inc(first_gain_loaded, 16)
            act.wait_ge(eps_ready, 2)
            n = 0
            def constants(part):
                if part == 0:
                    act.wait_ge(cpos_exp, 1)
                    act.activation(cpos[:, 1, :], cpos[:, 0, :], ACT.Exp, scale=-1.0).then_inc(cpos_exp, 1)
                if part == 1:
                    act.wait_ge(angles_ready, 1)
                    act.activation(rope[:, 0, :, :], rope[:, 4, :, :], ACT.Sin).then_inc(rope_ready, 1)
                    act.activation(rope[:, 1, :, :], rope[:, 5, :, :], ACT.Sin).then_inc(rope_ready, 1)
                if part == 2:
                    act.wait_ge(lb_in, 1)
                    act.activation(lbt[:, 4, :, :], lbt[:, 3, :, :], ACT.Exp, scale=-1.0).then_inc(lb_out, 1)
                    act.wait_ge(lb_out, 1)
                    act.activation(lbt[:, 5, :, :], lbt[:, 4, :, :], ACT.Ln, bias=eps[:, 1:2]).then_inc(lb_out, 1)
                    act.activation(lbt[:, 6, :, :], lbt[:, 2, :, :], ACT.Sigmoid, scale=-1.0).then_inc(lb_out, 1)

            for stage, nxt in zip(plan, plan[1:] + [("end",)]):
                kind = stage[0]
                if kind == "norm":
                    norm_stats()
                    for i, part in enumerate(norm_pieces):
                        if i == 2 and n == 0:
                            split_first(0)
                        if i == 4 and n == 0:
                            split_first(1)
                        piece(*part, nth=st["gain"])
                    st["gain"] += 1
                if kind == "rescale":
                    norm_stats()
                    st["updates"] += 1
                if kind == "pool":
                    norm_stats()
                    split_through(n + 1)
                    for part in pool_pieces:
                        piece(*part, nth=st["gain"])
                    st["gain"] += 1
                    n += 1
                    st["rows"] += 3
                    st["updates"] += 1
                if kind == "ffn":
                    def gated(c_at, c, used):
                        act.wait_ge(block_used, used)
                        act.activation(sil[:, c % 2, :], psA[:, c % 2, :], ACT.Silu).then_inc(silu_ready, 1)
                        act.wait_ge(prod_ready, c_at + 1)
                        act.activation(span(prod_hi[:, c % 2]), prod[:, c % 2, :], ACT.Copy).then_inc(prod_hi_ready, 1)

                    c0 = st["ffn"] * CH
                    for b in range(5):
                        split_to(n)
                        if b in (1, 3):
                            gated(c0 + b // 2, b // 2, n + 1)
                        if b == 4 and st["ffn"] < 3:
                            constants(st["ffn"])
                        n += 1
                    with act.Fori(0, (CH - 3) // 2) as j:
                        for b in range(6):
                            split(j, n + b + AHEAD)
                            if b % 3 == 1:
                                gated(2 * j + (c0 + 2 + b // 3), b // 3, 6 * j + (n + b + 1))
                    n += 3 * (CH - 3)
                    st["split"] += 3 * (CH - 3)
                    for b in range(4):
                        if b < 3:
                            split_to(n)
                        if b == 1:
                            gated(c0 + CH - 1, CH - 1, n + 1)
                        if b == 2 and nxt[0] == "ple":
                            piece(*ple_piece())
                        n += 1
                    st["ffn"] += 1
                    st["rows"] += 3
                    st["updates"] += 1
                if kind == "lru":
                    half = R // FC
                    xb, gelu = view(L_XB, RT, S + 3), view(L_GELU, RT, S)
                    r, ig, th = view(L_R, RT, S), view(L_IG, RT, S), view(L_XB, RT, S)

                    def recurrent_gates(g):
                        for ft in range(g * GT, (g + 1) * GT):
                            act.wait_ge(gates_done, ft + 1)
                            act.activation(r[:, ft, :], psD[:, ft % 4, 0:S], ACT.Sigmoid, bias=lru_c[:, 1, ft:ft + 1]).then_inc(gates_ready, 1)
                            act.activation(ig[:, ft, :], psD[:, ft % 4, S:2 * S], ACT.Sigmoid, bias=lru_c[:, 2, ft:ft + 1]).then_inc(gates_ready, 1)

                    def half_tanh(g):
                        act.wait_ge(cpos_ready, 2)
                        act.wait_ge(gates_ready, 2 * GT * (g + 1))
                        for ft in range(g * GT, (g + 1) * GT):
                            act.activation(th[:, ft, :], r[:, ft, :], ACT.Tanh, scale=cpos[:, 4, ft:ft + 1]).then_inc(tanh_ready, 1)

                    def recurrent_decay(g):
                        act.wait_ge(tanh_ready, GT * (g + 1))
                        for ft in range(g * GT, (g + 1) * GT):
                            act.activation(r[:, ft, :], r[:, ft, :], ACT.Exp, scale=cpos[:, 5, ft:ft + 1]).then_inc(decay_ready, 1)
                        v = th[:, g * GT:(g + 1) * GT, :]
                        act.activation(v, v, ACT.Sqrt).then_inc(mult_ready, 1)

                    def gelus(ft0, ft1):
                        v = gelu[:, ft0:ft1, :]
                        act.wait_ge(gate_in, ft1 // 2)
                        act.activation(v, v, ACT.Gelu_apprx_tanh).then_inc(gelu_ready, 1)

                    for i in range(2 * half):
                        split_to(n)
                        if i == half + 2:
                            half_tanh(1)
                        if i == half + 3:
                            recurrent_decay(1)
                        n += 1
                        act.wait_ge(block_used, n)
                        ps = psA[:, i % 4, :].rearrange("p (f s) -> p f s", f=2)
                        if i < half:
                            act.activation(xb[:, 2 * i:2 * i + 2, 3:S + 3], ps, ACT.Copy).then_inc(xb_ready, 1)
                        else:
                            i2 = 2 * (i - half)
                            act.activation(gelu[:, i2:i2 + 2, :], ps, ACT.Copy).then_inc(gate_in, 1)
                        if i == half:
                            recurrent_gates(0)
                            half_tanh(0)
                        if i == half + 1:
                            recurrent_decay(0)
                            gelus(0, 4)
                            recurrent_gates(1)
                        if i == half + 2:
                            for c in range(2):
                                act.wait_ge(y_ready, c + 1)
                                piece(view(L_XC, RT, S)[:, 2 * c:2 * c + 2, :], c, turns=False)
                    gelus(4, RT)
                    split_to(n)
                    act.wait_ge(block_used, n)
                    for c in range(2, RT // 2):
                        act.wait_ge(y_ready, c + 1)
                        piece(view(L_XC, RT, S)[:, 2 * c:2 * c + 2, :], (slice(2 * c, 2 * c + 2), slice(0, S)), turns=False)
                    for i in range(R // (2 * P)):
                        if i < R // (2 * P) - 1:
                            split_to(n)
                        n += 1
                    st["rows"] += 3
                    st["updates"] += 1
                if kind == "ple":
                    norm_stats()
                    for i, part in enumerate(ple_pieces):
                        if i == 2:
                            split_through(n + 1)
                        piece(*part, nth=st["gain"])
                    st["gain"] += 1
                    for i in range(KT // 2 + 1):
                        if i < KT // 2:
                            split_to(n)
                        n += 1
                    st["rows"] += 3

                    def gate(t, c, n=n, rows_=st["rows"]):
                        if (t, c) == (1, 1):
                            act.wait_ge(block_used, n)
                        else:
                            act.wait_ge(rows_done, rows_ - 1 + t)
                        act.activation(view(SIG, T, D)[:, t, half_of[c]], psD[:, 2 * t + c, :], ACT.Sigmoid).then_inc(sig_ready, 1)

                    st["gate"] = gate
                    st["updates"] += 1
                if kind == "mix":
                    l = stage[1]
                    HS = HEADS * S
                    E0, A0 = EXPONENTS[l], SCORES[l]
                    z2, tmp2, e2, kk2 = (view(at, 2 * HS) for at in (Z, TMP, LOGF, KK))
                    near, cross = view(XN, 8, P), view(XN + 1024, 8, P)
                    pairs = psD[:, 0:2, :].rearrange("p b (e s) -> p (b e) s", s=P)
                    prob = view(PROB, 4, S)

                    def exponential(ds):
                        step(act.activation(tmp2[:, ds], tmp2[:, ds], ACT.Exp, scale=-1.0))

                    def logarithm(ds):
                        settle()
                        act.activation(tmp2[:, ds], tmp2[:, ds], ACT.Ln, bias=eps[:, 1:2]).then_inc(soft_ready, 1)

                    def soft(d):
                        act.wait_ge(forget_evac, 2 * FORGET * l + 4 * (d + 1))
                        exponential(slice(d * HS, (d + 1) * HS))
                        logarithm(slice(d * HS, (d + 1) * HS))

                    def complement(d):
                        ds = slice(d * HS, (d + 1) * HS)
                        last = act.activation(kk2[:, ds], z2[:, ds], ACT.Sigmoid, scale=-1.0)
                        if l:
                            step(last)
                            settle()
                            for c in range(HEADS):
                                v = kk2[:, d * HS + c * S:d * HS + (c + 1) * S]
                                last = act.activation(v, v, ACT.Copy, scale=lbt[:, 6, d, c:c + 1])
                        last.then_inc(kk_ready, 1)

                    def level(i):
                        act.wait_ge(decay_in, NL * l + i + 1)
                        act.activation(e2, e2, ACT.Exp).then_inc(decay_out, 1)

                    def take(i):
                        act.wait_ge(pair_done, (NL + 1) * l + i + 2)
                        act.activation(near if i < 0 else cross, pairs, ACT.Copy).then_inc(pair_taken, 1)

                    def exponentials(u):
                        k = UNITS * l + u
                        act.wait_ge(max_ready, k + 1)
                        if k:
                            act.wait_ge(w_ready, 2 * k)
                        for e in range(4):
                            ps = psA[:, 2 + e // 2, (e % 2) * S:(e % 2 + 1) * S]
                            act.activation(prob[:, e, :], ps, ACT.Exp, bias=stat[:, 48 + e:49 + e], scale=0.125,
                                           accum_out=stat[:, 56 + e:57 + e]).then_inc(exp_ready, 1)

                    def weights_turned(u):
                        act.wait_ge(w_turned, UNITS * l + u + 1)
                        act.activation(view(W_T, 512), psD[:, 2, :], ACT.Copy).then_inc(wT_ready, 1)

                    def rows_out(u):
                        act.wait_ge(att_done, UNITS * l + u + 1)
                        act.activation(view(ATT, T, 512)[:, u // 2, (u % 2) * S:(u % 2 + 1) * S], psD[:, 3, 0:S], ACT.Copy).then_inc(att_rows, 1)

                    for i, (c, first) in enumerate(PROJ):
                        for u in range(UNITS):
                            if i == A0 + 3 + 2 * u:
                                weights_turned(u)
                            if i == A0 + 4 + 2 * u:
                                rows_out(u)
                        if i in (10, 11):
                            e = i - 10
                            act.wait_ge(qk_turned, 2 * l + e + 1)
                            act.activation(view(QK_T + 1024 * e, 1024), span(psA[:, 2:4, :]), ACT.Copy).then_inc(qkT_ready, 1)
                        if i == A0 + 4 + 2 * (UNITS - 1):
                            act.wait_ge(att_rows, UNITS * (l + 1))
                            act.activation(tmp_att, view(ATT, T * 512), ACT.Square).then_inc(att_square, 1)
                        split_to(n)
                        if i in (E0 + 1, E0 + 3):
                            take((i - E0 - 3) // 2)
                        if (i - E0 - 1) % 2 == 0 and 0 <= (i - E0 - 1) // 2 < NL:
                            level((i - E0 - 1) // 2)
                        if i == A0 + 5 + 2 * (UNITS - 1):
                            act.wait_ge(att_sum, l + 1)
                            act.activation(stat[:, 24:32], stat[:, 16:24], ACT.Sqrt, bias=eps[:, 0:1], scale=1.0 / P).then_inc(att_rms, 1)
                        if i == 4:
                            soft(1)
                        if i == 5:
                            complement(1)
                        for u in range(UNITS):
                            if i == A0 + 1 + 2 * u:
                                exponentials(u)
                        n += 1
                        if i >= FORGET:
                            act.wait_ge(block_used, n)
                            j = c - first
                            ps = psA[:, i % 2, :].rearrange("p (f s) -> p f s", f=2)
                            if first == QB:
                                to, fn = view(Q_B + 512 * j, 2, S), ACT.Copy
                            else:
                                at, wide, fn = {AQ: (A_QK, 512, ACT.Copy), AK: (A_QK + 1024, 512, ACT.Copy), AV: (A_V, 512, ACT.Copy),
                                                IB: (V_B, 512, ACT.Copy), GB_: (G_B, 512, ACT.Tanh),
                                                16: (GATE_A, D, ACT.Tanh), 20: (GATE_B, D, ACT.Tanh)}[first]
                                to = view(at, T, wide)[:, :, j * FC:(j + 1) * FC]
                            act.activation(to, ps, fn, scale=0.5 if fn == ACT.Tanh else 1.0).then_inc(proj_evac, 1)
                        if i == 1:
                            soft(0)
                        if i == 2:
                            complement(0)
                        if i == 5 and l:
                            act.wait_ge(gap_ready, 2)
                            exponential(slice(0, 2 * HS))
                        if i == 6 and l:
                            logarithm(slice(0, 2 * HS))
                        if i == 10:
                            act.wait_ge(lam_in, l + 1)
                            act.activation(stat[:, 42:44], stat[:, 40:42], ACT.Exp).then_inc(lam_exp, 1)
                    split_to(n)
                    for part in att_pieces:
                        piece(*part)
                    act.wait_ge(rec_done, l + 1)
                    act.activation(tmp2[:, 0:T * 512], span(psD[:, 0:2, :]), ACT.Square).then_inc(rec_square, 1)
                    act.wait_ge(rec_sum, l + 1)
                    act.activation(stat[:, 24:32], stat[:, 16:24], ACT.Sqrt, bias=eps[:, 0:1], scale=1.0 / P).then_inc(rec_rms, 1)
                    for part in rec_pieces:
                        piece(*part)
                    n += 4
                    split_through(n)
                    for part in merge_pieces[:3]:
                        piece(*part)
                    split_through(n + 1)
                    piece(*merge_pieces[3])
                    for i in range(4):
                        if i < 3:
                            split_to(n)
                        n += 1
                    st["rows"] += 6
                    st["updates"] += 1

        @block.vector
        def _(dve):
            st = {"split": 0, "norm": 0, "updates": 0, "piece": 0, "ffn": 0, "step": 0, "rows": 0, "update": None, "early": 2, "gain": 0, "rescaled": 0, "updated": 0}

            def step(ins):
                ins.then_inc(dve_step, 1)
                st["step"] += 1

            def settle():
                dve.wait_ge(dve_step, st["step"])

            def split(n_at, n):
                dve.wait_ge(hi_ready, n_at if n_at is not None else n + 1)
                dve.tensor_tensor(lo[:, n % RING, :], raw[:, n % RAW, :], hi[:, n % RING, :].bitcast(F32), ALU.subtract).then_inc(lo_ready, 1)

            def split_through(n):
                while st["split"] <= min(n, TOTAL - 1):
                    split(None, st["split"])
                    st["split"] += 1

            def split_to(n):
                split_through(n + AHEAD)

            def split_first(c):
                cs = slice(c * BW // 2, (c + 1) * BW // 2)
                dve.wait_ge((first_hi, hi_ready)[c], 1)
                dve.tensor_tensor(lo[:, 0, cs], raw[:, 0, cs], hi[:, 0, cs].bitcast(F32), ALU.subtract).then_inc((first_lo, lo_ready)[c], 1)
                st["split"] = c

            def piece(src, to, nth=None):
                st["piece"] += 1
                dve.wait_ge(xTh_ready, st["piece"])
                x_hi, x_lo = (prod_hi[:, to], prod_lo[:, to]) if isinstance(to, int) else (xTh[:, to[0], to[1]], xTl[:, to[0], to[1]])
                if nth is None:
                    last = dve.tensor_tensor(x_lo, src, x_hi.bitcast(F32), ALU.subtract)
                else:
                    for j in range(src.shape[1]):
                        g = gain_col[:, nth, to[0].start + j:to[0].start + j + 1]
                        last = dve.scalar_tensor_tensor(x_lo[:, j, :], src[:, j, :], g, x_hi[:, j, :].bitcast(F32), ALU.mult, ALU.subtract)
                last.then_inc(xT_ready, 1)

            def inverse_root(count, width, mean, root, v, inv, t_):
                at = lambda c: stat[:, c:c + width]
                step(dve.tensor_scalar(at(v), at(mean), 1.0 / count, EPS, ALU.mult, ALU.add))
                step(dve.reciprocal(at(inv), at(root)))
                settle()
                step(dve.tensor_tensor(at(t_), at(inv), at(inv), ALU.mult))
                settle()
                step(dve.tensor_tensor(at(t_), at(t_), at(v), ALU.mult))
                settle()
                step(dve.tensor_scalar(at(t_), at(t_), -0.5, 1.5, ALU.mult, ALU.add))
                settle()
                step(dve.tensor_tensor(at(inv), at(inv), at(t_), ALU.mult))
                settle()

            def summed(t, c, n):
                if (t, c) == (0, 0):
                    st["rows"] += 3
                if (t, c) == (1, 1):
                    dve.wait_ge(block_used, n)
                else:
                    dve.wait_ge(rows_done, st["rows"] - 1 + t)

            def root(t):
                k = st["norm"] - 1
                dve.wait_ge(ssq_ready, 2 * T * k + 2 * (t + 1))
                dve.wait_ge(mean_ready, T * k + t + 1)
                step(dve.tensor_scalar(col(MEAN + t), col(SSQ + 2 * t + 1), 1.0 / D, col(MEAN_A + t), ALU.mult, ALU.add))
                dve.wait_ge(rms_ready, T * k + t + 1)
                step(dve.reciprocal(col(INV + t), col(ROOT + t)))
                settle()
                step(dve.scalar_tensor_tensor(col(STEP + t), col(INV + t), col(MEAN + t), col(INV + t), ALU.mult, ALU.mult))
                step(dve.tensor_scalar(col(NEG + t), col(INV + t), -0.5, None, ALU.mult))
                settle()
                step(dve.scalar_tensor_tensor(col(RSTD + t), col(STEP + t), -3.0, col(NEG + t), ALU.add, ALU.mult))
                settle()

            def norm_rows(scaled, also=None):
                update, early = st["update"], st["early"]
                st["norm"] += 1
                halves_ = [(t, c) for t in range(T) for c in range(2)]
                for t, c in halves_[st["updated"]:early]:
                    update(t, c).then_inc(h_ready, 1)
                st["updated"] = 0
                for t in range(T):
                    if t:
                        for half in halves_[early:]:
                            update(*half).then_inc(h_ready, 1)
                        if also:
                            also()
                    root(t)
                    scaled(t).then_inc(turner_ready, 1)

            def diagonal_of(t):
                dve.wait_ge(ident_loaded, 16)
                return dve.tensor_scalar(turner[:, t, :], ident[:], col(RSTD + t), None, ALU.mult)

            def head_sums(squares_, square_ready, nth, sum_ready):
                dve.wait_ge(square_ready, nth)
                dve.tensor_reduce(stat[:, 16:24], squares_.rearrange("p (e v) -> p e v", v=P), AX_X, ALU.add).then_inc(sum_ready, 1)

            def head_norm(src, nth, root_ready, nrm, factor, to):
                heads = lambda v: v.rearrange("p (e v) -> p e v", v=P)
                dve.wait_ge(root_ready, nth)
                inverse_root(P, 8, 16, 24, 32, 80, 88)
                step(dve.tensor_tensor(heads(to), heads(src), stat[:, 80:88].unsqueeze(2).broadcast_to([P, 8, P]), ALU.mult))
                settle()
                dve.wait_ge(mix_loaded, 48 * nth)
                rows_ = to.rearrange("p (t f) -> p t f", t=T)
                gains_ = scr[:, nrm:nrm + 512].unsqueeze(1).broadcast_to([P, T, 512])
                return dve.scalar_tensor_tensor(rows_, rows_, factor, gains_, ALU.mult, ALU.mult)

            dve.memset(eps[:, 0:1], EPS).then_inc(eps_ready, 1)
            dve.memset(eps[:, 1:2], 1.0).then_inc(eps_ready, 1)
            step(dve.memset(one_row[:], 1.0))

            def constants(part):
                if part == 0:
                    dve.wait_ge(consts_loaded, 16 * CONSTS)
                    step(dve.tensor_copy(level_mask[:], level_words))
                    dve.scalar_tensor_tensor(cpos[:, 0, :], lru_c[:, 3, :], -1.0, lru_c[:, 3, :], ALU.mult, ALU.max).then_inc(cpos_exp, 1)
                    dve.wait_ge(cpos_exp, 2)
                    step(dve.tensor_scalar(cpos[:, 2, :], cpos[:, 1, :], 2.0, None, ALU.add))
                    settle()
                    step(dve.reciprocal(cpos[:, 3, :], cpos[:, 2, :]))
                    settle()
                    step(dve.tensor_tensor(cpos[:, 1, :], cpos[:, 1, :], cpos[:, 3, :], ALU.mult))
                    settle()
                    step(dve.tensor_tensor(cpos[:, 2, :], cpos[:, 1, :], cpos[:, 1, :], ALU.mult))
                    settle()
                    step(dve.tensor_scalar(cpos[:, 3, :], cpos[:, 2, :], 1.0 / 17, None, ALU.mult))
                    settle()
                    for odd in (15, 13, 11, 9, 7, 5, 3):
                        step(dve.scalar_tensor_tensor(cpos[:, 3, :], cpos[:, 3, :], 1.0 / odd, cpos[:, 2, :], ALU.add, ALU.mult))
                        settle()
                    step(dve.scalar_tensor_tensor(cpos[:, 3, :], cpos[:, 3, :], 1.0, cpos[:, 1, :], ALU.add, ALU.mult))
                    step(dve.tensor_scalar(cpos[:, 0, :], lru_c[:, 3, :], -1.0, 0.0, ALU.mult, ALU.max))
                    settle()
                    step(dve.scalar_tensor_tensor(cpos[:, 2, :], cpos[:, 3, :], 2.0, cpos[:, 0, :], ALU.mult, ALU.add))
                    settle()
                    dve.tensor_scalar(cpos[:, 4, :], cpos[:, 2, :], 4.0, None, ALU.mult).then_inc(cpos_ready, 1)
                    dve.tensor_scalar(cpos[:, 5, :], cpos[:, 2, :], -8.0, None, ALU.mult).then_inc(cpos_ready, 1)
                if part == 1:
                    step(dve.tensor_copy(stat[:, 10:12], pos_i[:]))
                    settle()
                    for t in range(T):
                        step(dve.tensor_scalar(rope[:, 2, t, :], rope_in[:, 0:ROT], stat[:, 10 + t:11 + t], None, ALU.mult))
                    settle()
                    for shift, to in ((0.0, 4), (0.25, 5)):
                        step(dve.tensor_scalar(rope[:, 3, :, :], rope[:, 2, :, :], 1.0 / TWO_PI, shift, ALU.mult, ALU.add))
                        settle()
                        step(dve.tensor_scalar(rope[:, 3, :, :], rope[:, 3, :, :], ROUND, None, ALU.add))
                        settle()
                        step(dve.tensor_scalar(rope[:, 3, :, :], rope[:, 3, :, :], ROUND, None, ALU.subtract))
                        settle()
                        step(dve.scalar_tensor_tensor(rope[:, to, :, :], rope[:, 3, :, :], -PI_HI, rope[:, 2, :, :], ALU.mult, ALU.add))
                        settle()
                        step(dve.scalar_tensor_tensor(rope[:, to, :, :], rope[:, 3, :, :], -PI_MID, rope[:, to, :, :], ALU.mult, ALU.add))
                        settle()
                        step(dve.scalar_tensor_tensor(rope[:, to, :, :], rope[:, 3, :, :], -PI_LO, rope[:, to, :, :], ALU.mult, ALU.add))
                        settle()
                        if to == 5:
                            step(dve.tensor_scalar(rope[:, to, :, :], rope[:, to, :, :], TWO_PI / 4, None, ALU.add))
                            settle()
                        last = dve.tensor_scalar(rope[:, to, :, :], rope[:, to, :, :], 3.1415925, -3.1415925, ALU.min, ALU.max)
                        if to == 4:
                            step(last)
                            settle()
                        else:
                            last.then_inc(angles_ready, 1)
                if part == 2:
                    step(dve.tensor_tensor(lbt[:, 2], lbt[:, 1], lbt[:, 0], ALU.subtract))
                    settle()
                    dve.scalar_tensor_tensor(lbt[:, 3], lbt[:, 2], -1.0, lbt[:, 2], ALU.mult, ALU.max).then_inc(lb_in, 1)
                    dve.wait_ge(lb_out, 3)
                    step(dve.scalar_tensor_tensor(lbt[:, 7], lbt[:, 2], 0.0, lbt[:, 5], ALU.min, ALU.subtract))
                    step(dve.tensor_scalar(lbt[:, 8], lbt[:, 2], -1.0, 0.0, ALU.mult, ALU.min))
                    settle()
                    step(dve.tensor_tensor(lbt[:, 9], lbt[:, 8], lbt[:, 5], ALU.subtract))
                    settle()
                    step(dve.tensor_tensor(lbt[:, 10], lbt[:, 9], lbt[:, 7], ALU.subtract))
                    settle()

            def loaded(t, c):
                dve.wait_ge(x_loaded[t], 16)
                return dve.memset(col(SPARE + 1 + 2 * t + c), 0.0)

            st["update"] = loaded
            n = 0
            for stage, nxt in zip(plan, plan[1:] + [("end",)]):
                kind = stage[0]
                if kind == "norm":
                    def take_gains():
                        cols = span(gain_col[:, gain_cols[st["gain"]], :])
                        dve.wait_ge(gains_turned, st["gain"] + 1)
                        dve.tensor_copy(cols, psA[:, 3, 0:cols.shape[1]]).then_inc(gains_ready, 1)

                    norm_rows(diagonal_of, take_gains if st["gain"] < 2 else None)
                    dve.wait_ge(gains_ready, min(st["gain"] + 1, 2))
                    for i, part in enumerate(norm_pieces):
                        if i == 2 and n == 0:
                            split_first(0)
                        if i == 4 and n == 0:
                            split_first(1)
                        piece(*part, nth=st["gain"])
                    st["gain"] += 1
                if kind == "rescale":
                    update, k = st["update"], st["rescaled"]
                    st["norm"] += 1
                    halves_ = [(t, c) for t in range(T) for c in range(2)]
                    for t, c in halves_[:st["early"]]:
                        update(t, c).then_inc(h_ready, 1)
                    root(0)
                    for t, c in halves_[st["early"]:]:
                        update(t, c).then_inc(h_ready, 1)

                    def rescaled(t, c, k=k):
                        dve.wait_ge(hg_ready, 2 * T * k + 2 * t + c + 1)
                        return dve.tensor_scalar(h[:, t, half_of[c]], xn[:, t, half_of[c]], col(RSTD + t), None, ALU.mult)

                    rescaled(0, 0).then_inc(h_ready, 1)
                    rescaled(0, 1).then_inc(h_ready, 1)
                    root(1)
                    st["update"], st["early"], st["updated"] = rescaled, 4, 2
                    st["rescaled"] += 1
                    st["updates"] += 1
                if kind == "pool":
                    windows = view(POOL_M, T, 4, S)

                    def windows_of(t):
                        if t == 0:
                            dve.wait_ge(pool_loaded, 48)
                        v = windows[:, t, :, t * P:S]
                        return dve.tensor_scalar(v, v, col(RSTD + t), None, ALU.mult)

                    norm_rows(windows_of)
                    split_through(n + 1)
                    for part in pool_pieces:
                        piece(*part, nth=st["gain"])
                    st["gain"] += 1
                    n += 1

                    def pooled(t, c, n=n):
                        summed(t, c, n)
                        y = view(POOL_M, T, D)[:, t, half_of[c]]
                        step(dve.tensor_tensor(y, psD[:, 2 * t + c, :], view(POOL_S, D)[:, half_of[c]], ALU.mult))
                        settle()
                        dve.wait_ge(rows_biased, t + 2)
                        return dve.tensor_tensor(h[:, t, half_of[c]], xn[:, t, half_of[c]], y, ALU.add)

                    st["update"], st["early"] = pooled, 3
                    st["updates"] += 1
                if kind == "ffn":
                    def gated(c_at, c):
                        dve.wait_ge(silu_ready, c_at)
                        dve.tensor_tensor(prod[:, c % 2, :], sil[:, c % 2, :], psA[:, 2 + c % 2, :], ALU.mult).then_inc(prod_ready, 1)
                        dve.wait_ge(prod_hi_ready, c_at)
                        dve.tensor_tensor(span(prod_lo[:, c % 2]), prod[:, c % 2, :], span(prod_hi[:, c % 2]).bitcast(F32), ALU.subtract).then_inc(prod_lo_ready, 1)

                    c0 = st["ffn"] * CH
                    for b in range(5):
                        split_to(n)
                        if b in (1, 3):
                            gated(c0 + b // 2 + 1, b // 2)
                        if b == 4 and st["ffn"] < 3:
                            constants(st["ffn"])
                        n += 1
                    with dve.Fori(0, (CH - 3) // 2) as j:
                        for b in range(6):
                            split(6 * j + (n + b + AHEAD + 1), n + b + AHEAD)
                            if b % 3 == 1:
                                gated(2 * j + (c0 + 3 + b // 3), b // 3)
                    n += 3 * (CH - 3)
                    st["split"] += 3 * (CH - 3)
                    for b in range(4):
                        if b < 3:
                            split_to(n)
                        if b == 1:
                            gated(c0 + CH, CH - 1)
                        if b == 2 and nxt[0] == "ple":
                            piece(*ple_piece())
                        n += 1

                    def fed_forward(t, c, n=n, factor=stage[4]):
                        summed(t, c, n)
                        return dve.scalar_tensor_tensor(h[:, t, half_of[c]], psD[:, 2 * t + c, :], factor, h[:, t, half_of[c]], ALU.mult, ALU.add)

                    st["update"], st["early"] = fed_forward, 3
                    st["ffn"] += 1
                    st["updates"] += 1
                if kind == "lru":
                    half = R // FC
                    xb, xc = view(L_XB, RT, S + 3), view(L_XC, RT, S)
                    r, ig, th = view(L_R, RT, S), view(L_IG, RT, S), view(L_XB, RT, S)
                    gelu = view(L_GELU, RT, S)

                    step(dve.memset(xb[:, :, 0:3], 0.0))
                    settle()

                    def convolve(i):
                        dve.wait_ge(xb_ready, i + 1)
                        fts = (2 * i, 2 * i + 1)
                        for ft in fts:
                            step(dve.tensor_scalar(xc[:, ft, :], xb[:, ft, 0:S], conv_w[:, 0, ft:ft + 1], lru_c[:, 0, ft:ft + 1], ALU.mult, ALU.add))
                        for k in range(1, 4):
                            settle()
                            for ft in fts:
                                ins = dve.scalar_tensor_tensor(xc[:, ft, :], xb[:, ft, k:k + S], conv_w[:, k, ft:ft + 1], xc[:, ft, :], ALU.mult, ALU.add)
                                if k < 3:
                                    step(ins)
                                else:
                                    ins.then_inc(xc_ready, 1)

                    def recur(g):
                        gs = slice(g * GT, (g + 1) * GT)
                        dve.wait_ge(gates_ready, 2 * GT * (g + 1))
                        step(dve.tensor_tensor(ig[:, gs, :], ig[:, gs, :], xc[:, gs, :], ALU.mult))
                        dve.wait_ge(decay_ready, GT * (g + 1))
                        dve.wait_ge(mult_ready, g + 1)
                        step(dve.scalar_tensor_tensor(th[:, gs, :], r[:, gs, :], 1.0, th[:, gs, :], ALU.add, ALU.mult))
                        settle()
                        step(dve.tensor_tensor(ig[:, gs, :], ig[:, gs, :], th[:, gs, :], ALU.mult))
                        if g == 1:
                            split_to(n + 1)
                        settle()
                        for ft in range(g * GT, (g + 1) * GT):
                            step(dve.tensor_tensor_scan(ig[:, ft, :], r[:, ft, :], ig[:, ft, :], 0.0, ALU.mult, ALU.add))
                        settle()

                    def outputs(c0, c1):
                        for c in range(c0, c1):
                            fts = slice(2 * c, 2 * c + 2)
                            dve.tensor_tensor(xc[:, fts, :], ig[:, fts, :], gelu[:, fts, :], ALU.mult).then_inc(y_ready, 1)

                    for i in range(2 * half):
                        split_to(n)
                        if i < half:
                            convolve(i)
                        if i == half + 1:
                            recur(0)
                            dve.wait_ge(gelu_ready, 1)
                            outputs(0, 2)
                        if i == half + 2:
                            for c in range(2):
                                piece(xc[:, 2 * c:2 * c + 2, :], c)
                        if i == half + 3:
                            recur(1)
                        n += 1
                    dve.wait_ge(gelu_ready, 2)
                    outputs(2, RT // 2)
                    split_to(n)
                    for c in range(2, RT // 2):
                        piece(xc[:, 2 * c:2 * c + 2, :], (slice(2 * c, 2 * c + 2), slice(0, S)))
                    for i in range(R // (2 * P)):
                        if i < R // (2 * P) - 1:
                            split_to(n)
                        n += 1

                    def recurred(t, c, n=n):
                        summed(t, c, n)
                        return dve.tensor_tensor(h[:, t, half_of[c]], psD[:, 2 * t + c, :], h[:, t, half_of[c]], ALU.add)

                    st["update"], st["early"] = recurred, 3
                    st["updates"] += 1
                if kind == "ple":
                    norm_rows(diagonal_of)
                    for i, part in enumerate(ple_pieces):
                        if i == 2:
                            split_through(n + 1)
                        piece(*part, nth=st["gain"])
                    st["gain"] += 1
                    for i in range(KT // 2 + 1):
                        if i < KT // 2:
                            split_to(n)
                        n += 1
                    st["rows"] += 3

                    def gated_rows(t, c, i=stage[2]):
                        v = view(SIG, T, D)[:, t, half_of[c]]
                        dve.wait_ge(sig_ready, 2 * T * i + 2 * t + c + 1)
                        step(dve.tensor_tensor(v, v, psA[:, 2 * t + c, :], ALU.mult))
                        settle()
                        return dve.tensor_tensor(h[:, t, half_of[c]], h[:, t, half_of[c]], v, ALU.add)

                    st["update"], st["early"] = gated_rows, 4
                    st["updates"] += 1
                if kind == "mix":
                    l = stage[1]
                    HS = HEADS * S
                    z2, tmp2, e2, kk2 = (view(at, 2 * HS) for at in (Z, TMP, LOGF, KK))
                    bf, bb = view(Z, HS), view(Z + HS, HS)
                    near = view(XN, 8, P)
                    pairs = psD[:, 0:2, :].rearrange("p b (e s) -> p (b e) s", s=P)
                    heads = lambda v, d: [v[:, d * HS + c * S:d * HS + (c + 1) * S] for c in range(HEADS)]

                    def take_forget(i):
                        dve.wait_ge(block_used, n)
                        ps, ds = psA[:, i % 2, :], slice(512 * i, 512 * (i + 1))
                        dve.tensor_copy(z2[:, ds], ps).then_inc(forget_evac, 1)
                        dve.wait_ge(forget_evac, 2 * FORGET * l + 2 * i + 1)
                        dve.scalar_tensor_tensor(tmp2[:, ds], z2[:, ds], -1.0, z2[:, ds], ALU.mult, ALU.max).then_inc(forget_evac, 1)

                    def log_sigmoid(d):
                        ds = slice(d * HS, (d + 1) * HS)
                        dve.wait_ge(soft_ready, SOFTS[0] * l + d + 1)
                        step(dve.scalar_tensor_tensor(e2[:, ds], z2[:, ds], 0.0, tmp2[:, ds], ALU.min, ALU.subtract))
                        settle()
                        if l:
                            for c, (v, w) in enumerate(zip(heads(e2, d), heads(tmp2, d))):
                                step(dve.tensor_scalar(w, v, lbt[:, 10, d, c:c + 1], None, ALU.add))
                            settle()
                            dve.scalar_tensor_tensor(tmp2[:, ds], tmp2[:, ds], -1.0, tmp2[:, ds], ALU.mult, ALU.max).then_inc(gap_ready, 1)

                    def maximum(d):
                        for c, v in enumerate(heads(e2, d)):
                            step(dve.tensor_scalar(v, v, lbt[:, 9, d, c:c + 1], lbt[:, 7, d, c:c + 1], ALU.add, ALU.max))

                    def sums(d):
                        dve.wait_ge(kk_ready, 2 * l + d + 1)
                        settle()
                        way = slice(None, None, -1 if d else 1)
                        for c in range(2 * HEADS):
                            f = slice(d * HS + c * P, d * HS + (c + 1) * P)
                            if l:
                                step(dve.tensor_tensor_scan(z2[:, f][:, way], e2[:, f][:, way], tmp2[:, f][:, way], 0.0, ALU.add, ALU.add))
                            else:
                                step(dve.tensor_tensor_scan(z2[:, f][:, way], one_row[:], e2[:, f][:, way], 0.0, ALU.mult, ALU.add))

                    def diagonal():
                        dve.wait_ge(kk_ready, 2 * l + 2)
                        settle()
                        dve.tensor_tensor(view(K_SUM, HS), kk2[:, 0:HS], kk2[:, HS:2 * HS], ALU.add).then_inc(scaled_ready, 1)

                    def exponents(i):
                        m = LEVELS[i]
                        settle()
                        eq, ek, f, b = (halves(v, m) for v in (e2[:, 0:HS], e2[:, HS:2 * HS], bf, bb))
                        nb = HS // (2 * m)
                        f_end = f[:, :, 0, m - 1:m].broadcast_to([P, nb, m])
                        b_end = b[:, :, 1, 0:1].broadcast_to([P, nb, m])
                        if m == P:
                            step(dve.tensor_copy(eq[:, :, 1, :], f[:, :, 1, :]))
                            step(dve.tensor_copy(eq[:, :, 0, :], b[:, :, 0, :]))
                        else:
                            step(dve.tensor_tensor(eq[:, :, 1, :], f[:, :, 1, :], f_end, ALU.subtract))
                            step(dve.tensor_tensor(eq[:, :, 0, :], b[:, :, 0, :], b_end, ALU.subtract))
                        step(dve.tensor_tensor(ek[:, :, 0, :], f_end, f[:, :, 0, :], ALU.subtract))
                        step(dve.tensor_tensor(ek[:, :, 1, :], b_end, b[:, :, 1, :], ALU.subtract))
                        settle()
                        dve.memset(stat[:, 14:15], 0.0).then_inc(decay_in, 1)

                    def scaled(i):
                        m = LEVELS[i]
                        dve.wait_ge(decay_out, NL * l + i + 1)
                        dve.wait_ge(pair_done, (NL + 1) * l + i + 1)
                        step(dve.tensor_tensor(tmp2[:, 0:HS], view(Q_B, HS), e2[:, 0:HS], ALU.mult))
                        ek, kf, kb, to = (halves(v, m) for v in (e2[:, HS:2 * HS], kk2[:, 0:HS], kk2[:, HS:2 * HS], tmp2[:, HS:2 * HS]))
                        step(dve.tensor_tensor(to[:, :, 0, :], kf[:, :, 0, :], ek[:, :, 0, :], ALU.mult))
                        step(dve.tensor_tensor(to[:, :, 1, :], kb[:, :, 1, :], ek[:, :, 1, :], ALU.mult))
                        settle()
                        dve.memset(stat[:, 15:16], 0.0).then_inc(scaled_ready, 1)

                    def take(i):
                        dve.wait_ge(pair_done, (NL + 1) * l + i + 2)
                        dve.copy_predicated(near, level_mask[:, i, :].unsqueeze(1).broadcast_to([P, 8, P]), pairs).then_inc(pair_taken, 1)

                    def rotate(e):
                        dve.wait_ge(proj_evac, (NP - FORGET) * l + 8 + 2 * e - FORGET)
                        dve.wait_ge(rope_ready, 2)
                        x4 = view(A_QK + 1024 * e, T, 8, 64)
                        x1, x2 = x4[:, :, :, 0:ROT], x4[:, :, :, ROT:2 * ROT]
                        sin, cos = (rope[:, j, :, :].unsqueeze(2).broadcast_to([P, T, 8, ROT]) for j in (0, 1))
                        u, v, w, y = (view(ATT + 128 * j, T, 8, ROT) for j in range(4))
                        step(dve.tensor_tensor(u, x1, cos, ALU.mult))
                        step(dve.tensor_tensor(v, x2, sin, ALU.mult))
                        step(dve.tensor_tensor(w, x2, cos, ALU.mult))
                        step(dve.tensor_tensor(y, x1, sin, ALU.mult))
                        settle()
                        dve.tensor_tensor(x1, u, v, ALU.subtract).then_inc(roped, 1)
                        dve.tensor_tensor(x2, w, y, ALU.add).then_inc(roped, 1)

                    def mix_lambda_in():
                        dve.wait_ge(mix_loaded, 48 * (l + 1))
                        lam = view(LAM, 4, 64)
                        for e in range(2):
                            step(dve.tensor_tensor(lam[:, 2 * e, :], lam[:, 2 * e, :], lam[:, 2 * e + 1, :], ALU.mult))
                        settle()
                        for e in range(2):
                            step(dve.tensor_reduce(stat[:, 40 + e:41 + e], lam[:, 2 * e, :], AX_X, ALU.add))
                        settle()
                        dve.memset(stat[:, 14:15], 0.0).then_inc(lam_in, 1)

                    def mix_lambda_out():
                        dve.wait_ge(lam_exp, l + 1)
                        step(dve.scalar_tensor_tensor(stat[:, 44:45], stat[:, 42:43], LAM_INIT[l], stat[:, 43:44], ALU.add, ALU.subtract))
                        settle()
                        step(dve.tensor_scalar(stat[:, 45:46], stat[:, 44:45], -1.0, None, ALU.mult))
                        settle()

                    prob, w_att = view(PROB, 4, S), view(W_ATT, 2, S)

                    def maxima(u):
                        k = UNITS * l + u
                        dve.wait_ge(scores_done, k + 1)
                        step(dve.tensor_reduce(stat[:, 64:68], psA[:, 2:4, :].rearrange("p b (e s) -> p (b e) s", s=S), AX_X, ALU.max))
                        settle()
                        dve.tensor_scalar(stat[:, 48:52], stat[:, 64:68], -0.125, None, ALU.mult).then_inc(max_ready, 1)

                    def attention_weights(u):
                        k = UNITS * l + u
                        dve.wait_ge(exp_ready, 4 * (k + 1))
                        step(dve.reciprocal(stat[:, 68:72], stat[:, 56:60]))
                        settle()
                        step(dve.tensor_scalar(stat[:, 72:74], stat[:, 70:72], stat[:, 45:46], None, ALU.mult))
                        if k:
                            dve.wait_ge(w_turned, k)
                        for hh in range(2):
                            step(dve.tensor_scalar(w_att[:, hh, :], prob[:, hh, :], stat[:, 68 + hh:69 + hh], None, ALU.mult))
                        settle()
                        for hh in range(2):
                            dve.scalar_tensor_tensor(w_att[:, hh, :], prob[:, 2 + hh, :], stat[:, 72 + hh:73 + hh], w_att[:, hh, :],
                                                     ALU.mult, ALU.add).then_inc(w_ready, 1)

                    E0, A0 = EXPONENTS[l], SCORES[l]
                    att = view(ATT, T * 512)
                    for i, (c, first) in enumerate(PROJ):
                        for u in range(UNITS):
                            if i == A0 + 1 + 2 * u:
                                maxima(u)
                            if i == A0 + 2 + 2 * u:
                                attention_weights(u)
                        if i in (8, 10):
                            rotate((i - 8) // 2)
                        if i == A0 + 5 + 2 * (UNITS - 1):
                            head_sums(tmp_att, att_square, l + 1, att_sum)
                        if i == E0 + 3 + 2 * (NL - 1):
                            take(NL - 1)
                        if i == 7 and l:
                            dve.wait_ge(soft_ready, SOFTS[0] + SOFTS[1])
                            sums(0)
                            sums(1)
                        if l and i == E0 + 1:
                            scaled(0)
                        split_to(n)
                        n += 1
                        if i < FORGET:
                            take_forget(i)
                        if i == 4:
                            for d in range(2):
                                log_sigmoid(d)
                                if not l:
                                    sums(d)
                        if i == 5:
                            if l:
                                maximum(0)
                                maximum(1)
                            diagonal()
                        if i == 9:
                            mix_lambda_in()
                        if i == 11:
                            mix_lambda_out()
                        if (i - E0) % 2 == 0 and 0 <= (i - E0) // 2 < NL:
                            exponents((i - E0) // 2)
                        if (i - E0) % 2 == 1 and 0 <= (i - E0 - 1) // 2 < NL:
                            k = (i - E0 - 1) // 2
                            if k >= 2:
                                take(k - 1)
                            if k or not l:
                                scaled(k)
                        if i == A0 + 5 + 2 * (UNITS - 1):
                            head_norm(att, l + 1, att_rms, NRM_DA, 1.0 - LAM_INIT[l], att).then_inc(att_ready, 1)
                    if E0 + 3 + 2 * (NL - 1) >= NP:
                        take(NL - 1)
                    split_to(n)
                    for part in att_pieces:
                        piece(*part)
                    rec, o = view(LOGF, T * 512), span(psD[:, 0:2, :])
                    head_sums(tmp2[:, 0:T * 512], rec_square, l + 1, rec_sum)
                    step(head_norm(o, l + 1, rec_rms, NRM_HG, 0.5, rec))
                    settle()
                    dve.scalar_tensor_tensor(rec, view(G_B, T * 512), 1.0, rec, ALU.add, ALU.mult).then_inc(rec_ready, 1)
                    for part in rec_pieces:
                        piece(*part)
                    n += 4
                    split_through(n - 1)
                    mrg, ga, gb = xn, view(GATE_A, T, D), view(GATE_B, T, D)
                    dve.wait_ge(proj_evac, (NP - FORGET) * (l + 1))
                    dve.wait_ge(block_used, n - 2)
                    for t in range(T):
                        step(dve.scalar_tensor_tensor(mrg[:, t, :], ga[:, t, :], 1.0, span(psA[:, 2 * t:2 * t + 2, :]), ALU.add, ALU.mult))
                    split_through(n)
                    for t in range(T):
                        for c in range(2):
                            summed(t, c, n)
                            step(dve.scalar_tensor_tensor(gb[:, t, half_of[c]], gb[:, t, half_of[c]], 1.0, psD[:, 2 * t + c, :], ALU.add, ALU.mult))
                            settle()
                            dve.tensor_tensor(mrg[:, t, half_of[c]], mrg[:, t, half_of[c]], gb[:, t, half_of[c]], ALU.add).then_inc(merged, 1)
                            if (t, c) == (1, 0):
                                piece(*merge_pieces[0])
                    piece(*merge_pieces[1])
                    piece(*merge_pieces[2])
                    split_through(n + 1)
                    piece(*merge_pieces[3])
                    for i in range(4):
                        if i < 3:
                            split_to(n)
                        n += 1

                    def mixed(t, c, n=n):
                        summed(t, c, n)
                        return dve.scalar_tensor_tensor(h[:, t, half_of[c]], psD[:, 2 * t + c, :], 0.5, h[:, t, half_of[c]], ALU.mult, ALU.add)

                    st["update"], st["early"] = mixed, 3
                    st["updates"] += 1

            for c in range(2):
                st["update"](1, c).then_inc(h_ready, 1)

        @block.tensor
        def _(pe):
            st = {"norm": 0, "piece": 0, "ffn": 0, "updates": 0, "gain": 0}

            def features(n_at, n, to, fresh=False):
                if n == 0:
                    pe.wait_ge(first_lo, 1)
                else:
                    pe.wait_ge(lo_ready, n_at)
                w_hi = hi[:, n % RING, :].rearrange("p (k f) -> p k f", f=FC)
                w_lo = lo[:, n % RING, :].rearrange("p (k f) -> p k f", f=FC)
                for k0, k1 in [(k, k + 2) for k in range(0, KT, 2)] if fresh else [(0, KT)]:
                    if fresh:
                        xT_pieces(3 if k0 == 0 else 1)
                    if n == 0 and k0 == KT // 2:
                        pe.wait_ge(lo_ready, 1)
                    for f in range(2):
                        fs = slice(f * P, (f + 1) * P)
                        for k in range(k0, k1):
                            for e, (w, x) in enumerate(((w_hi, xTh), (w_hi, xTl), (w_lo, xTh))):
                                last = pe.matmul(to[:, f * S:(f + 1) * S], w[:, k, fs], x[:, k, :],
                                                 start=(k == 0 and e == 0 and not (fresh and f)),
                                                 stop=(k == KT - 1 and e == 2 and not (fresh and f == 0)))
                last.then_inc(block_used, 1)

            def tokens(n_at, n, to):
                pe.wait_ge(lo_ready, n_at)
                w_hi = hi[:, n % RING, :].rearrange("p (k f) -> p k f", f=FC)
                w_lo = lo[:, n % RING, :].rearrange("p (k f) -> p k f", f=FC)
                for t in range(T):
                    ts = slice(t * P, (t + 1) * P)
                    for k in range(KT):
                        for e, (x, w) in enumerate(((xTh, w_hi), (xTh, w_lo), (xTl, w_hi))):
                            last = pe.matmul(to[:, t * FC:(t + 1) * FC], x[:, k, ts], w[:, k, :], start=(k == 0 and e == 0),
                                             stop=(k == KT - 1 and e == 2))
                last.then_inc(block_used, 1)

            def share(n, x_hi, x_lo, to, t, cs, first, final):
                w_hi = hi[:, n % RING, :].rearrange("p (k f) -> p k f", f=D)
                w_lo = lo[:, n % RING, :].rearrange("p (k f) -> p k f", f=D)
                ts = slice(t * P, (t + 1) * P)
                for k in range(2):
                    for e, (x, w) in enumerate(((x_hi, w_hi), (x_hi, w_lo), (x_lo, w_hi))):
                        for c in cs:
                            last = pe.matmul(to[:, 2 * t + c, :], x[:, k, ts], w[:, k, half_of[c]],
                                             start=(first and k == 0 and e == 0), stop=(final and k == 1 and e == 2))
                return last

            def contract(n_at, n, x_hi, x_lo, to, first=False, final=False):
                pe.wait_ge(lo_ready, n_at)
                for t in range(T):
                    last = share(n, x_hi, x_lo, to, t, (0, 1), first, final)
                last.then_inc(block_used, 1)

            def contract_last(n, x, y, to, first=False, y_ready_at=None):
                pe.wait_ge(lo_ready, n + 1)
                share(n, *x, to, 0, (0, 1), first, False)
                share(n, *x, to, 1, (0,), first, False)
                pe.wait_ge(lo_ready, n + 2)
                if y_ready_at is not None:
                    pe.wait_ge(prod_lo_ready, y_ready_at)
                share(n + 1, *y, to, 0, (0, 1), False, True).then_inc(rows_done, 2)
                share(n + 1, *y, to, 1, (0,), False, True).then_inc(rows_done, 1)
                share(n, *x, to, 1, (1,), first, False).then_inc(block_used, 1)
                share(n + 1, *y, to, 1, (1,), False, True).then_inc(block_used, 1)

            def xT_rows(k):
                return xTh[:, k:k + 2], xTl[:, k:k + 2]

            def xT_pieces(k):
                st["piece"] += k
                pe.wait_ge(xT_ready, st["piece"])

            def turn(to, rows_, k, t):
                return pe.transpose(to, rows_[:, t, k * P:(k + 1) * P], ident[:])

            def turn_norm(t, parts):
                if t == 0:
                    st["norm"] += 1
                pe.wait_ge(h_ready, 2 * T * st["updates"] + 2 * (t + 1))
                pe.wait_ge(turner_ready, T * (st["norm"] - 1) + t + 1)
                for ps, (ks, _) in parts:
                    for k in range(ks.start, ks.stop):
                        last = pe.matmul(ps[:, k - ks.start, :], h[:, t, k * P:(k + 1) * P], turner[:, t, :], start=True, stop=True)
                    last.then_inc(turned, 1)

            pe.wait_ge(ident_loaded, 16)
            n = 0
            for stage, nxt in zip(plan, plan[1:] + [("end",)]):
                kind = stage[0]
                if kind == "norm":
                    if st["gain"] < 2:
                        rows_in = gain_rows[st["gain"]]
                        if st["gain"] == 0:
                            pe.wait_ge(first_gain_loaded, 16)
                        else:
                            pe.wait_ge(gains_loaded, 16 * (len(gains) - 1))
                        pe.transpose(psA[:, 3, 0:rows_in.shape[0]], rows_in, ident[0:rows_in.shape[0], 0:rows_in.shape[0]]).then_inc(gains_turned, 1)
                        st["gain"] += 1
                    turn_norm(0, norm_pieces[:2])
                    turn_norm(1, norm_pieces[2:])
                if kind == "pool":
                    windows = view(POOL_M, T, 4, S)
                    st["norm"] += 1
                    for t in range(T):
                        pe.wait_ge(h_ready, 2 * T * st["updates"] + 2 * (t + 1))
                        pe.wait_ge(turner_ready, T * (st["norm"] - 1) + t + 1)
                        for k in range(KT):
                            to = psA[:, k // 2, (k % 2) * S + t * P:(k % 2 + 1) * S]
                            last = pe.matmul(to, h[:, t, k * P:(k + 1) * P], windows[:, t, k // 2, t * P:S],
                                             start=(t == 0 and k % 2 == 0), stop=(t == 1 and k % 2 == 1))
                            if t == 1 and k % 2:
                                last.then_inc(turned, 1)
                    pe.wait_ge(lo_ready, n + 1)
                    w_hi, w_lo = (v[:, n % RING, :].rearrange("p (k f) -> p k f", f=FC) for v in (hi, lo))
                    for t in range(T):
                        for g in range(4):
                            if t == 0:
                                xT_pieces(1)
                            to = psD[:, 2 * t + g // 2, (g % 2) * FC:(g % 2 + 1) * FC]
                            for k in range(2):
                                for e, (x, w) in enumerate(((xTh, w_hi), (xTh, w_lo), (xTl, w_hi))):
                                    last = pe.matmul(to, x[:, 2 * g + k, t * P:(t + 1) * P], w[:, 2 * g + k, :],
                                                     start=(k == 0 and e == 0), stop=(k == 1 and e == 2))
                            if (t, g) == (0, 3):
                                last.then_inc(rows_done, 2)
                            if (t, g) == (1, 1):
                                last.then_inc(rows_done, 1)
                    last.then_inc(block_used, 1)
                    n += 1
                if kind == "ffn":
                    c0 = st["ffn"] * CH

                    def down(n_at, n, c_at, c, first=False):
                        pe.wait_ge(prod_lo_ready, c_at)
                        contract(n_at, n, prod_hi[:, c % 2], prod_lo[:, c % 2], psD, first)

                    features(n + 1, n, psA[:, 0, :], fresh=True)
                    features(n + 2, n + 1, psA[:, 2, :])
                    features(n + 3, n + 2, psA[:, 1, :])
                    features(n + 4, n + 3, psA[:, 3, :])
                    down(n + 5, n + 4, c0 + 1, 0, first=True)
                    n += 5
                    with pe.Fori(0, (CH - 3) // 2) as j:
                        for e in range(2):
                            pe.wait_ge(prod_ready, 2 * j + (c0 + e + 1))
                            features(6 * j + (n + 3 * e + 1), n + 3 * e, psA[:, e, :])
                            features(6 * j + (n + 3 * e + 2), n + 3 * e + 1, psA[:, 2 + e, :])
                            down(6 * j + (n + 3 * e + 3), n + 3 * e + 2, 2 * j + (c0 + e + 2), 1 + e)
                    n += 3 * (CH - 3)
                    pe.wait_ge(prod_ready, c0 + CH - 2)
                    features(n + 1, n, psA[:, 0, :])
                    features(n + 2, n + 1, psA[:, 2, :])
                    pe.wait_ge(prod_lo_ready, c0 + CH - 1)
                    if nxt[0] == "ple":
                        pe.wait_ge(p_loaded, 16 * (nxt[2] + 1))
                        for t in range(T):
                            for k in range(2):
                                last = turn(psA[:, 1, k * S + t * P:k * S + (t + 1) * P], view(PTOK, T, S), k, t)
                        last.then_inc(turned, 1)
                    x, y = ((prod_hi[:, c % 2], prod_lo[:, c % 2]) for c in (CH - 2, CH - 1))
                    contract_last(n + 2, x, y, psD, y_ready_at=c0 + CH)
                    n += 4
                    st["ffn"] += 1
                if kind == "lru":
                    half = R // FC
                    band, xc = view(BAND, 2, 2, GT, 384), view(L_XC, RT, S)

                    def recurrent_gates(g):
                        pe.wait_ge(xc_ready, GT * (g + 1))
                        for m in range(GT):
                            ft = g * GT + m
                            if ft >= 4:
                                pe.wait_ge(gates_ready, 2 * (ft - 3))
                            for e in range(2):
                                ks = [k for k in (m - 1, m, m + 1) if 0 <= k < GT]
                                for k in ks:
                                    last = pe.matmul(psD[:, ft % 4, e * S:(e + 1) * S], band[:, e, g, k, (m - k + 1) * P:(m - k + 2) * P],
                                                     xc[:, g * GT + k, :], start=(k == ks[0]), stop=(k == ks[-1]))
                            last.then_inc(gates_done, 1)

                    for i in range(2 * half):
                        if 4 <= i < 4 + half:
                            pe.wait_ge(xb_ready, i - 3)
                        elif i >= 4 + half:
                            pe.wait_ge(gate_in, i - 3 - half)
                        features(n + 1, n, psA[:, i % 4, :], fresh=(i == 0))
                        n += 1
                        if i == half:
                            pe.wait_ge(band_loaded, 16 * 2 * 2 * len(head_pieces()))
                            recurrent_gates(0)
                        if i == half + 1:
                            recurrent_gates(1)
                    ys = [(prod_hi[:, c], prod_lo[:, c]) for c in range(2)] + [xT_rows(2 * c) for c in range(2, RT // 2)]
                    for i, y in enumerate(ys[:-2]):
                        xT_pieces(1)
                        contract(n + 1, n, *y, psD, first=(i == 0))
                        n += 1
                    xT_pieces(2)
                    contract_last(n, *ys[-2:], psD)
                    n += 2
                if kind == "ple":
                    xT_pieces(1)
                    turn_norm(0, ple_pieces[:2])
                    contract(n + 1, n, *xT_rows(KT), psA, first=True, final=True)
                    n += 1
                    turn_norm(1, ple_pieces[2:])
                    xT_pieces(2)
                    pe.wait_ge(lo_ready, n + 1)
                    share(n, *xT_rows(0), psD, 0, (0, 1), True, False)
                    xT_pieces(2)
                    share(n, *xT_rows(0), psD, 1, (0, 1), True, False).then_inc(block_used, 1)
                    n += 1
                    for i in range(1, KT // 2 - 2):
                        contract(n + 1, n, *xT_rows(2 * i), psD)
                        n += 1
                    contract_last(n, xT_rows(KT - 4), xT_rows(KT - 2), psD)
                    n += 2
                if kind == "mix":
                    l = stage[1]
                    HS = HEADS * S
                    tmp2, q_b, v_b, v_a = view(TMP, 2, HEADS, S), view(Q_B, HEADS, S), view(V_B, T, 512), view(A_V, T, 512)
                    near, cross = view(XN, 8, P), view(XN + 1024, 8, P)
                    qkT, w_att, wT = view(QK_T, 2, HEADS, S), view(W_ATT, 2, S), view(W_T, 2, T, P)

                    def pair(i):
                        k0 = (NL + 1) * l
                        pe.wait_ge(scaled_ready, k0 + i + 2)
                        if i < 0:
                            pe.wait_ge(proj_evac, (NP - FORGET) * l + 2)
                        if i >= 0:
                            pe.wait_ge(pair_taken, k0 + i + 1)
                        q, k_ = (q_b, view(K_SUM, HEADS, S)) if i < 0 else (tmp2[:, 0], tmp2[:, 1])
                        ps = psD[:, 0:2, :].rearrange("p b (e s) -> p (b e) s", s=P)
                        for hh in range(HEADS):
                            for e in range(T):
                                te = 1 - e if i >= 0 and LEVELS[i] == P else e
                                last = pe.matmul(ps[:, 2 * hh + e, :], k_[:, hh, e * P:(e + 1) * P], q[:, hh, te * P:(te + 1) * P],
                                                 start=True, stop=True)
                        last.then_inc(pair_done, 1)

                    def turn_heads(e):
                        pe.wait_ge(roped, 4 * l + 2 * e + 2)
                        if e:
                            pe.wait_ge(qkT_ready, 2 * l + 1)
                        for t in range(T):
                            for hh in range(HEADS):
                                last = turn(psA[:, 2 + hh // 2, (hh % 2) * S + t * P:(hh % 2) * S + (t + 1) * P], view(A_QK + 1024 * e, T, 512), hh, t)
                        last.then_inc(qk_turned, 1)

                    def scores(u):
                        t, k = u // 2, UNITS * l + u
                        pe.wait_ge(qkT_ready, 2 * l + 2)
                        if u:
                            pe.wait_ge(exp_ready, 4 * k)
                        for e in range(2):
                            cs = slice(64 * e, 64 * e + 64)
                            for j in range(2):
                                hh = 2 * (u % 2) + j
                                last = pe.matmul(psA[:, 2 + e, j * S:(j + 1) * S], qkT[cs, 0, hh, t * P:(t + 1) * P], qkT[cs, 1, hh, :],
                                                 start=True, stop=True)
                        last.then_inc(scores_done, 1)

                    def turn_weights(u):
                        k = UNITS * l + u
                        pe.wait_ge(w_ready, 2 * (k + 1))
                        if k:
                            pe.wait_ge(wT_ready, k)
                        for j in range(2):
                            for e in range(T):
                                last = turn(psD[:, 2, (T * j + e) * P:(T * j + e + 1) * P], w_att, e, j)
                        last.then_inc(w_turned, 1)

                    def attend(u):
                        k = UNITS * l + u
                        pe.wait_ge(wT_ready, k + 1)
                        if k:
                            pe.wait_ge(att_rows, k)
                        for j in range(2):
                            hh = 2 * (u % 2) + j
                            for e in range(T):
                                last = pe.matmul(psD[:, 3, j * P:(j + 1) * P], wT[:, j, e, :], v_a[:, e, hh * P:(hh + 1) * P],
                                                 start=(e == 0), stop=(e == T - 1))
                        last.then_inc(att_done, 1)

                    E0, A0 = EXPONENTS[l], SCORES[l]
                    for i, (c, first) in enumerate(PROJ):
                        if 2 <= i < 2 + FORGET:
                            pe.wait_ge(forget_evac, 2 * FORGET * l + 2 * (i - 1))
                        elif i >= 2:
                            pe.wait_ge(proj_evac, (NP - FORGET) * l + i - 1 - FORGET)
                        if first in (FF, FB, QB):
                            features(n + 1, n, psA[:, i % 2, :], fresh=(i == 0))
                        else:
                            tokens(n + 1, n, psA[:, i % 2, :])
                        n += 1
                        if (i - E0) % 2 == 0 and 0 <= (i - E0) // 2 <= NL:
                            pair((i - E0) // 2 - 1)
                        if i in (9, 10):
                            turn_heads(i - 9)
                        for u in range(UNITS):
                            if i == A0 + 2 * u:
                                scores(u)
                            if i == A0 + 2 + 2 * u:
                                turn_weights(u)
                            if i == A0 + 3 + 2 * u:
                                attend(u)
                    pe.wait_ge(att_ready, l + 1)
                    for ps, c in att_pieces:
                        for t in range(T):
                            for k in range(2):
                                last = turn(ps[:, k, t * P:(t + 1) * P], view(ATT, T, 512), 2 * c + k, t)
                        last.then_inc(turned, 1)
                    pe.wait_ge(pair_taken, (NL + 1) * (l + 1))
                    for t in range(T):
                        for hh in range(HEADS):
                            to = psD[:, t, hh * P:(hh + 1) * P]
                            pe.matmul(to, near[:, 2 * hh + t, :], v_b[:, t, hh * P:(hh + 1) * P], start=True, stop=False)
                            last = pe.matmul(to, cross[:, 2 * hh + 1 - t, :], v_b[:, 1 - t, hh * P:(hh + 1) * P], start=False, stop=True)
                    last.then_inc(rec_done, 1)
                    xT_pieces(2)
                    pe.wait_ge(proj_evac, (NP - FORGET) * (l + 1))
                    contract(n + 1, n, prod_hi[:, 0], prod_lo[:, 0], psA, first=True)
                    n += 1
                    pe.wait_ge(lo_ready, n + 1)
                    share(n, prod_hi[:, 1], prod_lo[:, 1], psA, 0, (0, 1), False, True)
                    pe.wait_ge(rec_ready, l + 1)
                    for ps, (ks, _) in rec_pieces:
                        for t in range(T):
                            for k in range(2):
                                last = turn(ps[:, k, t * P:(t + 1) * P], view(LOGF, T, 512), ks.start - 4 + k, t)
                        last.then_inc(turned, 1)
                    share(n, prod_hi[:, 1], prod_lo[:, 1], psA, 1, (0, 1), False, True).then_inc(block_used, 1)
                    n += 1
                    xT_pieces(2)
                    contract_last(n, xT_rows(4), xT_rows(6), psD, first=True)
                    n += 2
                    def turn_merged(i):
                        ps, (ks, _) = merge_pieces[i]
                        pe.wait_ge(merged, 2 * T * l + i + 1)
                        for k in range(ks.start, ks.stop):
                            last = turn(ps[:, k - ks.start, :], xn, k, i // 2)
                        last.then_inc(turned, 1)

                    for i in range(3):
                        turn_merged(i)
                    xT_pieces(1)
                    pe.wait_ge(lo_ready, n + 1)
                    share(n, *xT_rows(0), psD, 0, (0, 1), True, False)
                    turn_merged(3)
                    xT_pieces(2)
                    share(n, *xT_rows(0), psD, 1, (0, 1), True, False).then_inc(block_used, 1)
                    n += 1
                    contract(n + 1, n, *xT_rows(2), psD)
                    n += 1
                    xT_pieces(1)
                    contract_last(n, xT_rows(KT - 4), xT_rows(KT - 2), psD)
                    n += 2
                if kind not in ("norm",):
                    st["updates"] += 1
            assert n == TOTAL


_INS = ["x", "p", "ffn1_norm", "ffn1_w_gate", "ffn1_w_up", "ffn1_w_down", "mix_norm", "lru_w_in", "lru_conv_w", "lru_conv_b",
        "lru_w_a", "lru_b_a", "lru_w_x", "lru_b_x", "lru_a_param", "lru_w_out", "pool_w", "pool_b", "pool_scale", "ffn2_norm",
        "ffn2_w_gate", "ffn2_w_up", "ffn2_w_down", "ple_norm", "ple_w_gate", "ple_w_proj", "final_norm", "positions_2", "w_in_2",
        "da_lambda_2", "da_norm_2", "hg_lb_logits_2", "hg_norm_2", "w_a_2", "w_b_2", "w_o_2", "attn_norm_2", "ffn_norm_2",
        "w_gate_2", "w_up_2", "w_down_2", "final_norm_2"]


def shape_constants():
    i = np.arange(P)
    level = np.zeros((P, len(LEVELS), P), np.int32)
    for e, m in enumerate(LEVELS):
        level[:, e, :] = (i[:, None] // m != i[None, :] // m) & (i[:, None] // (2 * m) == i[None, :] // (2 * m))
    pool = np.zeros((P, T, len(POOL_WINDOWS), S), np.float32)
    s = np.arange(S)
    for t in range(T):
        tok = t * P + i[:, None]
        for g, win in enumerate(POOL_WINDOWS):
            inside = (tok <= s[None, :]) & (tok > s[None, :] - win)
            pool[:, t, g, :] = inside / np.minimum(s[None, :] + 1, win).astype(np.float32) - (tok == s[None, :])
    freq = np.float32(500000.0) ** (-(np.arange(0, 2 * ROT, 2, dtype=np.float32) / np.float32(2 * ROT)))
    freq = np.tile(np.concatenate([freq, freq]).astype(np.float32), (P, 1))
    return {"c_ident": np.eye(P, dtype=np.float32), "c_level": level, "c_pool": pool, "c_freq": freq}


def kernel(**inputs):
    import concourse.bacc as bacc
    from concourse.bass_utils import run_bass_kernel_spmd

    nc = bacc.Bacc("TRN2", target_bir_lowering=False, num_devices=1)
    arrays, aps = {}, {}
    for name, v in [(k, inputs[k]) for k in _INS] + list(shape_constants().items()):
        v = np.ascontiguousarray(v)
        arrays[f"in_{name}"] = v
        aps[name] = nc.dram_tensor(f"in_{name}", v.shape, mybir.dt.from_np(v.dtype), kind="ExternalInput").ap()
    out = nc.dram_tensor("out_0", (1, S, D), F32, kind="ExternalOutput").ap()
    build(nc, aps, out)
    r = run_bass_kernel_spmd(nc, [arrays], core_ids=[0])
    return r.results[0]["out_0"]
```
